# Optimizing a Trainium2 kernel written in Bass

```python
import jax, jax.numpy as jnp
from jax import lax
import numpy as np

D_MODEL = 1024
BATCH = 1
SEQ = 1024
DEPTH = 2
DEC_BATCH = 1
DEC_SEQ = 32
PAST_LEN = 512

CHUNK = 64
HEAD_DIM = 64
MIX_WIDTH = D_MODEL
A_WIDTH = MIX_WIDTH // 2
N_HEADS_A = A_WIDTH // HEAD_DIM
N_KV_A = 2
GROUP_A = N_HEADS_A // N_KV_A
KV_WIDTH_A = N_KV_A * HEAD_DIM
WINDOW = 128
WINDOW_CHUNKS = WINDOW // CHUNK
SWA_CACHE = min(WINDOW, PAST_LEN)
ROPE_THETA = 10000.0
R_WIDTH = MIX_WIDTH - A_WIDTH
N_HEADS_R = R_WIDTH // HEAD_DIM
DECAY_LORA = max(32, int(round(1.8 * D_MODEL ** 0.5 / 32)) * 32)
AAA_LORA = max(32, int(round(1.8 * D_MODEL ** 0.5 / 32)) * 32)
GATE_LORA = max(32, int(round(0.6 * D_MODEL ** 0.8 / 32)) * 32)
RWKV_PROJ = 3 * R_WIDTH + DECAY_LORA + AAA_LORA + GATE_LORA
GN_EPS = 6.4e-4
IN_COLS = A_WIDTH + 2 * KV_WIDTH_A + RWKV_PROJ
MEM_LEN = 256
MEM_HEADS = 4
MEM_HEAD_DIM = 128
MEM_WIDTH = MEM_HEADS * MEM_HEAD_DIM
D_FF = -(-8 * D_MODEL // (3 * 256)) * 256
RMS_EPS = 1e-6
NEG_INF = -1e30
NORM_MIX_PRE, NORM_MIX_POST, NORM_X_PRE, NORM_X_POST, NORM_MEM, NORM_FFN_PRE, NORM_FFN_POST = range(7)
N_NORMS = 7

kernel_name = "hybrid_swa_rwkv7_streaming_step"

def rms_norm(x, g):
    xf = x.astype(jnp.float32)
    y = xf * lax.rsqrt(jnp.mean(xf * xf, axis=-1, keepdims=True) + RMS_EPS)
    return (y * g.astype(jnp.float32)).astype(x.dtype)

def rope(x, pos):
    half = HEAD_DIM // 2
    inv = ROPE_THETA ** (-jnp.arange(half, dtype=jnp.float32) / half)
    ang = pos.astype(jnp.float32)[:, None] * inv[None, :]
    cos = jnp.cos(ang)[:, None, :]
    sin = jnp.sin(ang)[:, None, :]
    xf = x.astype(jnp.float32)
    x1, x2 = xf[..., :half], xf[..., half:]
    return jnp.concatenate([x1 * cos - x2 * sin, x2 * cos + x1 * sin], axis=-1).astype(x.dtype)

def sink_attention(q, k, v, sink, mask):
    s = jnp.einsum('...qhgd,...khd->...hgqk', q.astype(jnp.float32), k.astype(jnp.float32)) * (HEAD_DIM ** -0.5)
    if mask is not None:
        s = jnp.where(mask, s, NEG_INF)
    sk = sink.astype(jnp.float32).reshape(N_KV_A, GROUP_A)[:, :, None, None]
    m = jnp.maximum(jnp.max(s, axis=-1, keepdims=True), sk)
    e = jnp.exp(s - m)
    p = e / (jnp.sum(e, axis=-1, keepdims=True) + jnp.exp(sk - m))
    o = jnp.einsum('...hgqk,...khd->...qhgd', p, v.astype(jnp.float32))
    return o.astype(q.dtype)

def swa_banded(q, k, v, sink):
    B, T = q.shape[:2]
    n_c = T // CHUNK
    qc = q.reshape(B, n_c, CHUNK, N_KV_A, GROUP_A, HEAD_DIM)
    pad = ((0, 0), (WINDOW_CHUNKS * CHUNK, 0), (0, 0), (0, 0))
    kp = jnp.pad(k, pad).reshape(B, n_c + WINDOW_CHUNKS, CHUNK, N_KV_A, HEAD_DIM)
    vp = jnp.pad(v, pad).reshape(B, n_c + WINDOW_CHUNKS, CHUNK, N_KV_A, HEAD_DIM)
    kb = jnp.concatenate([kp[:, j:j + n_c] for j in range(WINDOW_CHUNKS + 1)], axis=2)
    vb = jnp.concatenate([vp[:, j:j + n_c] for j in range(WINDOW_CHUNKS + 1)], axis=2)
    slot_chunk = jnp.arange((WINDOW_CHUNKS + 1) * CHUNK)[None, :] // CHUNK
    valid = (jnp.arange(n_c)[:, None] - WINDOW_CHUNKS + slot_chunk) >= 0
    mask = valid[:, None, None, None, :]
    o = sink_attention(qc, kb, vb, sink, mask)
    return o.reshape(B, T, A_WIDTH)

def rwkv_step(S, inp):
    r_t, w_t, k_t, v_t, kk_t, b_t = inp
    sa = jnp.einsum('bhvk,bhk->bhv', S, -kk_t)
    S = S * w_t[:, :, None, :] + sa[..., None] * b_t[:, :, None, :] + v_t[..., None] * k_t[:, :, None, :]
    return S, jnp.einsum('bhvk,bhk->bhv', S, r_t)

def rwkv_mix(P, shift0, S0, mu, rvecs, rk, w2, a2, g2):
    B, T, _ = P.shape
    f32 = jnp.float32
    p_prev = jnp.concatenate([shift0.astype(P.dtype), P[:, :-1]], axis=1)
    ps = P + (p_prev - P) * mu
    o = R_WIDTH
    r, k, v = ps[..., :o], ps[..., o:2 * o], ps[..., 2 * o:3 * o]
    xw = ps[..., 3 * o:3 * o + DECAY_LORA]
    xa = ps[..., 3 * o + DECAY_LORA:3 * o + DECAY_LORA + AAA_LORA]
    xg = ps[..., 3 * o + DECAY_LORA + AAA_LORA:]
    w0, a0, k_k, k_a, gn_g, gn_b = rvecs[0], rvecs[1], rvecs[2], rvecs[3], rvecs[4], rvecs[5]
    w_raw = -jax.nn.softplus(-(w0 + jnp.tanh(xw) @ w2).astype(f32)) - 0.5
    decay = jnp.exp(-jnp.exp(w_raw))
    a = jax.nn.sigmoid((a0 + xa @ a2).astype(f32))
    g = (jax.nn.sigmoid(xg) @ g2).astype(f32)

    def heads(t):
        return t.reshape(B, T, N_HEADS_R, HEAD_DIM)

    kk = heads((k * k_k).astype(f32))
    kk = kk * lax.rsqrt(jnp.maximum(jnp.sum(kk * kk, axis=-1, keepdims=True), 1e-24))
    k_f = heads(k.astype(f32) * (1.0 + (a - 1.0) * k_a.astype(f32)))
    r_f = heads(r.astype(f32))
    v_f = heads(v.astype(f32))
    a_h = heads(a)
    w_h = heads(decay)

    def tmaj(t):
        return jnp.moveaxis(t, 1, 0)

    S_fin, y = lax.scan(rwkv_step, S0.astype(f32),
                        (tmaj(r_f), tmaj(w_h), tmaj(k_f), tmaj(v_f), tmaj(kk), tmaj(kk * a_h)))
    y = jnp.moveaxis(y, 0, 1)
    mean = jnp.mean(y, axis=-1, keepdims=True)
    var = jnp.mean(jnp.square(y - mean), axis=-1, keepdims=True)
    yn = ((y - mean) * lax.rsqrt(var + GN_EPS)).reshape(B, T, R_WIDTH) * gn_g.astype(f32) + gn_b.astype(f32)
    bonus = (jnp.sum(r_f * k_f * rk.astype(f32), axis=-1, keepdims=True) * v_f).reshape(B, T, R_WIDTH)
    out = (yn + bonus) * g
    return out.astype(P.dtype), S_fin, P[:, -1:]

def token_mix(h, pos, w_in, sink, mu, rvecs, rk, w2, a2, g2, w_out, swa_k_past, swa_v_past, S0, shift0):
    B, T, _ = h.shape
    P = h @ w_in
    q = rope(P[..., :A_WIDTH].reshape(B, T, N_HEADS_A, HEAD_DIM), pos)
    ka = rope(P[..., A_WIDTH:A_WIDTH + KV_WIDTH_A].reshape(B, T, N_KV_A, HEAD_DIM), pos)
    va = P[..., A_WIDTH + KV_WIDTH_A:A_WIDTH + 2 * KV_WIDTH_A].reshape(B, T, N_KV_A, HEAD_DIM)
    pr = P[..., A_WIDTH + 2 * KV_WIDTH_A:]
    if swa_k_past is None:
        attn = swa_banded(q, ka, va, sink)
        keep = T - min(WINDOW, T)
        k_keep, v_keep = ka[:, keep:], va[:, keep:]
    else:
        keys = jnp.concatenate([swa_k_past.astype(ka.dtype), ka], axis=1)
        vals = jnp.concatenate([swa_v_past.astype(va.dtype), va], axis=1)
        qg = q.reshape(B, T, N_KV_A, GROUP_A, HEAD_DIM)
        attn = sink_attention(qg, keys, vals, sink, None).reshape(B, T, A_WIDTH)
        k_keep, v_keep = ka, va
    rw, S_fin, shift_new = rwkv_mix(pr, shift0, S0, mu, rvecs, rk, w2, a2, g2)
    out = jnp.concatenate([attn, rw], axis=-1) @ w_out
    return out, k_keep, v_keep, S_fin, shift_new

def memory_kv(mem, g_mem, w_mem_kv):
    B, M, _ = mem.shape
    kv = rms_norm(mem, g_mem) @ w_mem_kv
    mk = kv[..., :MEM_WIDTH].reshape(B, M, MEM_HEADS, MEM_HEAD_DIM)
    mv = kv[..., MEM_WIDTH:].reshape(B, M, MEM_HEADS, MEM_HEAD_DIM)
    return mk, mv

def cross_attend(h, mem_k, mem_v, w_q, w_o):
    B, T, _ = h.shape
    q = (h @ w_q).reshape(B, T, MEM_HEADS, MEM_HEAD_DIM)
    s = jnp.einsum('bqhd,bkhd->bhqk', q.astype(jnp.float32), mem_k.astype(jnp.float32)) * (MEM_HEAD_DIM ** -0.5)
    p = jax.nn.softmax(s, axis=-1)
    o = jnp.einsum('bhqk,bkhd->bqhd', p, mem_v.astype(jnp.float32)).astype(h.dtype)
    return o.reshape(B, T, MEM_WIDTH) @ w_o

def swiglu(h, w_gu, w_dn):
    gu = h @ w_gu
    return (jax.nn.silu(gu[..., :D_FF]) * gu[..., D_FF:]) @ w_dn

def layer(x, pos, mem_k, mem_v, swa_k_past, swa_v_past, S0, shift0, lw):
    ng, w_in, sink, mu, rvecs, rk, w2, a2, g2, w_out, w_mq, w_mo, w_gu, w_dn = lw
    m, k_keep, v_keep, S_fin, shift_new = token_mix(
        rms_norm(x, ng[NORM_MIX_PRE]), pos, w_in, sink, mu, rvecs, rk, w2, a2, g2, w_out,
        swa_k_past, swa_v_past, S0, shift0)
    x = x + rms_norm(m, ng[NORM_MIX_POST])
    c = cross_attend(rms_norm(x, ng[NORM_X_PRE]), mem_k, mem_v, w_mq, w_mo)
    x = x + rms_norm(c, ng[NORM_X_POST])
    f = swiglu(rms_norm(x, ng[NORM_FFN_PRE]), w_gu, w_dn)
    x = x + rms_norm(f, ng[NORM_FFN_POST])
    return x, k_keep, v_keep, S_fin, shift_new

def setup_inputs(seed: int = 0) -> dict:
    key = jax.random.key(seed)
    ks = jax.random.split(key, 24)
    nrm = jax.random.normal
    f32 = jnp.float32
    vec_off = jnp.array([0.0, 0.0, 0.85, 1.0, 1.0, 0.0], f32)[None, :, None]
    vec_scl = jnp.array([0.5, 0.5, 0.05, 0.05, 0.05, 0.02], f32)[None, :, None]
    return {
        "x_prompt": nrm(ks[0], (BATCH, SEQ, D_MODEL), f32),
        "mem_prompt": nrm(ks[1], (BATCH, MEM_LEN, D_MODEL), f32),
        "x_sample": nrm(ks[2], (DEC_BATCH, DEC_SEQ, D_MODEL), f32),
        "cache_swa_k": nrm(ks[3], (DEPTH, DEC_BATCH, SWA_CACHE, N_KV_A, HEAD_DIM), f32),
        "cache_swa_v": nrm(ks[4], (DEPTH, DEC_BATCH, SWA_CACHE, N_KV_A, HEAD_DIM), f32),
        "cache_mem_k": nrm(ks[5], (DEPTH, DEC_BATCH, MEM_LEN, MEM_HEADS, MEM_HEAD_DIM), f32),
        "cache_mem_v": nrm(ks[6], (DEPTH, DEC_BATCH, MEM_LEN, MEM_HEADS, MEM_HEAD_DIM), f32),
        "state_rwkv": 0.5 * nrm(ks[7], (DEPTH, DEC_BATCH, N_HEADS_R, HEAD_DIM, HEAD_DIM), f32),
        "state_shift": nrm(ks[8], (DEPTH, DEC_BATCH, 1, RWKV_PROJ), f32),
        "norm_gains": 1.0 + 0.05 * nrm(ks[9], (DEPTH, N_NORMS, D_MODEL), f32),
        "w_in": nrm(ks[10], (DEPTH, D_MODEL, IN_COLS), f32) * D_MODEL ** -0.5,
        "attn_sink": 0.5 * nrm(ks[11], (DEPTH, N_HEADS_A), f32),
        "shift_mu": jax.random.uniform(ks[12], (DEPTH, RWKV_PROJ), f32),
        "rwkv_vecs": vec_off + vec_scl * nrm(ks[13], (DEPTH, 6, R_WIDTH), f32),
        "rwkv_rk": 0.1 * nrm(ks[14], (DEPTH, N_HEADS_R, HEAD_DIM), f32),
        "rwkv_w2": nrm(ks[15], (DEPTH, DECAY_LORA, R_WIDTH), f32) * DECAY_LORA ** -0.5,
        "rwkv_a2": nrm(ks[16], (DEPTH, AAA_LORA, R_WIDTH), f32) * AAA_LORA ** -0.5,
        "rwkv_g2": nrm(ks[17], (DEPTH, GATE_LORA, R_WIDTH), f32) * GATE_LORA ** -0.5,
        "w_out": nrm(ks[18], (DEPTH, MIX_WIDTH, D_MODEL), f32) * MIX_WIDTH ** -0.5,
        "w_mem_q": nrm(ks[19], (DEPTH, D_MODEL, MEM_WIDTH), f32) * D_MODEL ** -0.5,
        "w_mem_kv": nrm(ks[20], (DEPTH, D_MODEL, 2 * MEM_WIDTH), f32) * D_MODEL ** -0.5,
        "w_mem_o": nrm(ks[21], (DEPTH, MEM_WIDTH, D_MODEL), f32) * MEM_WIDTH ** -0.5,
        "w_gate_up": nrm(ks[22], (DEPTH, D_MODEL, 2 * D_FF), f32) * D_MODEL ** -0.5,
        "w_down": nrm(ks[23], (DEPTH, D_FF, D_MODEL), f32) * D_FF ** -0.5,
    }

def reference(x_prompt, mem_prompt, x_sample, cache_swa_k, cache_swa_v, cache_mem_k, cache_mem_v,
              state_rwkv, state_shift, norm_gains, w_in, attn_sink, shift_mu, rwkv_vecs, rwkv_rk,
              rwkv_w2, rwkv_a2, rwkv_g2, w_out, w_mem_q, w_mem_kv, w_mem_o, w_gate_up, w_down):
    B, T, _ = x_prompt.shape
    Bd, Tn, _ = x_sample.shape
    pos_p = jnp.arange(T, dtype=jnp.int32)
    pos_s = PAST_LEN + jnp.arange(Tn, dtype=jnp.int32)
    S0_p = jnp.zeros((B, N_HEADS_R, HEAD_DIM, HEAD_DIM), jnp.float32)
    sh0_p = jnp.zeros((B, 1, RWKV_PROJ), x_prompt.dtype)
    xp, xs = x_prompt, x_sample
    pk, pv, pmk, pmv, pS, psh = [], [], [], [], [], []
    sk, sv, sS, ssh = [], [], [], []
    for l in range(DEPTH):
        lw = (norm_gains[l], w_in[l], attn_sink[l], shift_mu[l], rwkv_vecs[l], rwkv_rk[l], rwkv_w2[l],
              rwkv_a2[l], rwkv_g2[l], w_out[l], w_mem_q[l], w_mem_o[l], w_gate_up[l], w_down[l])
        mk_l, mv_l = memory_kv(mem_prompt, norm_gains[l, NORM_MEM], w_mem_kv[l])
        xp, k_l, v_l, S_l, sh_l = layer(xp, pos_p, mk_l, mv_l, None, None, S0_p, sh0_p, lw)
        pk.append(k_l); pv.append(v_l); pmk.append(mk_l); pmv.append(mv_l); pS.append(S_l); psh.append(sh_l)
        xs, k2, v2, S2, sh2 = layer(xs, pos_s, cache_mem_k[l], cache_mem_v[l], cache_swa_k[l], cache_swa_v[l],
                                    state_rwkv[l], state_shift[l], lw)
        sk.append(k2); sv.append(v2); sS.append(S2.astype(state_rwkv.dtype)); ssh.append(sh2)
    return (xp, xs, jnp.stack(pk), jnp.stack(pv), jnp.stack(pmk), jnp.stack(pmv), jnp.stack(pS), jnp.stack(psh),
            jnp.stack(sk), jnp.stack(sv), jnp.stack(sS), jnp.stack(ssh))


_drawn_inputs = setup_inputs


def setup_inputs(seed=0):
    import zlib

    import numpy as np

    out = dict(_drawn_inputs(seed))
    spreads = {}
    factors = {'attn_sink': 8.0}
    for name, (base, spread) in spreads.items():
        noise = np.random.default_rng([zlib.crc32(name.encode()), seed]).standard_normal(out[name].shape)
        drawn = base * np.exp(spread * noise) if base else spread * noise
        out[name] = __import__('jax').numpy.asarray(drawn.astype(out[name].dtype))
    for name, factor in factors.items():
        out[name] = (out[name] * factor).astype(out[name].dtype)
    return out
```

```python
from contextlib import ExitStack

import numpy as np

import concourse.bass as bass
from concourse import mybir

F32 = mybir.dt.float32
F32R = mybir.dt.float32r
ALU = mybir.AluOpType
ACT = mybir.ActivationFunctionType
AX = mybir.AxisListType

P = 128
D_MODEL, SEQ, DEC_SEQ, DEPTH, PAST_LEN = 1024, 1024, 32, 2, 512
T = SEQ + DEC_SEQ
CH = 3
CW = T // CH
DB = D_MODEL // P
HEAD, CHUNK, WINDOW = 64, 64, 128
A_WIDTH, KV_A, R_WIDTH = 512, 128, 512
N_HEADS_A = 8
PAIRS = R_WIDTH // P
UNITS = SEQ // 256
LORA_W, LORA_A, LORA_G = 64, 64, 160
RWKV_PROJ = 3 * R_WIDTH + LORA_W + LORA_A + LORA_G
IN_COLS = A_WIDTH + 2 * KV_A + RWKV_PROJ
R0 = A_WIDTH + 2 * KV_A
MEM, MEM_HEADS, MEM_WIDTH = 256, 4, 512
D_FF = 2816
FB = D_FF // P
TILES = SEQ // P
RMS_EPS, GN_EPS = 1e-6, 6.4e-4
NEG = -1e30
DECAY = float(np.exp(-0.5))
MIX_PRE, MIX_POST, X_PRE, X_POST, N_MEM, FFN_PRE, FFN_POST = range(7)

G_AT, MU_AT, SH_AT, RV_AT, RK_AT, PRM_ROWS = 0, 56, 71, 86, 110, 114
C_ID, C_PERM, C_ONE, C_BD, C_BDM, C_CEN = (i * P for i in range(6))
C_M3 = 6 * P
C_NL = 9 * P
C_NU = 10 * P
C_LV = 11 * P
C_AE = 16 * P
C_AO = C_AE + 4 * 256
C_EPS = C_AO + 256
C_COLS = C_EPS + 2


def constants():
    c = np.zeros((P, C_COLS), np.float32)
    i, j = np.arange(P)[:, None], np.arange(P)[None, :]
    same = (i // 64) == (j // 64)
    c[:, C_ID:C_ID + P] = i == j
    c[:, C_PERM:C_PERM + P] = np.where((j % 64 < 32) & (i == j + 32), -1.0, 0.0) + ((j % 64 >= 32) & (i == j - 32))
    c[:, C_ONE:C_ONE + P] = 1.0
    c[:, C_BD:C_BD + P] = same
    c[:, C_BDM:C_BDM + P] = same / 64.0
    c[:, C_CEN:C_CEN + P] = (i == j) - same / 64.0
    c[:, C_M3:C_M3 + 2 * P] = np.tile(same & (i < j), (1, 2))
    c[:, C_M3 + 2 * P:C_M3 + 3 * P] = same & (i <= j)
    c[:, C_NL:C_NL + P] = -1.0 * ((i // 2 == j // 2) & (i > j))
    c[:, C_NU:C_NU + P] = -1.0 * ((i // 2 == j // 2) & (i < j))
    for n in range(5):
        s = 2 << n
        c[:, C_LV + n * P:C_LV + (n + 1) * P] = (i // (2 * s) == j // (2 * s)) & (i // s < j // s)
    cur = np.where((i < 64) & (j >= 64), NEG, 0.0)
    prev = np.where((i >= 64) & (j < 64), NEG, 0.0)
    for it in range(4):
        at = C_AE + it * 256
        c[:, at:at + P] = cur
        c[:, at + P:at + 2 * P] = NEG if it == 0 else prev
    c[:, C_AO:C_AO + P] = prev
    c[:, C_AO + P:C_AO + 2 * P] = cur
    c[:, C_EPS] = RMS_EPS
    c[:, C_EPS + 1] = GN_EPS
    pos = np.concatenate([np.arange(SEQ), PAST_LEN + np.arange(DEC_SEQ)]).astype(np.float32)
    inv = np.float32(10000.0) ** (-np.arange(32, dtype=np.float32) / np.float32(32))
    ang = (pos[None, :] * inv[:, None]).astype(np.float32)
    long = np.zeros((2, P, T), np.float32)
    long[0] = np.tile(np.cos(ang), (4, 1))
    long[1] = np.tile(np.sin(ang), (4, 1))
    return c, long


def program(nc, io):
    with ExitStack() as ctx:
        build(nc, io, ctx)


def build(nc, io, ctx):
    def sb(name, shape, dt=F32):
        return ctx.enter_context(nc.sbuf_tensor(name, shape, dt))

    R1 = sb("R1", [P, DB, T])
    R2 = sb("R2", [P, DB, T])
    HH, HL = sb("HH", [P, DB, T], F32R), sb("HL", [P, DB, T], F32R)
    GH, GL = sb("GH", [P, 2, T], F32R), sb("GL", [P, 2, T], F32R)
    TMP = sb("TMP", [P, 3, T])
    WRAW = sb("WRAW", [P, 2, 1024])
    WH, WL = sb("WH", [P, 2, 1024], F32R), sb("WL", [P, 2, 1024], F32R)
    CST = sb("CST", [P, C_COLS])
    PRM = sb("PRM", [P, PRM_ROWS])
    PC = sb("PC", [P, 16])
    SINK = sb("SINK", [P, 8])
    ST = sb("ST", [P, 64])
    EC = sb("EC", [P, 40])
    AUX = sb("AUX", [P, 1088])
    PS = ctx.enter_context(nc.psum_tensor("PS", [P, 8 * 512], F32))

    x_spill = nc.dram_tensor("x_spill", [P, DB, T], F32, kind="Internal").ap()
    mix_dram = nc.dram_tensor("mix_dram", [P, DB, T], F32, kind="Internal").ap()
    mem_dram = nc.dram_tensor("mem_dram", [P, DB, MEM], F32, kind="Internal").ap()

    for_vector = {n + "_psum" for n in ("swap", "score", "sm", "l", "dx", "u", "ds", "kk", "rk", "sin", "cs", "up", "down", "xT_dve")}
    sems = {}

    def S(name):
        if name.endswith("_psum"):
            name = "product_for_vector" if name in for_vector else "product_for_scalar"
        if name not in sems:
            sems[name] = ctx.enter_context(nc.semaphore(name))
        return sems[name]

    def give(e, *names):
        for name in names:
            e.sem_inc(S(name), 1)

    def bank(b, a=0, z=512):
        return PS[:, b * 512 + a:b * 512 + z]

    ENG = ["act", "dve", "pe", "pool"]

    def barrier(e, who):
        e.drain()
        for other in ENG:
            if other != who:
                give(e, f"end_{who}_{other}")
        for other in ENG:
            if other != who:
                e.wait_ge(S(f"end_{other}_{who}"), 1)
                e.sem_inc(S(f"end_{other}_{who}"), -1)

    def cst(at, w=P):
        return CST[:, at:at + w]

    ident, perm, ones = cst(C_ID), cst(C_PERM), cst(C_ONE)

    def chunk(c):
        return slice(c * CW, (c + 1) * CW)

    r2flat = R2[:, :, :].rearrange("p a t -> p (a t)")
    tflat = TMP[:, :, :].rearrange("p a t -> p (a t)")
    PRAW = r2flat[:, 6 * T:6 * T + T + 2]
    r1tail = R1[:, 7, :]
    RT = r1tail[:, 0:768].rearrange("p (a t) -> p a t", t=P)
    SC = r2flat[:, 3 * T:3 * T + 2048].rearrange("p (h k) -> p h k", h=8)
    PT = tflat[:, 0:2048].rearrange("p (h k q) -> p h k q", h=8, k=2)
    RU = TMP[:, 2, 0:768].rearrange("p (a t) -> p a t", t=P)
    VST = TMP[:, 2, 768:896]
    KCR = TMP[:, 2, 896:1024]
    QR = R2[:, 5, 0:512].rearrange("p (a t) -> p a t", t=P)
    KR = R2[:, 5, 512:1024].rearrange("p (v s t) -> p v s t", v=2, s=2)
    VT = AUX[:, 0:256].rearrange("p (s t) -> p s t", s=2)
    OT = AUX[:, 256:768].rearrange("p (a t) -> p a t", t=P)
    KO = AUX[:, 768:896]
    COS, SIN = R2[:, 6, :], R2[:, 7, :]
    KK, RR, BB, KF, VV, GG, BON, YY = (R1[:, i, :] for i in range(8))
    TWA, SG1, SG2, DD2, DD, SEG = (R2[:, i, :] for i in range(6))
    LTM, XXF = r2flat[:, 3 * T:3 * T + 1536], r2flat[:, 3 * T + 1536:3 * T + 2560]
    T1F = r2flat[:, 3 * T + 2560:3 * T + 3072]
    ATM = AUX[:, 768:1024].rearrange("p (x t) -> p x t", x=2)
    QS = tflat[:, 2560:2816].rearrange("p (x t) -> p x t", x=2)
    w0 = 6 * T
    US = r2flat[:, w0:w0 + 256].rearrange("p (x t) -> p x t", x=2)
    MVS = r2flat[:, w0 + 256:w0 + 512].rearrange("p (x t) -> p x t", x=2)
    ELF = r2flat[:, w0 + 512:w0 + 1536]
    PTS = r2flat[:, w0 + 1536:w0 + 1792].rearrange("p (x t) -> p x t", x=2)

    def unit(u):
        return (u * 256, P, 2, 5) if u < UNITS else (SEQ, DEC_SEQ, 1, 4)

    def bkv(u):
        return tflat[:, (u % 2) * 768:(u % 2 + 1) * 768].rearrange("p (x a t) -> p x a t", x=2, a=3)

    def heads(buf, at, n, tiles):
        return buf[0:n, at:at + 2 * tiles * n].rearrange("p (g t) -> p g t", g=2 * tiles)

    SBD = AUX[:, 0:128]
    STMP = AUX[:, 128:256]
    SIO = AUX[:, 256:384]
    LW = AUX[:, 384:768]
    SHC = AUX[:, 1024:1056]
    xq = r2flat[:, 4 * T:8 * T]
    CKT = xq[:, 0:1024].rearrange("p (h k) -> p h k", h=4)
    CV = xq[:, 1024:2048].rearrange("p (k d) -> p k d", k=2)
    CKR = xq[:, 2048:3072].rearrange("p (k d) -> p k d", k=2)
    CP = xq[:, 3072:4096].rearrange("p (h k) -> p h k", h=4)
    CPT = tflat[:, 0:1024].rearrange("p (h k q) -> p h k q", h=4, k=2)
    CQ = tflat[:, 1024:1536].rearrange("p (h q) -> p h q", h=4)

    HS = [0, 2, 4, 6, 1, 3, 5, 7]
    block = ctx.enter_context(nc.Block())

    def w_block(w, l, c0, cols=P, kb=DB):
        return w[bass.ds(l, 1)].rearrange("a (k p) n -> p (a k) n", p=P)[:, 0:kb, bass.ds(c0, cols)]

    @block.sync
    def _(e):
        def weight(slot, src, view=None):
            e.wait_ge(S(f"w_free{slot}"), 1)
            e.sem_inc(S(f"w_free{slot}"), -1)
            dst = WRAW[:, slot, :]
            e.dma_start(view(dst) if view else dst, src).then_inc(S(f"w_full{slot}"), 16)

        def w8(slot, w, l, c0):
            weight(slot, w_block(w, l, c0), view=lambda d: d.rearrange("p (k n) -> p k n", k=DB))

        def stream(w, l, pairs, c0=0):
            with e.Fori(0, pairs) as i:
                for s in range(2):
                    w8(s, w, l, (i * 2 + s) * P + c0)

        with e.Fori(0, DEPTH) as l:
            stream(io["w_mem_kv"], l, 4)
            stream(io["w_in"], l, 2)
            for s in range(2):
                e.wait_ge(S(f"w_free{s}"), 1)
                e.sem_inc(S(f"w_free{s}"), -1)
                for g in range(2):
                    done = "k_part" if g == 0 else f"w_full{s}"
                    e.dma_start(WRAW[:, s, :].rearrange("p (k g n) -> p k g n", k=DB, g=2)[:, :, g, :],
                                w_block(io["w_in"], l, A_WIDTH + s * HEAD, HEAD)).then_inc(S(done), 16)
                    if g == 0:
                        e.wait_ge(S("k_part"), 16)
                        e.sem_inc(S("k_part"), -16)
            w8(0, io["w_in"], l, A_WIDTH + KV_A)
            w8(1, io["w_in"], l, R0 + 3 * R_WIDTH)
            w8(0, io["w_in"], l, R0 + 3 * R_WIDTH + P)
            weight(1, w_block(io["w_in"], l, R0 + 3 * R_WIDTH + 2 * P, 32),
                   view=lambda d: d.rearrange("p (k n) -> p k n", k=DB)[:, :, 0:32])
            with e.Fori(0, PAIRS) as j:
                for b in range(3):
                    w8(b % 2, io["w_in"], l, j * P + R0 + b * R_WIDTH)
                e.wait_ge(S("w_free1"), 1)
                e.sem_inc(S("w_free1"), -1)
                lw = WRAW[:, 1, :]
                parts = ((lw[0:64, 0:P], io["rwkv_w2"][bass.ds(l, 1)]), (lw[64:128, 0:P], io["rwkv_a2"][bass.ds(l, 1)]),
                         (lw[:, P:2 * P], io["rwkv_g2"][bass.ds(l, 1), 0:P, :]),
                         (lw[0:32, 2 * P:3 * P], io["rwkv_g2"][bass.ds(l, 1), P:LORA_G, :]))
                for n, (dst, src) in enumerate(parts):
                    e.dma_start(dst, src.rearrange("a r n -> (a r) n")[:, bass.ds(j * P, P)]).then_inc(S("lw_part" if n < 3 else "w_full1"), 16)
                    if n == 2:
                        e.wait_ge(S("lw_part"), 48)
                        e.sem_inc(S("lw_part"), -48)
            stream(io["w_out"], l, 4)
            stream(io["w_mem_q"], l, 2)
            with e.Fori(0, 2) as i:
                for s in range(2):
                    weight(s, w_block(io["w_mem_o"], l, (i * 2 + s) * 2 * P, 2 * P, 4),
                           view=lambda d: d.rearrange("p (k n) -> p k n", k=4))
            with e.Fori(0, FB // 2) as i:
                for f in range(2):
                    w8(0, io["w_gate_up"], l, (i * 2 + f) * P)
                    w8(1, io["w_gate_up"], l, (i * 2 + f) * P + D_FF)
                for f in range(2):
                    weight(f, io["w_down"][bass.ds(l, 1), bass.ds((i * 2 + f) * P, P), :].rearrange("a p n -> p (a n)"))
        for s in range(2):
            weight(s, io["w_down"][0, 0:P, :])

    @block.gpsimd
    def _(e):
        due = e.alloc_register("moves_due")
        e.reg_mov(due, 0)

        def move(dst, src):
            e.dma_start(dst, src).then_inc(S("moves"), 16)

        def moved(n=1):
            e.reg_add(due, due, 16 * n)
            e.wait_ge(S("moves"), e.snap(due, min_val=16))
            give(e, "moves_seen")

        move(CST[:, :], io["consts"])
        moved()
        give(e, "cst_act", "cst_dve", "cst_pe")

        def tokens_in(src, rows):
            e.wait_ge(S("xin_free"), 1)
            e.sem_inc(S("xin_free"), -1)
            move(R2[0:rows, 0, 0:D_MODEL], src)
            moved()
            give(e, "xin_full")

        with e.Fori(0, MEM // P) as j:
            tokens_in(io["mem_prompt"][0, bass.ds(j * P, P), :], P)
        e.wait_ge(S("memT_ready"), 1)
        e.sem_inc(S("memT_ready"), -1)
        move(mem_dram, R1[:, :, 0:MEM])
        moved()
        give(e, "memT_saved_act", "memT_saved_dve")
        with e.Fori(0, TILES) as j:
            tokens_in(io["x_prompt"][0, bass.ds(j * P, P), :], P)
        tokens_in(io["x_sample"][0], DEC_SEQ)
        barrier(e, "pool")

        with e.Fori(0, DEPTH) as l:
            prow = TMP[:, 0, 0:P]

            def rows(at, src):
                move(prow[at:at + src.shape[0], 0:src.shape[1]], src)

            lay = lambda name: io[name][bass.ds(l, 1)]
            e.wait_ge(S("prow_clear"), 1)
            e.sem_inc(S("prow_clear"), -1)
            rows(G_AT, lay("norm_gains").rearrange("a n (b p) -> (a n b) p", p=P))
            for at, src in ((MU_AT, lay("shift_mu")), (SH_AT, lay("state_shift").rearrange("a b c n -> (a b c) n"))):
                rows(at, src[:, 0:14 * P].rearrange("a (b p) -> (a b) p", p=P))
                rows(at + 14, src[:, 14 * P:RWKV_PROJ])
            rows(RV_AT, lay("rwkv_vecs").rearrange("a n (b p) -> (a n b) p", p=P))
            rows(RK_AT, lay("rwkv_rk").rearrange("a (b g) p -> (a b) (g p)", g=2))
            move(SINK[:, :], lay("attn_sink").broadcast_to([P, 8]))
            moved(8)
            give(e, "prm_rows")
            move(R2[:, :, 0:MEM], mem_dram)
            moved()
            give(e, "memT_act", "memT_dve")
            move(x_spill, R1[:, :, :])
            moved()
            for k, out in ((0, "new_mem_k_prompt"), (1, "new_mem_v_prompt")):
                for tt in range(2):
                    e.wait_ge(S("memtok_ready"), 1)
                    e.sem_inc(S("memtok_ready"), -1)
                    move(lay(out).rearrange("a b m h d -> (a b m) (h d)")[tt * P:(tt + 1) * P, :], R2[:, 2 + 2 * k + tt, 512:1024])
            moved(4)
            barrier(e, "pool")
            e.wait_ge(S("cos_free"), 1)
            e.sem_inc(S("cos_free"), -1)
            move(COS, io["long"][0])
            move(SIN, io["long"][1])
            moved(2)
            give(e, "cos_ready")

            def store_att(n, c0):
                e.wait_ge(S("ot_ready"), 1)
                e.sem_inc(S("ot_ready"), -1)
                move(mix_dram[:, 0:4, bass.ds(c0, n)], OT[:, :, 0:n])
                moved()
                give(e, "ot_free")

            with e.Fori(0, TILES) as i:
                store_att(P, i * P)

            def store_kv(n, slot, okey, oval):
                e.wait_ge(S("ko_ready"), 1)
                e.sem_inc(S("ko_ready"), -1)
                move(lay(okey).rearrange("a b m h d -> (a b m) (h d)"), KO[0:n, :])
                move(lay(oval).rearrange("a b m h d -> (a b m) (h d)"), VT[0:n, slot, :])
                moved(2)

            store_kv(P, 1, "new_swa_k_prompt", "new_swa_v_prompt")
            for v in range(2):
                e.wait_ge(S("kcr_free"), 1)
                e.sem_inc(S("kcr_free"), -1)
                for g in range(2):
                    move(KCR[:, g * HEAD:(g + 1) * HEAD], lay("cache_swa_k").rearrange("a b m h d -> (a b m) h d")[:, v, :])
                moved(2)
                give(e, "kcr_ready")
            e.wait_ge(S("vt_free"), 1)
            e.sem_inc(S("vt_free"), -1)
            move(VT[:, 1, :], lay("cache_swa_v").rearrange("a b m h d -> (a b m) (h d)"))
            moved()
            give(e, "vcache_ready")
            store_att(DEC_SEQ, SEQ)
            store_kv(DEC_SEQ, 0, "new_swa_k_sample", "new_swa_v_sample")
            barrier(e, "pool")

            def level_masks(u):
                _, n, tiles, levels = unit(u)
                mask = lambda at: CST[0:n, at:at + n].unsqueeze(1).broadcast_to([n, 2 * tiles, n])
                lt, xt = heads(LTM, 0, n, tiles), heads(XXF, 512, n, tiles)
                e.wait_ge(S("lt_ready"), 1)
                e.sem_inc(S("lt_ready"), -1)
                for s in range(levels):
                    e.wait_ge(S("elt_free"), 1)
                    e.sem_inc(S("elt_free"), -1)
                    e.tensor_tensor(heads(ELF, (s % 2) * 512, n, tiles), lt, mask(C_LV + s * P), ALU.mult).then_inc(S("elt_ready"), 1)
                    if s == 0:
                        e.tensor_tensor(xt, lt, mask(C_NU), ALU.mult).then_inc(S("pool_done"), 1)
                        e.wait_ge(S("pool_done"), 1)
                        e.sem_inc(S("pool_done"), -1)
                        e.tensor_tensor(xt, xt, mask(C_ID), ALU.add).then_inc(S("xt_ready"), 1)

            with e.Fori(0, PAIRS) as j:
                def states(name, store):
                    dram = lay(name).rearrange("a b h v k -> (a b h v) k")
                    for h in range(2):
                        d = dram[bass.ds(j * P + h * HEAD, HEAD), :]
                        t = SIO[h * HEAD:(h + 1) * HEAD, h * HEAD:(h + 1) * HEAD]
                        move(d if store else t, t if store else d)
                    moved(2)

                for u in range(UNITS + 1):
                    level_masks(u)
                e.wait_ge(S("state_out"), 1)
                e.sem_inc(S("state_out"), -1)
                states("new_state_rwkv_prompt", True)
                states("state_rwkv", False)
                give(e, "state_in")
                e.wait_ge(S("state_out"), 1)
                e.sem_inc(S("state_out"), -1)
                states("new_state_rwkv_sample", True)
                give(e, "state_saved")
                e.wait_ge(S("y_ready"), 1)
                e.sem_inc(S("y_ready"), -1)
                move(mix_dram[:, bass.ds(j + 4, 1), :].rearrange("p a t -> p (a t)"), YY)
                moved()
                give(e, "y_saved")
            e.wait_ge(S("shc_ready"), 1)
            e.sem_inc(S("shc_ready"), -1)
            for g, out in ((0, "new_state_shift_prompt"), (1, "new_state_shift_sample")):
                o = lay(out).rearrange("a b c n -> (a b c) n")
                at = g * 64
                move(o[:, 0:14 * P].rearrange("a (b p) -> (a b) p", p=P), AUX[at:at + 14, 256:384])
                move(o[:, 14 * P:RWKV_PROJ], AUX[at + 14:at + 15, 256:288])
            moved(4)
            barrier(e, "pool")
            move(R2[:, :, :], mix_dram)
            move(R1[:, :, :], x_spill)
            moved(2)
            give(e, "mix_act", "mix_dve")
            barrier(e, "pool")

            def mem_in(ksrc, vsrc):
                e.wait_ge(S("cv_free"), 1)
                e.sem_inc(S("cv_free"), -1)
                for dst, name in ((CKR, ksrc), (CV, vsrc)):
                    move(dst, lay(name).rearrange("a b (t m) h d -> m (a b t) (h d)", t=2))
                moved(2)
                give(e, "ckr_ready")

            mem_in("new_mem_k_prompt", "new_mem_v_prompt")
            mem_in("cache_mem_k", "cache_mem_v")
            barrier(e, "pool")
            barrier(e, "pool")

        def tokens_out(dst, n):
            e.wait_ge(S("xout_ready"), 1)
            e.sem_inc(S("xout_ready"), -1)
            move(dst, R2[0:n, 4, 0:D_MODEL])
            moved()
            give(e, "xout_free")

        with e.Fori(0, TILES) as j:
            tokens_out(io["y_prompt"][0, bass.ds(j * P, P), :], P)
        tokens_out(io["y_sample"][0], DEC_SEQ)

    @block.tensor
    def _(e):
        def claim(*banks):
            for b in banks:
                e.wait_ge(S(f"bank{b}"), 1)
                e.sem_inc(S(f"bank{b}"), -1)

        def transposes(items, b, name, base=0):
            claim(b)
            for n, (src, off) in enumerate(items):
                k, m = src.shape
                ins = e.matmul(PS[0:m, b * 512 + off:b * 512 + off + k], src, CST[0:k, C_ID:C_ID + k],
                               is_transpose=True, start=True, stop=True)
            ins.then_inc(S(name), 1)

        def products(out, lhs, rhs, slot_w, n):
            first = True
            for k in range(n):
                for wp, xp in ((0, 0), (1, 0), (0, 1)):
                    ins = e.matmul(out, lhs(k, wp), rhs(k, xp), start=first, stop=(k == n - 1 and xp == 1))
                    first = False
            return ins

        def dense8(slot, b0, name, m=P, n=T, cw=CW, ch=CH):
            e.wait_ge(S(f"w_ready{slot}"), 1)
            e.sem_inc(S(f"w_ready{slot}"), -1)
            W = [x[:, slot, :].rearrange("p (k n) -> p k n", k=DB) for x in (WH, WL)]
            H = [HH, HL]
            for c in range(ch):
                claim(b0 + c)
                products(PS[0:m, (b0 + c) * 512:(b0 + c) * 512 + cw], lambda k, p: W[p][:, k, 0:m],
                         lambda k, p: H[p][:, k, c * cw:(c + 1) * cw], slot, DB).then_inc(S(name), 1)

        def stats(n=T):
            e.wait_ge(S("sq_sum"), 1)
            e.sem_inc(S("sq_sum"), -1)
            cw = CW if n == T else n
            for c in range(n // cw):
                claim(c)
                e.matmul(bank(c, 0, cw), ones, TMP[:, 2, c * cw:(c + 1) * cw], start=True, stop=True).then_inc(S("var_psum"), 1)

        e.wait_ge(S("cst_pe"), 1)
        e.sem_inc(S("cst_pe"), -1)

        def tokens_in(n):
            e.wait_ge(S("xin_full"), 1)
            e.sem_inc(S("xin_full"), -1)
            for g in range(2):
                transposes([(R2[0:n, 0, (4 * g + b) * P:(4 * g + b + 1) * P], b * P) for b in range(4)], g, "xT_psum" if g == 0 else "xT_dve_psum")
            
        with e.Fori(0, MEM // P) as j:
            tokens_in(P)
        with e.Fori(0, TILES) as j:
            tokens_in(P)
        tokens_in(DEC_SEQ)
        barrier(e, "pe")
        with e.Fori(0, DEPTH) as l:
            e.wait_ge(S("prm_rows_pe"), 1)
            e.sem_inc(S("prm_rows_pe"), -1)
            transposes([(TMP[0:PRM_ROWS, 0, 0:P], 0)], 7, "prm_psum")
            stats(MEM)
            e.wait_ge(S("h_ready"), 1)
            e.sem_inc(S("h_ready"), -1)
            with e.Fori(0, 4) as i:
                for s in range(2):
                    dense8(s, 3 * s, "dense_psum", n=MEM, cw=MEM, ch=1)
            e.wait_ge(S("kvT_ready"), 1)
            e.sem_inc(S("kvT_ready"), -1)
            for k in range(2):
                for tt in range(2):
                    transposes([(R2[:, k * 4 + b, MEM + tt * P:MEM + (tt + 1) * P], b * P) for b in range(4)], k * 2 + tt, "memtok_psum")
            stats()
            e.wait_ge(S("h_ready"), 1)
            e.sem_inc(S("h_ready"), -1)
            barrier(e, "pe")
            with e.Fori(0, 2) as i:
                for s in range(2):
                    dense8(s, 3 * s, "dense_psum")
            for n in range(6):
                dense8(n % 2, 3 * (n % 2), "dense_psum")
            e.wait_ge(S("cos_pe"), 1)
            e.sem_inc(S("cos_pe"), -1)

            def att(i, n, slot, parts):
                tok = bass.ds(i, n)
                claim(0, 1)
                e.matmul(PS[:, 0:4 * n].rearrange("p (a t) -> p a t", a=4), perm, R1[:, 0:4, tok], start=True, stop=True)
                e.matmul(PS[:, 512:512 + 2 * n].rearrange("p (a t) -> p a t", a=2), perm, R1[:, 4:6, tok], start=True, stop=True).then_inc(S("swap_psum"), 1)
                e.wait_ge(S("vst_ready"), 1)
                e.sem_inc(S("vst_ready"), -1)
                transposes([(VST[:, 0:n], 0)], 6, "v_psum")
                e.wait_ge(S("qk_ready"), 1)
                e.sem_inc(S("qk_ready"), -1)
                for hs, h in enumerate(HS):
                    p = (h % 2) * HEAD
                    if hs % 2 == 0:
                        claim(2 + hs // 2)
                    for ks, nk, col in parts:
                        at = 1024 + hs * 256 + col
                        ins = e.matmul(PS[0:n, at:at + nk], QR[p:p + HEAD, h // 2, 0:n], KR[p:p + HEAD, h // 4, ks, 0:nk] if not (len(parts) == 1)
                                       else KR[p:p + HEAD, h // 4, :, :].rearrange("p s t -> p (s t)"), start=True, stop=True)
                    if hs % 2 == 1:
                        ins.then_inc(S("score_psum"), 1)
                e.wait_ge(S("prob_ready"), 1)
                e.sem_inc(S("prob_ready"), -1)
                kparts = [(0, 0, P), (1, P, P)] if len(parts) == 1 else [(ks, col, nk) for ks, nk, col in parts]
                for g in range(4):
                    b = (0, 1, 6, 7)[g]
                    transposes([(SC[0:n, 2 * g + hh, col:col + nk], hh * 256 + kt * P) for hh in range(2)
                                for kt, (ks, col, nk) in enumerate(kparts)], b, "pT_psum")
                e.wait_ge(S("pT_ready"), 1)
                e.sem_inc(S("pT_ready"), -1)
                claim(2)
                for hs, h in enumerate(HS):
                    p, kv = (h % 2) * HEAD, h // 4
                    for kt, (ks, col, nk) in enumerate(kparts):
                        ins = e.matmul(PS[p:p + HEAD, 1024 + (h // 2) * n:1024 + (h // 2) * n + n],
                                       VT[0:nk, ks, kv * HEAD:(kv + 1) * HEAD], PT[0:nk, hs, kt, 0:n],
                                       start=(kt == 0), stop=(kt == 1))
                ins.then_inc(S("o_psum"), 1)

            def keys_out(n, slot):
                claim(0)
                for v in range(2):
                    ins = e.matmul(PS[0:n, v * HEAD:(v + 1) * HEAD], KR[0:HEAD, v, slot, 0:n], CST[0:HEAD, C_ID:C_ID + HEAD],
                                   is_transpose=True, start=True, stop=True)
                ins.then_inc(S("ko_psum"), 1)

            with e.Fori(0, TILES // 2) as i:
                for s in range(2):
                    att((i * 2 + s) * P, P, s, [(0, 256, 0)])
            keys_out(P, 1)
            for v in range(2):
                e.wait_ge(S("kcr_ready"), 1)
                e.sem_inc(S("kcr_ready"), -1)
                transposes([(KCR[:, :], 0)], v, "kc_psum")
            e.wait_ge(S("vcache_ready"), 1)
            e.sem_inc(S("vcache_ready"), -1)
            att(SEQ, DEC_SEQ, 0, [(0, DEC_SEQ, 0), (1, P, DEC_SEQ)])
            keys_out(DEC_SEQ, 0)
            barrier(e, "pe")

            def by_token(u):
                t0, n, tiles, _ = unit(u)
                for x in range(tiles):
                    transposes([(R1[:, a, t0 + x * n:t0 + (x + 1) * n], o * P) for o, a in enumerate((0, 2, 3, 4))], x, "tm_psum")

            def scores(u, x):
                t0, n, _, _ = unit(u)
                tok = slice(t0 + x * n, t0 + (x + 1) * n)
                for h in range(2):
                    p = slice(h * HEAD, (h + 1) * HEAD)
                    claim(2 + h)
                    out = PS[0:n, (2 + h) * 512:(2 + h) * 512 + 4 * n].rearrange("p (a t) -> p a t", a=4)
                    e.matmul(out[:, 0:4:3, :], R1[p, 2, tok], R1[p, 0:2, tok], start=True, stop=True)
                    e.matmul(out[:, 1:3, :], R1[p, 3, tok], R1[p, 0:2, tok], start=True, stop=True).then_inc(S("sm_psum"), 1)

            def low(u):
                t0, n, tiles, _ = unit(u)
                for h in range(2):
                    p = slice(h * HEAD, (h + 1) * HEAD)
                    claim(h)
                    for x in range(tiles):
                        tok = slice(t0 + x * n, t0 + (x + 1) * n)
                        ins = e.matmul(PS[0:n, h * 512 + x * n:h * 512 + (x + 1) * n], R1[p, 0, tok], R1[p, 2, tok], start=True, stop=True)
                    ins.then_inc(S("l_psum"), 1)

            def value_parts(u):
                _, n, tiles, _ = unit(u)
                e.wait_ge(S("tm_ready"), 1)
                e.sem_inc(S("tm_ready"), -1)
                e.wait_ge(S("sm_ready"), 1)
                e.sem_inc(S("sm_ready"), -1)
                yb = (4, 7)[u % 2]
                claim(yb)
                for x in range(tiles):
                    for h in range(2):
                        e.matmul(PS[h * HEAD:(h + 1) * HEAD, yb * 512 + x * n:yb * 512 + (x + 1) * n], bkv(u)[0:n, x, 2, h * HEAD:(h + 1) * HEAD],
                                 heads(LTM, 1024, n, tiles)[:, 2 * x + h, :], start=(x == 0), stop=False, skip_group_check=True)
                claim(3)
                for x in range(tiles):
                    for h in range(2):
                        at = 1536 + x * P + h * HEAD
                        ins = e.matmul(PS[0:n, at:at + HEAD], heads(LTM, 512, n, tiles)[:, 2 * x + h, :], bkv(u)[0:n, x, 2, h * HEAD:(h + 1) * HEAD],
                                       start=True, stop=True)
                ins.then_inc(S("mv_psum"), 1)

            def level_left(u, s):
                _, n, tiles, _ = unit(u)
                e.wait_ge(S("elt_ready"), 1)
                e.sem_inc(S("elt_ready"), -1)
                e.wait_ge(S("x_ready"), 1)
                e.sem_inc(S("x_ready"), -1)
                claim(2)
                for g in range(2 * tiles):
                    ins = e.matmul(PS[0:n, 1024 + g * n:1024 + (g + 1) * n], heads(ELF, (s % 2) * 512, n, tiles)[:, g, :],
                                   heads(XXF, 0, n, tiles)[:, g, :], start=True, stop=True)
                ins.then_inc(S("t1_psum"), 1)

            def level_right(u, s):
                _, n, tiles, levels = unit(u)
                xt, t1 = heads(XXF, 512, n, tiles), heads(T1F, 0, n, tiles)
                e.wait_ge(S("t1_ready"), 1)
                e.sem_inc(S("t1_ready"), -1)
                e.wait_ge(S("xt_ready"), 1)
                e.sem_inc(S("xt_ready"), -1)
                if s < levels - 1:
                    claim(0)
                    for g in range(2 * tiles):
                        ins = e.matmul(PS[0:n, g * n:(g + 1) * n], xt[:, g, :], t1[:, g, :], start=True, stop=True)
                    ins.then_inc(S("dx_psum"), 1)
                claim(1)
                for g in range(2 * tiles):
                    ins = e.matmul(PS[0:n, 512 + g * n:512 + (g + 1) * n], t1[:, g, :], xt[:, g, :], start=True, stop=True)
                ins.then_inc(S("dx_psum"), 1)

            def solved(u):
                _, n, tiles, _ = unit(u)
                xt = heads(XXF, 512, n, tiles)
                e.wait_ge(S("xt_ready"), 1)
                e.sem_inc(S("xt_ready"), -1)
                claim(2)
                for x in range(tiles):
                    for h in range(2):
                        ins = e.matmul(PS[h * HEAD:(h + 1) * HEAD, 1024 + x * n:1024 + (x + 1) * n], ATM[0:n, x, h * HEAD:(h + 1) * HEAD],
                                       xt[:, 2 * x + h, :], start=True, stop=True)
                ins.then_inc(S("pts_psum"), 1)
                e.wait_ge(S("mv_ready"), 1)
                e.sem_inc(S("mv_ready"), -1)
                claim(3)
                for x in range(tiles):
                    for h in range(2):
                        at = 1536 + x * P + h * HEAD
                        ins = e.matmul(PS[0:n, at:at + HEAD], xt[:, 2 * x + h, :], MVS[0:n, x, h * HEAD:(h + 1) * HEAD], start=True, stop=True)
                ins.then_inc(S("q_psum"), 1)

            def chunk_u(u, c):
                t0, n, _, _ = unit(u)
                cn, x, yb = min(n, CHUNK), c // 2, (4, 7)[u % 2]
                a = (c % 2) * CHUNK
                if c == 0:
                    e.wait_ge(S("pq_ready"), 1)
                    e.sem_inc(S("pq_ready"), -1)
                e.wait_ge(S("state_ready"), 1)
                e.sem_inc(S("state_ready"), -1)
                claim(6)
                e.matmul(PS[a:a + cn, 3072:3072 + P], PTS[:, x, a:a + cn], SBD, start=True, stop=True).then_inc(S("u_psum"), 1)
                e.matmul(PS[:, yb * 512 + c * CHUNK:yb * 512 + c * CHUNK + cn], SBD, RR[:, t0 + c * CHUNK:t0 + c * CHUNK + cn],
                         start=False, stop=False, skip_group_check=True)

            def chunk_state(u, c):
                _, n, _, _ = unit(u)
                r, x = slice((c % 2) * CHUNK, (c % 2) * CHUNK + min(n, CHUNK)), c // 2
                e.wait_ge(S("u_ready"), 1)
                e.sem_inc(S("u_ready"), -1)
                claim(5)
                e.matmul(PS[:, 2560:2560 + P], bkv(u)[r, x, 1, :], bkv(u)[r, x, 2, :], start=True, stop=False)
                e.matmul(PS[:, 2560:2560 + P], bkv(u)[r, x, 0, :], US[r, x, :], start=False, stop=True).then_inc(S("ds_psum"), 1)

            def outputs(u):
                _, n, tiles, _ = unit(u)
                yb = (4, 7)[u % 2]
                for x in range(tiles):
                    for h in range(2):
                        ins = e.matmul(PS[h * HEAD:(h + 1) * HEAD, yb * 512 + x * n:yb * 512 + (x + 1) * n], US[0:n, x, h * HEAD:(h + 1) * HEAD],
                                       heads(tflat, 1536 + (u % 2) * 512, n, tiles)[:, 2 * x + h, :], start=False, stop=True, skip_group_check=True)
                ins.then_inc(S("y_psum"), 1)

            with e.Fori(0, PAIRS) as j:
                for s in (0, 1, 0):
                    dense8(s, 3 * s, "dense_psum")
                e.wait_ge(S("w_ready1"), 1)
                e.sem_inc(S("w_ready1"), -1)
                e.wait_ge(S("lw_ready"), 1)
                e.sem_inc(S("lw_ready"), -1)
                for c in range(CH):
                    claim(3 + c)
                    e.matmul(bank(3 + c, 0, CW), LW[0:64, 0:P], TWA[0:64, chunk(c)], start=True, stop=True).then_inc(S("z_psum"), 1)
                for c in range(CH):
                    claim(c)
                    e.matmul(bank(c, 0, CW), LW[64:128, 0:P], TWA[64:128, chunk(c)], start=True, stop=True).then_inc(S("z_psum"), 1)
                for c in range(CH):
                    claim(3 + c)
                    e.matmul(bank(3 + c, 0, CW), LW[:, P:2 * P], SG1[:, chunk(c)], start=True, stop=False)
                    e.matmul(bank(3 + c, 0, CW), LW[0:32, 2 * P:3 * P], SG2[0:32, chunk(c)], start=False, stop=True).then_inc(S("z_psum"), 1)
                e.wait_ge(S("kksq_ready"), 1)
                e.sem_inc(S("kksq_ready"), -1)
                for c in range(CH):
                    claim(c)
                    e.matmul(bank(c, 0, CW), cst(C_BD), TMP[:, 0, chunk(c)], start=True, stop=True).then_inc(S("kk_psum"), 1)
                e.wait_ge(S("rk_ready"), 1)
                e.sem_inc(S("rk_ready"), -1)
                for c in range(CH):
                    claim(3 + c)
                    e.matmul(bank(3 + c, 0, CW), cst(C_BD), TMP[:, 1, chunk(c)], start=True, stop=True).then_inc(S("rk_psum"), 1)
                e.wait_ge(S("til_ready"), 1)
                e.sem_inc(S("til_ready"), -1)
                for u in range(UNITS + 1):
                    _, _, tiles, levels = unit(u)
                    by_token(u)
                    if u > 0:
                        chunk_u(u - 1, 0)
                    scores(u, 0)
                    if u > 0:
                        chunk_state(u - 1, 0)
                    low(u)
                    if tiles == 2:
                        scores(u, 1)
                    value_parts(u)
                    for s in range(levels):
                        level_left(u, s)
                        if u > 0 and s < 3:
                            chunk_u(u - 1, s + 1)
                        level_right(u, s)
                        if u > 0 and s < 3:
                            chunk_state(u - 1, s + 1)
                    if u > 0:
                        outputs(u - 1)
                    solved(u)

                def state_out():
                    e.wait_ge(S("state_ready"), 1)
                    e.sem_inc(S("state_ready"), -1)
                    transposes([(SBD, 0)], 0, "sio_psum")

                state_out()
                e.wait_ge(S("state_in"), 1)
                e.sem_inc(S("state_in"), -1)
                transposes([(SIO, 0)], 1, "sin_psum")
                chunk_u(UNITS, 0)
                chunk_state(UNITS, 0)
                outputs(UNITS)
                state_out()
                e.wait_ge(S("yy_ready"), 1)
                e.sem_inc(S("yy_ready"), -1)
                for c in range(CH):
                    claim(c)
                    e.matmul(bank(c, 0, CW), cst(C_CEN), YY[:, chunk(c)], start=True, stop=True).then_inc(S("yc_psum"), 1)
                e.wait_ge(S("ysq_ready"), 1)
                e.sem_inc(S("ysq_ready"), -1)
                for c in range(CH):
                    claim(3 + c)
                    e.matmul(bank(3 + c, 0, CW), cst(C_BDM), TMP[:, 0, chunk(c)], start=True, stop=True).then_inc(S("yv_psum"), 1)
            e.wait_ge(S("shc_full"), 1)
            e.sem_inc(S("shc_full"), -1)
            claim(0)
            for g in range(2):
                ins = e.matmul(PS[g * 64:g * 64 + 16, 0:P], SHC[:, g * 16:(g + 1) * 16], ident, start=True, stop=True)
            ins.then_inc(S("shc_psum"), 1)
            barrier(e, "pe")
            e.wait_ge(S("h_ready"), 1)
            e.sem_inc(S("h_ready"), -1)
            with e.Fori(0, 4) as i:
                for s in range(2):
                    dense8(s, 3 * s, "dense_psum")
            stats()
            barrier(e, "pe")
            stats()
            e.wait_ge(S("h_ready"), 1)
            e.sem_inc(S("h_ready"), -1)
            with e.Fori(0, 2) as i:
                for s in range(2):
                    dense8(s, 3 * s, "dense_psum")

            def mem_keys():
                e.wait_ge(S("ckr_ready"), 1)
                e.sem_inc(S("ckr_ready"), -1)
                for kt in range(2):
                    transposes([(CKR[:, kt, h * P:(h + 1) * P], h * P) for h in range(4)], 6 + kt, "ckt_psum")
                e.wait_ge(S("ckt_ready"), 1)
                e.sem_inc(S("ckt_ready"), -1)

            def cross(n):
                e.wait_ge(S("cq_ready"), 1)
                e.sem_inc(S("cq_ready"), -1)
                claim(0, 1)
                for h in range(4):
                    ins = e.matmul(PS[0:n, h * MEM:(h + 1) * MEM], CQ[:, h, 0:n], CKT[:, h, :], start=True, stop=True)
                ins.then_inc(S("cs_psum"), 1)
                e.wait_ge(S("cp_ready"), 1)
                e.sem_inc(S("cp_ready"), -1)
                for g in range(2):
                    transposes([(CP[0:n, 2 * g + hh, kt * P:(kt + 1) * P], (hh * 2 + kt) * P) for hh in range(2) for kt in range(2)], 2 + g, "cpt_psum")
                e.wait_ge(S("cpt_ready"), 1)
                e.sem_inc(S("cpt_ready"), -1)
                claim(4)
                for h in range(4):
                    for kt in range(2):
                        ins = e.matmul(PS[:, 2048 + h * n:2048 + (h + 1) * n], CV[:, kt, h * P:(h + 1) * P], CPT[:, h, kt, 0:n],
                                       start=(kt == 0), stop=(kt == 1))
                ins.then_inc(S("co_psum"), 1)

            mem_keys()
            with e.Fori(0, TILES) as t:
                cross(P)
            mem_keys()
            cross(DEC_SEQ)
            e.wait_ge(S("h_ready"), 1)
            e.sem_inc(S("h_ready"), -1)
            with e.Fori(0, 2) as i:
                for s in range(2):
                    e.wait_ge(S(f"w_ready{s}"), 1)
                    e.sem_inc(S(f"w_ready{s}"), -1)
                    W = [x[:, s, :].rearrange("p (k n) -> p k n", k=4) for x in (WH, WL)]
                    for o in range(2):
                        for c in range(CH):
                            claim(3 * o + c)
                            products(bank(3 * o + c, 0, CW), lambda k, p: W[p][:, k, o * P:(o + 1) * P],
                                     lambda k, p: (HH, HL)[p][:, k, chunk(c)], s, 4).then_inc(S("dense_psum"), 1)
            stats()
            barrier(e, "pe")
            stats()
            e.wait_ge(S("h_ready"), 1)
            e.sem_inc(S("h_ready"), -1)
            with e.Fori(0, FB // 2) as i:
                for f in range(2):
                    dense8(0, 0, "gate_psum")
                    dense8(1, 3, "up_psum")
                e.wait_ge(S("w_ready0"), 1)
                e.sem_inc(S("w_ready0"), -1)
                e.wait_ge(S("w_ready1"), 1)
                e.sem_inc(S("w_ready1"), -1)
                n = 0
                for c in range(CH):
                    e.wait_ge(S("g_ready"), 2)
                    e.sem_inc(S("g_ready"), -2)
                    for m in range(DB):
                        b = 6 + n % 2
                        n += 1
                        claim(b)
                        products(bank(b, 0, CW), lambda k, p: (WH, WL)[p][:, k, m * P:(m + 1) * P],
                                 lambda k, p: (GH, GL)[p][:, k, chunk(c)], 0, 2).then_inc(S("down_psum"), 1)
            stats()
            barrier(e, "pe")

        def tokens_out(n):
            e.wait_ge(S("xo_ready"), 1)
            e.sem_inc(S("xo_ready"), -1)
            for g in range(2):
                transposes([(R2[:, 0, 0:1024].rearrange("p (b t) -> p b t", b=8)[:, 4 * g + b, 0:n], b * P) for b in range(4)], g, "xo_psum")

        with e.Fori(0, TILES) as j:
            tokens_out(P)
        tokens_out(DEC_SEQ)

    @block.scalar
    def _(e):
        def copy(dst, src):
            return e.copy(dst, src)

        def split(slot):
            e.wait_ge(S(f"w_full{slot}"), 16)
            e.sem_inc(S(f"w_full{slot}"), -16)
            copy(WH[:, slot, :], WRAW[:, slot, :]).then_inc(S(f"wh_ready{slot}"), 1)

        def evac(slot, dst, m=P, cw=CW, ch=CH, name="dense_psum", b0=None, then=True):
            b0 = 3 * slot if b0 is None else b0
            for c in range(ch):
                e.wait_ge(S(name), 1)
                e.sem_inc(S(name), -1)
                for out, a, z in dst(c):
                    ins = copy(out, PS[0:m, (b0 + c) * 512 + a:(b0 + c) * 512 + z])
                ins.then_inc(S("act_done"), 1)
                e.wait_ge(S("act_done"), 1)
                e.sem_inc(S("act_done"), -1)
                give(e, f"bank{b0 + c}")
            if then:
                split(slot)

        def squares(src, n=T):
            for b in range(DB):
                e.wait_ge(S("sq_free"), 1)
                e.sem_inc(S("sq_free"), -1)
                e.activation(TMP[:, b % 2, 0:n], src[:, b, 0:n], ACT.Square).then_inc(S("sq_ready"), 1)
            cw = CW if n == T else n
            for c in range(n // cw):
                e.wait_ge(S("var_psum"), 1)
                e.sem_inc(S("var_psum"), -1)
                ins = e.activation(TMP[:, 0, c * cw:(c + 1) * cw], bank(c, 0, cw), ACT.Sqrt, bias=CST[:, C_EPS:C_EPS + 1], scale=1.0 / D_MODEL)
                ins.then_inc(S("act_done"), 1)
                e.wait_ge(S("act_done"), 1)
                e.sem_inc(S("act_done"), -1)
                give(e, f"bank{c}", "rms_ready")

        def highs(n=T):
            for b in range(DB):
                e.wait_ge(S("ht_ready"), 1)
                e.sem_inc(S("ht_ready"), -1)
                copy(HH[:, b, 0:n], TMP[:, 1 + b % 2, 0:n]).then_inc(S("hh_ready"), 1)

        e.wait_ge(S("cst_act"), 1)
        e.sem_inc(S("cst_act"), -1)
        for b in range(8):
            give(e, f"bank{b}")

        def tokens_in(n, dst):
            e.wait_ge(S("xT_psum"), 1)
            e.sem_inc(S("xT_psum"), -1)
            ins = copy(dst, PS[:, 0:512].rearrange("p (b t) -> p b t", b=4)[:, :, 0:n])
            ins.then_inc(S("act_done"), 1)
            e.wait_ge(S("act_done"), 1)
            e.sem_inc(S("act_done"), -1)
            give(e, "bank0", "xin_act")

        give(e, "sq_free", "sq_free", "ot_free", "elt_free", "elt_free")
        with e.Fori(0, MEM // P) as j:
            tokens_in(P, R1[:, 0:4, bass.ds(j * P, P)])
        e.wait_ge(S("memT_saved_act"), 1)
        e.sem_inc(S("memT_saved_act"), -1)
        with e.Fori(0, TILES) as j:
            tokens_in(P, R1[:, 0:4, bass.ds(j * P, P)])
        tokens_in(DEC_SEQ, R1[:, 0:4, SEQ:T])
        barrier(e, "act")
        split(0)
        split(1)
        with e.Fori(0, DEPTH) as l:
            e.wait_ge(S("prm_psum"), 1)
            e.sem_inc(S("prm_psum"), -1)
            ins = copy(PRM[:, :], PS[:, 3584:3584 + PRM_ROWS])
            ins.then_inc(S("act_done"), 1)
            e.wait_ge(S("act_done"), 1)
            e.sem_inc(S("act_done"), -1)
            give(e, "bank7", "prm_ready")
            e.wait_ge(S("memT_act"), 1)
            e.sem_inc(S("memT_act"), -1)
            squares(R2, MEM)
            highs(MEM)
            with e.Fori(0, 4) as i:
                for s in range(2):
                    evac(s, lambda c: [(R2[:, bass.ds(i * 2 + s, 1), MEM:2 * MEM].rearrange("p a m -> p (a m)"), 0, MEM)], cw=MEM, ch=1)
            give(e, "kvT_ready")
            for k in range(4):
                e.wait_ge(S("memtok_psum"), 1)
                e.sem_inc(S("memtok_psum"), -1)
                ins = copy(R2[:, 2 + k, 512:1024], bank(k))
                ins.then_inc(S("act_done"), 1)
                e.wait_ge(S("act_done"), 1)
                e.sem_inc(S("act_done"), -1)
                give(e, f"bank{k}", "memtok_ready")
            squares(R1)
            highs()
            barrier(e, "act")
            with e.Fori(0, 2) as i:
                for s in range(2):
                    evac(s, lambda c: [(R1[:, bass.ds(i * 2 + s, 1), chunk(c)].rearrange("p a t -> p (a t)"), 0, CW)])
            for s in range(2):
                evac(s, lambda c: [(R1[:, 4 + s, chunk(c)], 0, CW)])
            evac(0, lambda c: [(R1[:, 6, chunk(c)], 0, CW)])

            def raw(m=P):
                def dst(c):
                    if c < CH - 1:
                        return [(PRAW[0:m, 1 + c * CW:1 + (c + 1) * CW], 0, CW)]
                    w = SEQ - c * CW
                    return [(PRAW[0:m, 1 + c * CW:1 + SEQ], 0, w), (PRAW[0:m, SEQ + 2:T + 2], w, CW)]
                return dst

            for n, (s, m) in enumerate(((1, P), (0, P), (1, 32))):
                e.wait_ge(S("praw_free"), 1)
                e.sem_inc(S("praw_free"), -1)
                evac(s, raw(m), m=m)
                give(e, "praw_ready")
            e.wait_ge(S("lora_ready"), 1)
            e.sem_inc(S("lora_ready"), -1)
            e.activation(TWA[0:64, :], TWA[0:64, :], ACT.Tanh).then_inc(S("act_done"), 1)
            e.wait_ge(S("act_done"), 1)
            e.sem_inc(S("act_done"), -1)
            e.activation(SG1, SG1, ACT.Sigmoid).then_inc(S("act_done"), 1)
            e.wait_ge(S("act_done"), 1)
            e.sem_inc(S("act_done"), -1)
            e.activation(SG2[0:32, :], SG2[0:32, :], ACT.Sigmoid).then_inc(S("act_done"), 1)
            e.wait_ge(S("act_done"), 1)
            e.sem_inc(S("act_done"), -1)

            def att(i, n, slot, width, kts):
                copy(VST[:, 0:n], R1[:, 6, bass.ds(i, n)]).then_inc(S("vst_ready"), 1)
                e.wait_ge(S("v_psum"), 1)
                e.sem_inc(S("v_psum"), -1)
                copy(VT[0:n, slot, :], PS[0:n, 3072:3072 + P]).then_inc(S("act_done"), 1)
                e.wait_ge(S("act_done"), 1)
                e.sem_inc(S("act_done"), -1)
                give(e, "bank6")
                e.wait_ge(S("nm_ready"), 1)
                e.sem_inc(S("nm_ready"), -1)
                for hs in range(8):
                    ins = e.activation(SC[0:n, hs, 0:width], SC[0:n, hs, 0:width], ACT.Exp, bias=ST[0:n, 16 + hs:17 + hs], scale=1.0,
                                       accum_out=ST[0:n, 24 + hs:25 + hs])
                e.activation(ST[0:n, 32:40], ST[0:n, 32:40], ACT.Exp).then_inc(S("exp_ready"), 1)
                for g in range(4):
                    b = (0, 1, 6, 7)[g]
                    e.wait_ge(S("pT_psum"), 1)
                    e.sem_inc(S("pT_psum"), -1)
                    for kt, nk in enumerate(kts):
                        src = bank(b).rearrange("p (h k q) -> p h k q", h=2, k=2)
                        ins = copy(PT[0:nk, 2 * g:2 * g + 2, kt, 0:n], src[0:nk, :, kt, 0:n])
                    ins.then_inc(S("act_done"), 1)
                    e.wait_ge(S("act_done"), 1)
                    e.sem_inc(S("act_done"), -1)
                    give(e, f"bank{b}")
                give(e, "pT_ready")
                e.wait_ge(S("ot_free"), 1)
                e.sem_inc(S("ot_free"), -1)
                e.wait_ge(S("o_psum"), 1)
                e.sem_inc(S("o_psum"), -1)
                copy(OT[:, :, 0:n], PS[:, 1024:1024 + 4 * n].rearrange("p (a t) -> p a t", a=4)).then_inc(S("act_done"), 1)
                e.wait_ge(S("act_done"), 1)
                e.sem_inc(S("act_done"), -1)
                give(e, "bank2", "ot_ready")

            def keys_out(n):
                e.wait_ge(S("ko_psum"), 1)
                e.sem_inc(S("ko_psum"), -1)
                copy(KO[0:n, :], PS[0:n, 0:P]).then_inc(S("act_done"), 1)
                e.wait_ge(S("act_done"), 1)
                e.sem_inc(S("act_done"), -1)
                give(e, "bank0", "ko_ready")

            with e.Fori(0, TILES // 2) as i:
                for s in range(2):
                    att((i * 2 + s) * P, P, s, 256, (P, P))
            keys_out(P)
            give(e, "vt_free", "kcr_free")
            for v in range(2):
                e.wait_ge(S("kc_psum"), 1)
                e.sem_inc(S("kc_psum"), -1)
                copy(KR[:, v, 1, :], PS[:, v * 512:v * 512 + P]).then_inc(S("act_done"), 1)
                e.wait_ge(S("act_done"), 1)
                e.sem_inc(S("act_done"), -1)
                give(e, f"bank{v}")
                if v == 0:
                    give(e, "kcr_free")
            give(e, "kc_ready")
            att(SEQ, DEC_SEQ, 0, DEC_SEQ + P, (DEC_SEQ, P))
            keys_out(DEC_SEQ)
            barrier(e, "act")

            def by_token(u):
                _, n, tiles, _ = unit(u)
                for x in range(tiles):
                    e.wait_ge(S("tm_psum"), 1)
                    e.sem_inc(S("tm_psum"), -1)
                    copy(ATM[0:n, x, :], PS[0:n, x * 512:x * 512 + P])
                    copy(bkv(u)[0:n, x, :, :], PS[0:n, x * 512 + P:(x + 1) * 512].rearrange("p (a t) -> p a t", a=3)).then_inc(S("act_done"), 1)
                    e.wait_ge(S("act_done"), 1)
                    e.sem_inc(S("act_done"), -1)
                    give(e, f"bank{x}")
                give(e, "tm_ready")
                e.wait_ge(S("mv_psum"), 1)
                e.sem_inc(S("mv_psum"), -1)
                copy(MVS[0:n, 0:tiles, :], PS[0:n, 1536:1536 + tiles * P].rearrange("p (x t) -> p x t", x=tiles)).then_inc(S("act_done"), 1)
                e.wait_ge(S("act_done"), 1)
                e.sem_inc(S("act_done"), -1)
                give(e, "bank3", "mv_ready")

            def levels_left(u):
                _, n, tiles, levels = unit(u)
                for s in range(levels):
                    e.wait_ge(S("t1_psum"), 1)
                    e.sem_inc(S("t1_psum"), -1)
                    copy(T1F[0:n, 0:2 * tiles * n], PS[0:n, 1024:1024 + 2 * tiles * n]).then_inc(S("act_done"), 1)
                    e.wait_ge(S("act_done"), 1)
                    e.sem_inc(S("act_done"), -1)
                    give(e, "bank2", "t1_ready", "elt_free")

            def solved(u):
                _, n, tiles, _ = unit(u)
                e.wait_ge(S("pts_psum"), 1)
                e.sem_inc(S("pts_psum"), -1)
                copy(PTS[:, 0:tiles, 0:n], PS[:, 1024:1024 + tiles * n].rearrange("p (x t) -> p x t", x=tiles)).then_inc(S("act_done"), 1)
                e.wait_ge(S("act_done"), 1)
                e.sem_inc(S("act_done"), -1)
                give(e, "bank2")
                e.wait_ge(S("q_psum"), 1)
                e.sem_inc(S("q_psum"), -1)
                copy(QS[0:n, 0:tiles, :], PS[0:n, 1536:1536 + tiles * P].rearrange("p (x t) -> p x t", x=tiles)).then_inc(S("act_done"), 1)
                e.wait_ge(S("act_done"), 1)
                e.sem_inc(S("act_done"), -1)
                give(e, "bank3", "pq_ready", "q_ready")

            def outputs(u):
                t0, n, tiles, _ = unit(u)
                yb = (4, 7)[u % 2]
                e.wait_ge(S("y_psum"), 1)
                e.sem_inc(S("y_psum"), -1)
                copy(YY[:, t0:t0 + tiles * n], PS[:, yb * 512:yb * 512 + tiles * n]).then_inc(S("act_done"), 1)
                e.wait_ge(S("act_done"), 1)
                e.sem_inc(S("act_done"), -1)
                give(e, f"bank{yb}")

            with e.Fori(0, PAIRS) as j:
                for b, s in enumerate((0, 1, 0)):
                    e.wait_ge(S("praw_free"), 1)
                    e.sem_inc(S("praw_free"), -1)
                    evac(s, raw())
                    give(e, "praw_ready")
                e.wait_ge(S("pc_ready"), 1)
                e.sem_inc(S("pc_ready"), -1)
                for c in range(CH):
                    e.wait_ge(S("z_psum"), 1)
                    e.sem_inc(S("z_psum"), -1)
                    e.activation(DD2[:, chunk(c)], bank(3 + c, 0, CW), ACT.Sigmoid, bias=PC[:, 3:4]).then_inc(S("act_done"), 1)
                    e.wait_ge(S("act_done"), 1)
                    e.sem_inc(S("act_done"), -1)
                    give(e, f"bank{3 + c}")
                for c in range(CH):
                    e.wait_ge(S("z_psum"), 1)
                    e.sem_inc(S("z_psum"), -1)
                    e.activation(BB[:, chunk(c)], bank(c, 0, CW), ACT.Sigmoid, bias=PC[:, 4:5]).then_inc(S("act_done"), 1)
                    e.wait_ge(S("act_done"), 1)
                    e.sem_inc(S("act_done"), -1)
                    give(e, f"bank{c}")
                for c in range(CH):
                    e.wait_ge(S("z_psum"), 1)
                    e.sem_inc(S("z_psum"), -1)
                    copy(GG[:, chunk(c)], bank(3 + c, 0, CW)).then_inc(S("act_done"), 1)
                    e.wait_ge(S("act_done"), 1)
                    e.sem_inc(S("act_done"), -1)
                    give(e, f"bank{3 + c}")
                split(1)
                give(e, "sig_ready")
                e.wait_ge(S("kkr_ready"), 1)
                e.sem_inc(S("kkr_ready"), -1)
                e.activation(TMP[:, 0, :], KK, ACT.Square).then_inc(S("kksq_ready"), 1)
                e.wait_ge(S("kkn_ready"), 1)
                e.sem_inc(S("kkn_ready"), -1)
                e.activation(TMP[:, 2, :], TMP[:, 2, :], ACT.Sqrt).then_inc(S("act_done"), 1)
                e.wait_ge(S("act_done"), 1)
                e.sem_inc(S("act_done"), -1)
                give(e, "kks_ready")
                e.wait_ge(S("dd_ready"), 1)
                e.sem_inc(S("dd_ready"), -1)
                e.activation(TMP[:, 0, :], DD, ACT.Exp, scale=-DECAY)
                e.activation(TMP[:, 1, :], DD2, ACT.Exp, scale=-DECAY)
                e.activation(TMP[:, 2, :], DD, ACT.Exp, scale=DECAY)
                e.activation(EC[:, 20:38], EC[:, 0:18], ACT.Exp, scale=-DECAY).then_inc(S("e_ready"), 1)
                for u in range(UNITS + 1):
                    by_token(u)
                    levels_left(u)
                    if u > 0:
                        outputs(u - 1)
                    solved(u)

                def state_out():
                    e.wait_ge(S("sio_psum"), 1)
                    e.sem_inc(S("sio_psum"), -1)
                    copy(SIO, PS[:, 0:P]).then_inc(S("act_done"), 1)
                    e.wait_ge(S("act_done"), 1)
                    e.sem_inc(S("act_done"), -1)
                    give(e, "bank0", "state_out")

                state_out()
                outputs(UNITS)
                state_out()
                e.wait_ge(S("state_saved"), 1)
                e.sem_inc(S("state_saved"), -1)
                give(e, "yy_ready")
                for c in range(CH):
                    e.wait_ge(S("yc_psum"), 1)
                    e.sem_inc(S("yc_psum"), -1)
                    copy(TMP[:, 1, chunk(c)], bank(c, 0, CW)).then_inc(S("act_done"), 1)
                    e.wait_ge(S("act_done"), 1)
                    e.sem_inc(S("act_done"), -1)
                    give(e, f"bank{c}")
                e.activation(TMP[:, 0, :], TMP[:, 1, :], ACT.Square).then_inc(S("act_done"), 1)
                e.wait_ge(S("act_done"), 1)
                e.sem_inc(S("act_done"), -1)
                give(e, "ysq_ready")
                for c in range(CH):
                    e.wait_ge(S("yv_psum"), 1)
                    e.sem_inc(S("yv_psum"), -1)
                    e.activation(TMP[:, 2, chunk(c)], bank(3 + c, 0, CW), ACT.Sqrt, bias=CST[:, C_EPS + 1:C_EPS + 2]).then_inc(S("act_done"), 1)
                    e.wait_ge(S("act_done"), 1)
                    e.sem_inc(S("act_done"), -1)
                    give(e, f"bank{3 + c}")
                give(e, "ystd_ready")
            e.wait_ge(S("shc_psum"), 1)
            e.sem_inc(S("shc_psum"), -1)
            for g in range(2):
                ins = copy(AUX[g * 64:g * 64 + 16, 256:384], PS[g * 64:g * 64 + 16, 0:P])
            ins.then_inc(S("act_done"), 1)
            e.wait_ge(S("act_done"), 1)
            e.sem_inc(S("act_done"), -1)
            give(e, "bank0", "shc_ready")
            barrier(e, "act")
            e.wait_ge(S("mix_act"), 1)
            e.sem_inc(S("mix_act"), -1)
            for b in range(DB):
                copy(HH[:, b, :], R2[:, b, :]).then_inc(S("hh_ready"), 1)
            e.wait_ge(S("r2_free"), 1)
            e.sem_inc(S("r2_free"), -1)

            def out8():
                with e.Fori(0, 4) as i:
                    for s in range(2):
                        evac(s, lambda c: [(R2[:, bass.ds(i * 2 + s, 1), chunk(c)].rearrange("p a t -> p (a t)"), 0, CW)])

            out8()
            give(e, "m_ready")
            squares(R2)
            barrier(e, "act")
            squares(R1)
            highs()
            with e.Fori(0, 2) as i:
                for s in range(2):
                    evac(s, lambda c: [(R2[:, bass.ds(i * 2 + s, 1), chunk(c)].rearrange("p a t -> p (a t)"), 0, CW)])

            def mem_keys():
                for kt in range(2):
                    e.wait_ge(S("ckt_psum"), 1)
                    e.sem_inc(S("ckt_psum"), -1)
                    copy(CKT[:, :, kt * P:(kt + 1) * P], bank(6 + kt).rearrange("p (h k) -> p h k", h=4)).then_inc(S("act_done"), 1)
                    e.wait_ge(S("act_done"), 1)
                    e.sem_inc(S("act_done"), -1)
                    give(e, f"bank{6 + kt}")
                give(e, "ckt_ready")

            def cross(i, n):
                copy(CQ[:, :, 0:n], R2[:, 0:4, bass.ds(i, n)]).then_inc(S("cq_ready"), 1)
                e.wait_ge(S("cnm_ready"), 1)
                e.sem_inc(S("cnm_ready"), -1)
                for h in range(4):
                    ins = e.activation(CP[0:n, h, :], PS[0:n, h * MEM:(h + 1) * MEM], ACT.Exp, bias=ST[0:n, 4 + h:5 + h], scale=float(P) ** -0.5,
                                       accum_out=ST[0:n, 8 + h:9 + h])
                ins.then_inc(S("act_done"), 1)
                e.wait_ge(S("act_done"), 1)
                e.sem_inc(S("act_done"), -1)
                give(e, "bank0", "bank1", "cexp_ready")
                for g in range(2):
                    e.wait_ge(S("cpt_psum"), 1)
                    e.sem_inc(S("cpt_psum"), -1)
                    copy(CPT[:, 2 * g:2 * g + 2, :, 0:n], bank(2 + g).rearrange("p (h k q) -> p h k q", h=2, k=2)[:, :, :, 0:n]).then_inc(S("act_done"), 1)
                    e.wait_ge(S("act_done"), 1)
                    e.sem_inc(S("act_done"), -1)
                    give(e, f"bank{2 + g}")
                give(e, "cpt_ready")
                e.wait_ge(S("co_psum"), 1)
                e.sem_inc(S("co_psum"), -1)
                copy(HH[:, 0:4, bass.ds(i, n)], PS[:, 2048:2048 + 4 * n].rearrange("p (h q) -> p h q", h=4)).then_inc(S("coh_ready"), 1)

            mem_keys()
            with e.Fori(0, TILES) as t:
                cross(t * P, P)
            mem_keys()
            cross(SEQ, DEC_SEQ)
            with e.Fori(0, 2) as i:
                for s in range(2):
                    for o in range(2):
                        evac(s, lambda c: [(R2[:, bass.ds((i * 2 + s) * 2 + o, 1), chunk(c)].rearrange("p a t -> p (a t)"), 0, CW)],
                             b0=3 * o, then=(o == 1))
            squares(R2)
            barrier(e, "act")
            squares(R1)
            highs()
            with e.Fori(0, FB // 2) as i:
                for f in range(2):
                    for c in range(CH):
                        e.wait_ge(S("gate_psum"), 1)
                        e.sem_inc(S("gate_psum"), -1)
                        e.wait_ge(S("silu_free"), 1)
                        e.sem_inc(S("silu_free"), -1)
                        e.activation(TMP[:, 0, chunk(c)], bank(c, 0, CW), ACT.Silu).then_inc(S("act_done"), 1)
                        e.wait_ge(S("act_done"), 1)
                        e.sem_inc(S("act_done"), -1)
                        give(e, f"bank{c}", "silu_ready")
                    split(0)
                    for c in range(CH):
                        e.wait_ge(S("gu_ready"), 1)
                        e.sem_inc(S("gu_ready"), -1)
                        copy(GH[:, f, chunk(c)], TMP[:, 1, chunk(c)]).then_inc(S("gh_ready"), 1)
                    split(1)
                e.wait_ge(S("down_end"), 1)
                e.sem_inc(S("down_end"), -1)
                split(0)
                split(1)
            squares(R2)
            barrier(e, "act")

        def tokens_out(i, n):
            e.wait_ge(S("xo_free"), 1)
            e.sem_inc(S("xo_free"), -1)
            copy(R2[:, 0, 0:1024].rearrange("p (b t) -> p b t", b=8)[:, :, 0:n], R1[:, :, bass.ds(i, n)]).then_inc(S("xo_ready"), 1)
            e.wait_ge(S("xout_free"), 1)
            e.sem_inc(S("xout_free"), -1)
            for g in range(2):
                e.wait_ge(S("xo_psum"), 1)
                e.sem_inc(S("xo_psum"), -1)
                copy(R2[0:n, 4, g * 512:(g + 1) * 512], PS[0:n, g * 512:(g + 1) * 512]).then_inc(S("act_done"), 1)
                e.wait_ge(S("act_done"), 1)
                e.sem_inc(S("act_done"), -1)
                give(e, f"bank{g}")
            give(e, "xout_ready", "xo_free")

        give(e, "xo_free", "xout_free")
        with e.Fori(0, TILES) as j:
            tokens_out(j * P, P)
        tokens_out(SEQ, DEC_SEQ)

    @block.vector
    def _(e):
        def lo(slot):
            e.wait_ge(S(f"wh_ready{slot}"), 1)
            e.sem_inc(S(f"wh_ready{slot}"), -1)
            e.tensor_tensor(WL[:, slot, :], WRAW[:, slot, :], WH[:, slot, :].bitcast(F32), ALU.subtract).then_inc(S("dve_done"), 1)
            e.wait_ge(S("dve_done"), 1)
            e.sem_inc(S("dve_done"), -1)
            give(e, f"w_ready{slot}", f"w_free{slot}")

        def los(n):
            with e.Fori(0, n) as i:
                lo(0)
                lo(1)

        def sum_squares(n=T):
            e.wait_ge(S("sq_ready"), 2)
            e.sem_inc(S("sq_ready"), -2)
            e.tensor_tensor(TMP[:, 2, 0:n], TMP[:, 0, 0:n], TMP[:, 1, 0:n], ALU.add).then_inc(S("dve_done"), 1)
            e.wait_ge(S("dve_done"), 1)
            e.sem_inc(S("dve_done"), -1)
            give(e, "sq_free", "sq_free")
            for b in range(2, DB):
                e.wait_ge(S("sq_ready"), 1)
                e.sem_inc(S("sq_ready"), -1)
                e.tensor_tensor(TMP[:, 2, 0:n], TMP[:, 2, 0:n], TMP[:, b % 2, 0:n], ALU.add).then_inc(S("dve_done"), 1)
                e.wait_ge(S("dve_done"), 1)
                e.sem_inc(S("dve_done"), -1)
                give(e, *(["sq_free"] if b < DB - 2 else []))
            give(e, "sq_sum")
            e.wait_ge(S("rms_ready"), CH if n == T else 1)
            e.sem_inc(S("rms_ready"), -(CH if n == T else 1))
            e.reciprocal(TMP[:, 0, 0:n], TMP[:, 0, 0:n]).then_inc(S("dve_done"), 1)
            e.wait_ge(S("dve_done"), 1)
            e.sem_inc(S("dve_done"), -1)

        def scaled(dst, src, gain, n):
            return e.scalar_tensor_tensor(out=dst, in0=src, scalar=PRM[:, gain:gain + 1], in1=TMP[:, 0, 0:n], op0=ALU.mult, op1=ALU.mult)

        def normed(src, which, n=T):
            sum_squares(n)
            t = lambda b: TMP[:, 1 + b % 2, 0:n]
            scaled(t(0), src[:, 0, 0:n], G_AT + which * DB, n).then_inc(S("dve_done"), 1)
            e.wait_ge(S("dve_done"), 1)
            e.sem_inc(S("dve_done"), -1)
            give(e, "ht_ready")
            for b in range(DB):
                if b < DB - 1:
                    scaled(t(b + 1), src[:, b + 1, 0:n], G_AT + which * DB + b + 1, n).then_inc(S("dve_done"), 1)
                    e.wait_ge(S("dve_done"), 1)
                    e.sem_inc(S("dve_done"), -1)
                    give(e, "ht_ready")
                e.wait_ge(S("hh_ready"), 1)
                e.sem_inc(S("hh_ready"), -1)
                e.tensor_tensor(HL[:, b, 0:n], t(b), HH[:, b, 0:n].bitcast(F32), ALU.subtract).then_inc(S("dve_done"), 1)
                e.wait_ge(S("dve_done"), 1)
                e.sem_inc(S("dve_done"), -1)
            give(e, "h_ready", "sq_free", "sq_free")

        def add_normed(which):
            sum_squares()
            for b in range(DB):
                scaled(TMP[:, 1 + b % 2, :], R2[:, b, :], G_AT + which * DB + b, T).then_inc(S("dve_done"), 1)
                e.wait_ge(S("dve_done"), 1)
                e.sem_inc(S("dve_done"), -1)
                e.tensor_tensor(R1[:, b, :], R1[:, b, :], TMP[:, 1 + b % 2, :], ALU.add).then_inc(S("dve_done"), 1)
                e.wait_ge(S("dve_done"), 1)
                e.sem_inc(S("dve_done"), -1)
            give(e, "sq_free", "sq_free")

        e.wait_ge(S("cst_dve"), 1)
        e.sem_inc(S("cst_dve"), -1)
        give(e, "xin_free", "w_free0", "w_free1", "praw_free", "cv_free")
        e.memset(SHC, 0.0).then_inc(S("dve_done"), 1)
        e.wait_ge(S("dve_done"), 1)
        e.sem_inc(S("dve_done"), -1)

        def tokens_in(n, dst):
            e.wait_ge(S("xT_dve_psum"), 1)
            e.sem_inc(S("xT_dve_psum"), -1)
            e.tensor_copy(dst, PS[:, 512:1024].rearrange("p (b t) -> p b t", b=4)[:, :, 0:n]).then_inc(S("dve_done"), 1)
            e.wait_ge(S("dve_done"), 1)
            e.sem_inc(S("dve_done"), -1)
            give(e, "bank1")
            e.wait_ge(S("xin_act"), 1)
            e.sem_inc(S("xin_act"), -1)
            give(e, "xin_free")

        with e.Fori(0, MEM // P) as j:
            tokens_in(P, R1[:, 4:8, bass.ds(j * P, P)])
        give(e, "memT_ready")
        e.wait_ge(S("memT_saved_dve"), 1)
        e.sem_inc(S("memT_saved_dve"), -1)
        with e.Fori(0, TILES) as j:
            tokens_in(P, R1[:, 4:8, bass.ds(j * P, P)])
        tokens_in(DEC_SEQ, R1[:, 4:8, SEQ:T])
        barrier(e, "dve")
        lo(0)
        lo(1)
        with e.Fori(0, DEPTH) as l:
            e.memset(TMP[:, 0, 0:P], 0.0).then_inc(S("dve_done"), 1)
            e.wait_ge(S("dve_done"), 1)
            e.sem_inc(S("dve_done"), -1)
            give(e, "prow_clear")
            e.wait_ge(S("prm_rows"), 1)
            e.sem_inc(S("prm_rows"), -1)
            give(e, "prm_rows_pe")
            e.wait_ge(S("prm_ready"), 1)
            e.sem_inc(S("prm_ready"), -1)
            e.wait_ge(S("memT_dve"), 1)
            e.sem_inc(S("memT_dve"), -1)
            normed(R2, N_MEM, MEM)
            los(4)
            normed(R1, MIX_PRE)
            barrier(e, "dve")
            los(3)
            lo(0)

            def shifted(dst, mu, sh, m=P):
                e.memset(PRAW[0:m, 0:1], 0.0).then_inc(S("dve_done"), 1)
                e.wait_ge(S("dve_done"), 1)
                e.sem_inc(S("dve_done"), -1)
                e.tensor_copy(PRAW[0:m, SEQ + 1:SEQ + 2], sh).then_inc(S("dve_done"), 1)
                e.wait_ge(S("dve_done"), 1)
                e.sem_inc(S("dve_done"), -1)
                e.wait_ge(S("praw_ready"), 1)
                e.sem_inc(S("praw_ready"), -1)
                e.tensor_tensor(dst[:, 0:SEQ], PRAW[0:m, 0:SEQ], PRAW[0:m, 1:SEQ + 1], ALU.subtract).then_inc(S("dve_done"), 1)
                e.wait_ge(S("dve_done"), 1)
                e.sem_inc(S("dve_done"), -1)
                e.tensor_tensor(dst[:, SEQ:T], PRAW[0:m, SEQ + 1:T + 1], PRAW[0:m, SEQ + 2:T + 2], ALU.subtract).then_inc(S("dve_done"), 1)
                e.wait_ge(S("dve_done"), 1)
                e.sem_inc(S("dve_done"), -1)
                e.scalar_tensor_tensor(out=dst[:, 0:SEQ], in0=dst[:, 0:SEQ], scalar=mu, in1=PRAW[0:m, 1:SEQ + 1], op0=ALU.mult, op1=ALU.add).then_inc(S("dve_done"), 1)
                e.wait_ge(S("dve_done"), 1)
                e.sem_inc(S("dve_done"), -1)
                e.scalar_tensor_tensor(out=dst[:, SEQ:T], in0=dst[:, SEQ:T], scalar=mu, in1=PRAW[0:m, SEQ + 2:T + 2], op0=ALU.mult, op1=ALU.add).then_inc(S("dve_done"), 1)
                e.wait_ge(S("dve_done"), 1)
                e.sem_inc(S("dve_done"), -1)

            def kept(at, m=P):
                for g, col in ((0, SEQ), (16, T + 1)):
                    e.tensor_copy(at(g), PRAW[0:m, col:col + 1]).then_inc(S("dve_done"), 1)
                    e.wait_ge(S("dve_done"), 1)
                    e.sem_inc(S("dve_done"), -1)
                give(e, "praw_free")

            for b, (dst, m) in enumerate(((TWA, P), (SG1, P), (SG2[0:32, :], 32))):
                shifted(dst, PRM[0:m, MU_AT + 12 + b:MU_AT + 13 + b], PRM[0:m, SH_AT + 12 + b:SH_AT + 13 + b], m)
                kept(lambda g: SHC[0:m, 12 + b + g:13 + b + g], m)
                lo(1 - b % 2)
            give(e, "lora_ready", "cos_free")
            e.wait_ge(S("cos_ready"), 1)
            e.sem_inc(S("cos_ready"), -1)
            give(e, "cos_pe")
            e.memset(KR[:, :, 1, :], 0.0).then_inc(S("dve_done"), 1)
            e.wait_ge(S("dve_done"), 1)
            e.sem_inc(S("dve_done"), -1)
            e.memset(VT[:, 1, :], 0.0).then_inc(S("dve_done"), 1)
            e.wait_ge(S("dve_done"), 1)
            e.sem_inc(S("dve_done"), -1)

            def att(i, n, slot, width, mask):
                tok = bass.ds(i, n)
                cs, sn = (x[:, tok].unsqueeze(1).broadcast_to([P, 6, n]) for x in (COS, SIN))
                e.tensor_tensor(RT[:, :, 0:n], R1[:, 0:6, tok], cs, ALU.mult).then_inc(S("dve_done"), 1)
                e.wait_ge(S("dve_done"), 1)
                e.sem_inc(S("dve_done"), -1)
                e.wait_ge(S("swap_psum"), 1)
                e.sem_inc(S("swap_psum"), -1)
                e.tensor_tensor(RU[:, 0:4, 0:n], PS[:, 0:4 * n].rearrange("p (a t) -> p a t", a=4), sn[:, 0:4, :], ALU.mult).then_inc(S("dve_done"), 1)
                e.wait_ge(S("dve_done"), 1)
                e.sem_inc(S("dve_done"), -1)
                e.tensor_tensor(RU[:, 4:6, 0:n], PS[:, 512:512 + 2 * n].rearrange("p (a t) -> p a t", a=2), sn[:, 0:2, :], ALU.mult).then_inc(S("dve_done"), 1)
                e.wait_ge(S("dve_done"), 1)
                e.sem_inc(S("dve_done"), -1)
                give(e, "bank0", "bank1")
                e.tensor_tensor(QR[:, :, 0:n], RT[:, 0:4, 0:n], RU[:, 0:4, 0:n], ALU.add).then_inc(S("dve_done"), 1)
                e.wait_ge(S("dve_done"), 1)
                e.sem_inc(S("dve_done"), -1)
                e.tensor_tensor(KR[:, :, slot, 0:n], RT[:, 4:6, 0:n], RU[:, 4:6, 0:n], ALU.add).then_inc(S("dve_done"), 1)
                e.wait_ge(S("dve_done"), 1)
                e.sem_inc(S("dve_done"), -1)
                if mask is None:
                    e.wait_ge(S("kc_ready"), 1)
                    e.sem_inc(S("kc_ready"), -1)
                give(e, "qk_ready")
                s = SC[0:n, :, 0:width]
                for g in range(4):
                    e.wait_ge(S("score_psum"), 1)
                    e.sem_inc(S("score_psum"), -1)
                    src = PS[0:n, 1024 + g * 512:1536 + g * 512].rearrange("p (h k) -> p h k", h=2)[:, :, 0:width]
                    dst = SC[0:n, 2 * g:2 * g + 2, 0:width]
                    if mask is None:
                        e.tensor_scalar(dst, src, HEAD ** -0.5, None, ALU.mult).then_inc(S("dve_done"), 1)
                        e.wait_ge(S("dve_done"), 1)
                        e.sem_inc(S("dve_done"), -1)
                        give(e, f"bank{2 + g}")
                    else:
                        e.scalar_tensor_tensor(out=dst, in0=src, scalar=HEAD ** -0.5, in1=mask.unsqueeze(1).broadcast_to([n, 2, width]),
                                                    op0=ALU.mult, op1=ALU.add).then_inc(S("dve_done"), 1)
                        e.wait_ge(S("dve_done"), 1)
                        e.sem_inc(S("dve_done"), -1)
                        give(e, f"bank{2 + g}")
                e.tensor_reduce(ST[0:n, 0:8], s, AX.X, ALU.max).then_inc(S("dve_done"), 1)
                e.wait_ge(S("dve_done"), 1)
                e.sem_inc(S("dve_done"), -1)
                e.tensor_tensor(ST[0:n, 8:16], ST[0:n, 0:8], ST[0:n, 40:48], ALU.max).then_inc(S("dve_done"), 1)
                e.wait_ge(S("dve_done"), 1)
                e.sem_inc(S("dve_done"), -1)
                e.tensor_scalar(ST[0:n, 16:24], ST[0:n, 8:16], -1.0, None, ALU.mult).then_inc(S("dve_done"), 1)
                e.wait_ge(S("dve_done"), 1)
                e.sem_inc(S("dve_done"), -1)
                e.tensor_tensor(ST[0:n, 32:40], ST[0:n, 40:48], ST[0:n, 8:16], ALU.subtract).then_inc(S("dve_done"), 1)
                e.wait_ge(S("dve_done"), 1)
                e.sem_inc(S("dve_done"), -1)
                give(e, "nm_ready")
                e.wait_ge(S("exp_ready"), 1)
                e.sem_inc(S("exp_ready"), -1)
                e.tensor_tensor(ST[0:n, 0:8], ST[0:n, 24:32], ST[0:n, 32:40], ALU.add).then_inc(S("dve_done"), 1)
                e.wait_ge(S("dve_done"), 1)
                e.sem_inc(S("dve_done"), -1)
                e.reciprocal(ST[0:n, 0:8], ST[0:n, 0:8]).then_inc(S("dve_done"), 1)
                e.wait_ge(S("dve_done"), 1)
                e.sem_inc(S("dve_done"), -1)
                e.tensor_tensor(s, s, ST[0:n, 0:8].unsqueeze(2).broadcast_to([n, 8, width]), ALU.mult).then_inc(S("dve_done"), 1)
                e.wait_ge(S("dve_done"), 1)
                e.sem_inc(S("dve_done"), -1)
                give(e, "prob_ready")

            e.tensor_copy(ST[:, 40:44], SINK[:, 0:8:2]).then_inc(S("dve_done"), 1)
            e.wait_ge(S("dve_done"), 1)
            e.sem_inc(S("dve_done"), -1)
            e.tensor_copy(ST[:, 44:48], SINK[:, 1:8:2]).then_inc(S("dve_done"), 1)
            e.wait_ge(S("dve_done"), 1)
            e.sem_inc(S("dve_done"), -1)
            with e.Fori(0, TILES // 2) as i:
                att((i * 2) * P, P, 0, 256, CST[:, bass.ds(C_AE + i * 256, 256)])
                att((i * 2 + 1) * P, P, 1, 256, CST[:, C_AO:C_AO + 256])
            att(SEQ, DEC_SEQ, 0, DEC_SEQ + P, None)
            barrier(e, "dve")

            def scores(u, x):
                _, n, tiles, _ = unit(u)
                e.wait_ge(S("sm_psum"), 2)
                e.sem_inc(S("sm_psum"), -2)
                src = PS[0:n, 1024:2048].rearrange("p (h c) -> p h c", h=2)
                dst = LTM[0:n, :].rearrange("p (a c) -> p a c", a=3)[:, :, 0:2 * tiles * n].rearrange("p a (g t) -> p g a t", t=n)
                m3 = CST[0:n, C_M3:C_M3 + 3 * P].rearrange("p (a t) -> p a t", a=3)[:, :, 0:n]
                e.tensor_tensor(dst[:, 2 * x:2 * x + 2, :, :], src[:, :, 0:3 * n].rearrange("p h (a t) -> p h a t", a=3),
                                m3.unsqueeze(1).broadcast_to([n, 2, 3, n]), ALU.mult)
                e.tensor_tensor(heads(tflat, 1536 + (u % 2) * 512, n, tiles)[:, 2 * x:2 * x + 2, :], src[:, :, 3 * n:4 * n],
                                     m3[:, 2, :].unsqueeze(1).broadcast_to([n, 2, n]), ALU.mult).then_inc(S("dve_done"), 1)
                e.wait_ge(S("dve_done"), 1)
                e.sem_inc(S("dve_done"), -1)
                give(e, "bank2", "bank3")
                if x == tiles - 1:
                    give(e, "lt_ready", "sm_ready")

            def low(u):
                _, n, tiles, _ = unit(u)
                e.wait_ge(S("l_psum"), 2)
                e.sem_inc(S("l_psum"), -2)
                mask = lambda at: CST[0:n, at:at + n].unsqueeze(1).broadcast_to([n, 2 * tiles, n])
                src = PS[0:n, 0:1024].rearrange("p (h c) -> p h c", h=2)[:, :, 0:tiles * n].rearrange("p h (x t) -> p x h t", x=tiles)
                dst = heads(XXF, 0, n, tiles)
                e.tensor_tensor(dst.rearrange("p (x h) t -> p x h t", h=2), src,
                                     mask(C_NL).rearrange("p (x h) t -> p x h t", h=2), ALU.mult).then_inc(S("dve_done"), 1)
                e.wait_ge(S("dve_done"), 1)
                e.sem_inc(S("dve_done"), -1)
                give(e, "bank0", "bank1")
                e.tensor_tensor(dst, dst, mask(C_ID), ALU.add).then_inc(S("dve_done"), 1)
                e.wait_ge(S("dve_done"), 1)
                e.sem_inc(S("dve_done"), -1)
                give(e, "x_ready")

            def level_right(u, s):
                _, n, tiles, levels = unit(u)
                w = 2 * tiles * n
                for k in range(0 if s < levels - 1 else 1, 2):
                    xx = XXF[0:n, k * 512:k * 512 + w]
                    e.wait_ge(S("dx_psum"), 1)
                    e.sem_inc(S("dx_psum"), -1)
                    e.tensor_tensor(xx, xx, PS[0:n, k * 512:k * 512 + w], ALU.subtract).then_inc(S("dve_done"), 1)
                    e.wait_ge(S("dve_done"), 1)
                    e.sem_inc(S("dve_done"), -1)
                    give(e, f"bank{k}", "x_ready" if k == 0 else "xt_ready")

            def chunk_u(u, c):
                _, n, _, _ = unit(u)
                r, x = slice((c % 2) * CHUNK, (c % 2) * CHUNK + min(n, CHUNK)), c // 2
                if c == 0:
                    e.wait_ge(S("q_ready"), 1)
                    e.sem_inc(S("q_ready"), -1)
                e.wait_ge(S("u_psum"), 1)
                e.sem_inc(S("u_psum"), -1)
                e.scalar_tensor_tensor(out=US[r, x, :], in0=PS[r, 3072:3072 + P], scalar=-1.0, in1=QS[r, x, :], op0=ALU.mult, op1=ALU.subtract).then_inc(S("dve_done"), 1)
                e.wait_ge(S("dve_done"), 1)
                e.sem_inc(S("dve_done"), -1)
                give(e, "bank6", "u_ready")
                ec = 20 + 4 * u + c
                e.tensor_scalar(STMP, SBD, EC[:, ec:ec + 1], None, ALU.mult).then_inc(S("dve_done"), 1)
                e.wait_ge(S("dve_done"), 1)
                e.sem_inc(S("dve_done"), -1)

            def chunk_state(u, c):
                ec = 20 + 4 * u + c
                e.wait_ge(S("ds_psum"), 1)
                e.sem_inc(S("ds_psum"), -1)
                for h in range(2):
                    p, q = slice(h * HEAD, (h + 1) * HEAD), 2560 + h * HEAD
                    ins = e.scalar_tensor_tensor(out=SBD[p, h * HEAD:(h + 1) * HEAD], in0=PS[p, q:q + HEAD], scalar=EC[p, ec:ec + 1],
                                                 in1=STMP[p, h * HEAD:(h + 1) * HEAD], op0=ALU.mult, op1=ALU.add)
                ins.then_inc(S("dve_done"), 1)
                e.wait_ge(S("dve_done"), 1)
                e.sem_inc(S("dve_done"), -1)
                give(e, "bank5", "state_ready")

            give(e, "y_saved")
            with e.Fori(0, PAIRS) as j:
                e.wait_ge(S("y_saved"), 1)
                e.sem_inc(S("y_saved"), -1)
                e.tensor_copy(PC[:, 0:3], PRM[:, bass.ds(MU_AT + j, 9)][:, 0:9:4]).then_inc(S("dve_done"), 1)
                e.wait_ge(S("dve_done"), 1)
                e.sem_inc(S("dve_done"), -1)
                e.tensor_copy(PC[:, 3:9], PRM[:, bass.ds(RV_AT + j, 21)][:, 0:21:4]).then_inc(S("dve_done"), 1)
                e.wait_ge(S("dve_done"), 1)
                e.sem_inc(S("dve_done"), -1)
                e.tensor_copy(PC[:, 9:12], PRM[:, bass.ds(SH_AT + j, 9)][:, 0:9:4]).then_inc(S("dve_done"), 1)
                e.wait_ge(S("dve_done"), 1)
                e.sem_inc(S("dve_done"), -1)
                e.tensor_copy(PC[:, 12:13], PRM[:, bass.ds(RK_AT + j, 1)]).then_inc(S("dve_done"), 1)
                e.wait_ge(S("dve_done"), 1)
                e.sem_inc(S("dve_done"), -1)
                e.tensor_scalar(PC[:, 13:14], PC[:, 6:7], -1.0, 1.0, ALU.mult, ALU.add).then_inc(S("dve_done"), 1)
                e.wait_ge(S("dve_done"), 1)
                e.sem_inc(S("dve_done"), -1)
                give(e, "pc_ready")
                for b, dst in enumerate((RR, KF, VV)):
                    shifted(dst, PC[:, b:b + 1], PC[:, 9 + b:10 + b])
                    kept(lambda g: SHC[:, bass.ds(j + (b * 4 + g), 1)])
                    if b == 1:
                        e.wait_ge(S("wh_ready1"), 1)
                        e.sem_inc(S("wh_ready1"), -1)
                        e.tensor_copy(LW, WRAW[:, 1, 0:3 * P]).then_inc(S("dve_done"), 1)
                        e.wait_ge(S("dve_done"), 1)
                        e.sem_inc(S("dve_done"), -1)
                        give(e, "lw_ready")
                        give(e, "wh_ready1")
                    lo(b % 2)
                e.memset(SEG, 1.0).then_inc(S("dve_done"), 1)
                e.wait_ge(S("dve_done"), 1)
                e.sem_inc(S("dve_done"), -1)
                e.memset(SEG[:, 0:T:CHUNK], 0.0).then_inc(S("dve_done"), 1)
                e.wait_ge(S("dve_done"), 1)
                e.sem_inc(S("dve_done"), -1)
                e.wait_ge(S("sig_ready"), 1)
                e.sem_inc(S("sig_ready"), -1)
                lo(1)
                e.tensor_tensor_scan(DD, SEG, DD2, 0.0, ALU.mult, ALU.add).then_inc(S("dve_done"), 1)
                e.wait_ge(S("dve_done"), 1)
                e.sem_inc(S("dve_done"), -1)
                d = DD[:, 0:SEQ].rearrange("p (c t) -> p c t", t=CHUNK)
                e.tensor_copy(ST[:, 0:16], d[:, :, 31]).then_inc(S("dve_done"), 1)
                e.wait_ge(S("dve_done"), 1)
                e.sem_inc(S("dve_done"), -1)
                e.tensor_copy(ST[:, 16:17], DD[:, SEQ + 15:SEQ + 16]).then_inc(S("dve_done"), 1)
                e.wait_ge(S("dve_done"), 1)
                e.sem_inc(S("dve_done"), -1)
                e.tensor_tensor(EC[:, 0:16], d[:, :, 63], ST[:, 0:16], ALU.subtract).then_inc(S("dve_done"), 1)
                e.wait_ge(S("dve_done"), 1)
                e.sem_inc(S("dve_done"), -1)
                e.tensor_tensor(EC[:, 0:15], EC[:, 0:15], ST[:, 1:16], ALU.add).then_inc(S("dve_done"), 1)
                e.wait_ge(S("dve_done"), 1)
                e.sem_inc(S("dve_done"), -1)
                e.tensor_tensor(EC[:, 16:17], DD[:, T - 1:T], ST[:, 16:17], ALU.subtract).then_inc(S("dve_done"), 1)
                e.wait_ge(S("dve_done"), 1)
                e.sem_inc(S("dve_done"), -1)
                e.tensor_copy(EC[:, 17:18], ST[:, 16:17]).then_inc(S("dve_done"), 1)
                e.wait_ge(S("dve_done"), 1)
                e.sem_inc(S("dve_done"), -1)
                e.tensor_tensor(d, d, ST[:, 0:16].unsqueeze(2).broadcast_to([P, 16, CHUNK]), ALU.subtract).then_inc(S("dve_done"), 1)
                e.wait_ge(S("dve_done"), 1)
                e.sem_inc(S("dve_done"), -1)
                e.tensor_scalar(DD[:, SEQ:T], DD[:, SEQ:T], ST[:, 16:17], None, ALU.subtract).then_inc(S("dve_done"), 1)
                e.wait_ge(S("dve_done"), 1)
                e.sem_inc(S("dve_done"), -1)
                e.tensor_tensor(DD2, DD, DD2, ALU.subtract).then_inc(S("dve_done"), 1)
                e.wait_ge(S("dve_done"), 1)
                e.sem_inc(S("dve_done"), -1)
                e.tensor_scalar(KK, KF, PC[:, 5:6], None, ALU.mult).then_inc(S("dve_done"), 1)
                e.wait_ge(S("dve_done"), 1)
                e.sem_inc(S("dve_done"), -1)
                give(e, "kkr_ready")
                e.tensor_scalar(TMP[:, 1, :], BB, PC[:, 6:7], PC[:, 13:14], ALU.mult, ALU.add).then_inc(S("dve_done"), 1)
                e.wait_ge(S("dve_done"), 1)
                e.sem_inc(S("dve_done"), -1)
                e.tensor_tensor(KF, KF, TMP[:, 1, :], ALU.mult).then_inc(S("dve_done"), 1)
                e.wait_ge(S("dve_done"), 1)
                e.sem_inc(S("dve_done"), -1)
                e.scalar_tensor_tensor(out=TMP[:, 1, :], in0=RR, scalar=PC[:, 12:13], in1=KF, op0=ALU.mult, op1=ALU.mult).then_inc(S("dve_done"), 1)
                e.wait_ge(S("dve_done"), 1)
                e.sem_inc(S("dve_done"), -1)
                give(e, "rk_ready")
                for c in range(CH):
                    e.wait_ge(S("kk_psum"), 1)
                    e.sem_inc(S("kk_psum"), -1)
                    e.tensor_scalar(TMP[:, 2, chunk(c)], bank(c, 0, CW), 1e-24, None, ALU.max).then_inc(S("dve_done"), 1)
                    e.wait_ge(S("dve_done"), 1)
                    e.sem_inc(S("dve_done"), -1)
                    give(e, f"bank{c}")
                give(e, "kkn_ready")
                for c in range(CH):
                    e.wait_ge(S("rk_psum"), 1)
                    e.sem_inc(S("rk_psum"), -1)
                    e.tensor_tensor(BON[:, chunk(c)], VV[:, chunk(c)], bank(3 + c, 0, CW), ALU.mult).then_inc(S("dve_done"), 1)
                    e.wait_ge(S("dve_done"), 1)
                    e.sem_inc(S("dve_done"), -1)
                    give(e, f"bank{3 + c}")
                e.wait_ge(S("kks_ready"), 1)
                e.sem_inc(S("kks_ready"), -1)
                e.reciprocal(TMP[:, 2, :], TMP[:, 2, :]).then_inc(S("dve_done"), 1)
                e.wait_ge(S("dve_done"), 1)
                e.sem_inc(S("dve_done"), -1)
                e.tensor_tensor(KK, KK, TMP[:, 2, :], ALU.mult).then_inc(S("dve_done"), 1)
                e.wait_ge(S("dve_done"), 1)
                e.sem_inc(S("dve_done"), -1)
                e.tensor_tensor(BB, BB, KK, ALU.mult).then_inc(S("dve_done"), 1)
                e.wait_ge(S("dve_done"), 1)
                e.sem_inc(S("dve_done"), -1)
                give(e, "dd_ready")
                e.wait_ge(S("e_ready"), 1)
                e.sem_inc(S("e_ready"), -1)
                e.tensor_tensor(RR, RR, TMP[:, 0, :], ALU.mult).then_inc(S("dve_done"), 1)
                e.wait_ge(S("dve_done"), 1)
                e.sem_inc(S("dve_done"), -1)
                e.tensor_tensor(KK, KK, TMP[:, 1, :], ALU.mult).then_inc(S("dve_done"), 1)
                e.wait_ge(S("dve_done"), 1)
                e.sem_inc(S("dve_done"), -1)
                e.tensor_tensor(BB, BB, TMP[:, 2, :], ALU.mult).then_inc(S("dve_done"), 1)
                e.wait_ge(S("dve_done"), 1)
                e.sem_inc(S("dve_done"), -1)
                e.tensor_tensor(KF, KF, TMP[:, 2, :], ALU.mult).then_inc(S("dve_done"), 1)
                e.wait_ge(S("dve_done"), 1)
                e.sem_inc(S("dve_done"), -1)
                e.memset(SBD, 0.0).then_inc(S("dve_done"), 1)
                e.wait_ge(S("dve_done"), 1)
                e.sem_inc(S("dve_done"), -1)
                give(e, "state_ready", "til_ready")
                for u in range(UNITS + 1):
                    _, _, tiles, levels = unit(u)
                    if u > 0:
                        chunk_u(u - 1, 0)
                    scores(u, 0)
                    if u > 0:
                        chunk_state(u - 1, 0)
                    low(u)
                    if tiles == 2:
                        scores(u, 1)
                    for s in range(levels):
                        if u > 0 and s < 3:
                            chunk_u(u - 1, s + 1)
                        level_right(u, s)
                        if u > 0 and s < 3:
                            chunk_state(u - 1, s + 1)
                e.wait_ge(S("sin_psum"), 1)
                e.sem_inc(S("sin_psum"), -1)
                e.tensor_scalar(SBD, PS[:, 512:512 + P], EC[:, 37:38], None, ALU.mult).then_inc(S("dve_done"), 1)
                e.wait_ge(S("dve_done"), 1)
                e.sem_inc(S("dve_done"), -1)
                give(e, "bank1", "state_ready")
                chunk_u(UNITS, 0)
                chunk_state(UNITS, 0)
                e.wait_ge(S("ystd_ready"), 1)
                e.sem_inc(S("ystd_ready"), -1)
                e.reciprocal(TMP[:, 2, :], TMP[:, 2, :]).then_inc(S("dve_done"), 1)
                e.wait_ge(S("dve_done"), 1)
                e.sem_inc(S("dve_done"), -1)
                e.tensor_tensor(YY, TMP[:, 1, :], TMP[:, 2, :], ALU.mult).then_inc(S("dve_done"), 1)
                e.wait_ge(S("dve_done"), 1)
                e.sem_inc(S("dve_done"), -1)
                e.tensor_scalar(YY, YY, PC[:, 7:8], PC[:, 8:9], ALU.mult, ALU.add).then_inc(S("dve_done"), 1)
                e.wait_ge(S("dve_done"), 1)
                e.sem_inc(S("dve_done"), -1)
                e.tensor_tensor(YY, YY, BON, ALU.add).then_inc(S("dve_done"), 1)
                e.wait_ge(S("dve_done"), 1)
                e.sem_inc(S("dve_done"), -1)
                e.tensor_tensor(YY, YY, GG, ALU.mult).then_inc(S("dve_done"), 1)
                e.wait_ge(S("dve_done"), 1)
                e.sem_inc(S("dve_done"), -1)
                give(e, "y_ready")
            e.wait_ge(S("y_saved"), 1)
            e.sem_inc(S("y_saved"), -1)
            give(e, "shc_full")
            barrier(e, "dve")
            e.wait_ge(S("mix_dve"), 1)
            e.sem_inc(S("mix_dve"), -1)
            for b in range(DB):
                e.wait_ge(S("hh_ready"), 1)
                e.sem_inc(S("hh_ready"), -1)
                e.tensor_tensor(HL[:, b, :], R2[:, b, :], HH[:, b, :].bitcast(F32), ALU.subtract).then_inc(S("dve_done"), 1)
                e.wait_ge(S("dve_done"), 1)
                e.sem_inc(S("dve_done"), -1)
            give(e, "h_ready", "r2_free")
            los(4)
            e.wait_ge(S("m_ready"), 1)
            e.sem_inc(S("m_ready"), -1)
            add_normed(MIX_POST)
            barrier(e, "dve")
            normed(R1, X_PRE)
            los(2)

            def cross(i, n):
                e.wait_ge(S("cs_psum"), 1)
                e.sem_inc(S("cs_psum"), -1)
                e.tensor_reduce(ST[0:n, 0:4], PS[0:n, 0:1024].rearrange("p (h k) -> p h k", h=4), AX.X, ALU.max).then_inc(S("dve_done"), 1)
                e.wait_ge(S("dve_done"), 1)
                e.sem_inc(S("dve_done"), -1)
                e.tensor_scalar(ST[0:n, 4:8], ST[0:n, 0:4], -float(P) ** -0.5, None, ALU.mult).then_inc(S("dve_done"), 1)
                e.wait_ge(S("dve_done"), 1)
                e.sem_inc(S("dve_done"), -1)
                give(e, "cnm_ready")
                e.wait_ge(S("cexp_ready"), 1)
                e.sem_inc(S("cexp_ready"), -1)
                e.reciprocal(ST[0:n, 0:4], ST[0:n, 8:12]).then_inc(S("dve_done"), 1)
                e.wait_ge(S("dve_done"), 1)
                e.sem_inc(S("dve_done"), -1)
                e.tensor_tensor(CP[0:n, :, :], CP[0:n, :, :], ST[0:n, 0:4].unsqueeze(2).broadcast_to([n, 4, MEM]), ALU.mult).then_inc(S("dve_done"), 1)
                e.wait_ge(S("dve_done"), 1)
                e.sem_inc(S("dve_done"), -1)
                give(e, "cp_ready")
                e.wait_ge(S("coh_ready"), 1)
                e.sem_inc(S("coh_ready"), -1)
                e.tensor_tensor(HL[:, 0:4, bass.ds(i, n)], PS[:, 2048:2048 + 4 * n].rearrange("p (h q) -> p h q", h=4),
                                     HH[:, 0:4, bass.ds(i, n)].bitcast(F32), ALU.subtract).then_inc(S("dve_done"), 1)
                e.wait_ge(S("dve_done"), 1)
                e.sem_inc(S("dve_done"), -1)
                give(e, "bank4")

            with e.Fori(0, TILES) as t:
                cross(t * P, P)
            give(e, "cv_free")
            cross(SEQ, DEC_SEQ)
            give(e, "cv_free", "h_ready")
            los(2)
            add_normed(X_POST)
            barrier(e, "dve")
            e.memset(R2[:, :, :], 0.0).then_inc(S("dve_done"), 1)
            e.wait_ge(S("dve_done"), 1)
            e.sem_inc(S("dve_done"), -1)
            normed(R1, FFN_PRE)
            give(e, "silu_free", "silu_free", "silu_free")
            with e.Fori(0, FB // 2) as i:
                for f in range(2):
                    for c in range(CH):
                        e.wait_ge(S("silu_ready"), 1)
                        e.sem_inc(S("silu_ready"), -1)
                        e.wait_ge(S("up_psum"), 1)
                        e.sem_inc(S("up_psum"), -1)
                        e.tensor_tensor(TMP[:, 1, chunk(c)], TMP[:, 0, chunk(c)], bank(3 + c, 0, CW), ALU.mult).then_inc(S("dve_done"), 1)
                        e.wait_ge(S("dve_done"), 1)
                        e.sem_inc(S("dve_done"), -1)
                        give(e, f"bank{3 + c}", "gu_ready", "silu_free")
                    lo(0)
                    for c in range(CH):
                        e.wait_ge(S("gh_ready"), 1)
                        e.sem_inc(S("gh_ready"), -1)
                        e.tensor_tensor(GL[:, f, chunk(c)], TMP[:, 1, chunk(c)], GH[:, f, chunk(c)].bitcast(F32), ALU.subtract).then_inc(S("dve_done"), 1)
                        e.wait_ge(S("dve_done"), 1)
                        e.sem_inc(S("dve_done"), -1)
                        if f == 1:
                            give(e, "g_ready", "g_ready")
                    lo(1)
                n = 0
                for c in range(CH):
                    for m in range(DB):
                        b = 6 + n % 2
                        n += 1
                        e.wait_ge(S("down_psum"), 1)
                        e.sem_inc(S("down_psum"), -1)
                        e.tensor_tensor(R2[:, m, chunk(c)], R2[:, m, chunk(c)], bank(b, 0, CW), ALU.add).then_inc(S("dve_done"), 1)
                        e.wait_ge(S("dve_done"), 1)
                        e.sem_inc(S("dve_done"), -1)
                        give(e, f"bank{b}")
                give(e, "down_end")
                lo(0)
                lo(1)
            e.wait_ge(S("silu_free"), 3)
            e.sem_inc(S("silu_free"), -3)
            add_normed(FFN_POST)
            barrier(e, "dve")


INPUTS = ["x_prompt", "mem_prompt", "x_sample", "cache_swa_k", "cache_swa_v", "cache_mem_k", "cache_mem_v", "state_rwkv",
          "state_shift", "norm_gains", "w_in", "attn_sink", "shift_mu", "rwkv_vecs", "rwkv_rk", "rwkv_w2", "rwkv_a2",
          "rwkv_g2", "w_out", "w_mem_q", "w_mem_kv", "w_mem_o", "w_gate_up", "w_down"]
OUTPUTS = [("y_prompt", (1, SEQ, D_MODEL)), ("y_sample", (1, DEC_SEQ, D_MODEL)),
           ("new_swa_k_prompt", (DEPTH, 1, WINDOW, 2, HEAD)), ("new_swa_v_prompt", (DEPTH, 1, WINDOW, 2, HEAD)),
           ("new_mem_k_prompt", (DEPTH, 1, MEM, MEM_HEADS, P)), ("new_mem_v_prompt", (DEPTH, 1, MEM, MEM_HEADS, P)),
           ("new_state_rwkv_prompt", (DEPTH, 1, 8, HEAD, HEAD)), ("new_state_shift_prompt", (DEPTH, 1, 1, RWKV_PROJ)),
           ("new_swa_k_sample", (DEPTH, 1, DEC_SEQ, 2, HEAD)), ("new_swa_v_sample", (DEPTH, 1, DEC_SEQ, 2, HEAD)),
           ("new_state_rwkv_sample", (DEPTH, 1, 8, HEAD, HEAD)), ("new_state_shift_sample", (DEPTH, 1, 1, RWKV_PROJ))]


def kernel(**inputs):
    import concourse.bacc as bacc
    from concourse.bass_utils import run_bass_kernel_spmd

    nc = bacc.Bacc("TRN2", target_bir_lowering=False, num_devices=1)
    arrays, io = {}, {}
    c, long = constants()
    for name, a in [(n, inputs[n]) for n in INPUTS] + [("consts", c), ("long", long)]:
        arrays[f"in_{name}"] = np.ascontiguousarray(a)
        io[name] = nc.dram_tensor(f"in_{name}", arrays[f"in_{name}"].shape, F32, kind="ExternalInput").ap()
    for name, shape in OUTPUTS:
        io[name] = nc.dram_tensor(f"out_{name}", shape, F32, kind="ExternalOutput").ap()
    program(nc, io)
    r = run_bass_kernel_spmd(nc, [arrays], core_ids=[0])
    return tuple(r.results[0][f"out_{name}"] for name, _ in OUTPUTS)
```

```python
from contextlib import ExitStack

import numpy as np

import concourse.bass as bass
from concourse import mybir

F32 = mybir.dt.float32
F32R = mybir.dt.float32r
ALU = mybir.AluOpType
ACT = mybir.ActivationFunctionType
AX = mybir.AxisListType

P = 128
D_MODEL, SEQ, DEC_SEQ, DEPTH, PAST_LEN = 1024, 1024, 32, 2, 512
T = SEQ + DEC_SEQ
CH = 3
CW = T // CH
DB = D_MODEL // P
HEAD, CHUNK, WINDOW = 64, 64, 128
A_WIDTH, KV_A, R_WIDTH = 512, 128, 512
N_HEADS_A = 8
PAIRS = R_WIDTH // P
UNITS = SEQ // 256
LORA_W, LORA_A, LORA_G = 64, 64, 160
RWKV_PROJ = 3 * R_WIDTH + LORA_W + LORA_A + LORA_G
IN_COLS = A_WIDTH + 2 * KV_A + RWKV_PROJ
R0 = A_WIDTH + 2 * KV_A
MEM, MEM_HEADS, MEM_WIDTH = 256, 4, 512
D_FF = 2816
FB = D_FF // P
TILES = SEQ // P
RMS_EPS, GN_EPS = 1e-6, 6.4e-4
NEG = -1e30
DECAY = float(np.exp(-0.5))
MIX_PRE, MIX_POST, X_PRE, X_POST, N_MEM, FFN_PRE, FFN_POST = range(7)

G_AT, MU_AT, SH_AT, RV_AT, RK_AT, PRM_ROWS = 0, 56, 71, 86, 110, 114
C_ID, C_PERM, C_MEAN, C_BD, C_BDM, C_CEN = (i * P for i in range(6))
C_M3 = 6 * P
C_NL = 9 * P
C_NU = 10 * P
C_LV = 11 * P
C_AE = 16 * P
C_AO = C_AE + 4 * 256
C_EPS = C_AO + 256
C_COLS = C_EPS + 2


def constants():
    c = np.zeros((P, C_COLS), np.float32)
    i, j = np.arange(P)[:, None], np.arange(P)[None, :]
    same = (i // 64) == (j // 64)
    c[:, C_ID:C_ID + P] = i == j
    c[:, C_PERM:C_PERM + P] = np.where((j % 64 < 32) & (i == j + 32), -1.0, 0.0) + ((j % 64 >= 32) & (i == j - 32))
    c[:, C_MEAN:C_MEAN + P] = 1.0 / D_MODEL
    c[:, C_BD:C_BD + P] = same
    c[:, C_BDM:C_BDM + P] = same / 64.0
    c[:, C_CEN:C_CEN + P] = (i == j) - same / 64.0
    c[:, C_M3:C_M3 + 2 * P] = np.tile(same & (i < j), (1, 2))
    c[:, C_M3 + 2 * P:C_M3 + 3 * P] = same & (i <= j)
    c[:, C_NL:C_NL + P] = -1.0 * ((i // 2 == j // 2) & (i > j))
    c[:, C_NU:C_NU + P] = -1.0 * ((i // 2 == j // 2) & (i < j))
    for n in range(5):
        s = 2 << n
        c[:, C_LV + n * P:C_LV + (n + 1) * P] = (i // (2 * s) == j // (2 * s)) & (i // s < j // s)
    cur = np.where((i < 64) & (j >= 64), NEG, 0.0)
    prev = np.where((i >= 64) & (j < 64), NEG, 0.0)
    for it in range(4):
        at = C_AE + it * 256
        c[:, at:at + P] = cur
        c[:, at + P:at + 2 * P] = NEG if it == 0 else prev
    c[:, C_AO:C_AO + P] = prev
    c[:, C_AO + P:C_AO + 2 * P] = cur
    c[:, C_EPS] = RMS_EPS
    c[:, C_EPS + 1] = GN_EPS
    pos = np.concatenate([np.arange(SEQ), PAST_LEN + np.arange(DEC_SEQ)]).astype(np.float32)
    inv = np.float32(10000.0) ** (-np.arange(32, dtype=np.float32) / np.float32(32))
    ang = (pos[None, :] * inv[:, None]).astype(np.float32)
    long = np.zeros((2, P, T), np.float32)
    long[0] = np.tile(np.cos(ang), (4, 1))
    long[1] = np.tile(np.sin(ang), (4, 1))
    return c, long


def program(nc, io):
    with ExitStack() as ctx:
        build(nc, io, ctx)


def build(nc, io, ctx):
    def sb(name, shape, dt=F32):
        return ctx.enter_context(nc.sbuf_tensor(name, shape, dt))

    R1 = sb("R1", [P, DB, T])
    R2 = sb("R2", [P, DB, T])
    HH, HL = sb("HH", [P, DB, T], F32R), sb("HL", [P, DB, T], F32R)
    GH, GL = sb("GH", [P, 2, T], F32R), sb("GL", [P, 2, T], F32R)
    TMP = sb("TMP", [P, 3, T])
    WRAW = sb("WRAW", [P, 2, 1024])
    WH, WL = sb("WH", [P, 2, 1024], F32R), sb("WL", [P, 2, 1024], F32R)
    CST = sb("CST", [P, C_COLS])
    PRM = sb("PRM", [P, PRM_ROWS])
    PC = sb("PC", [P, 16])
    SINK = sb("SINK", [P, 8])
    ST = sb("ST", [P, 64])
    EC = sb("EC", [P, 40])
    AUX = sb("AUX", [P, 1088])
    PS = ctx.enter_context(nc.psum_tensor("PS", [P, 8 * 512], F32))

    x_spill = nc.dram_tensor("x_spill", [P, DB, T], F32, kind="Internal").ap()
    mix_dram = nc.dram_tensor("mix_dram", [P, DB, T], F32, kind="Internal").ap()
    mem_dram = nc.dram_tensor("mem_dram", [P, DB, MEM], F32, kind="Internal").ap()

    for_vector = {n + "_psum" for n in ("swap", "score", "sm", "l", "dx", "u", "ds", "kk", "rk", "sin", "cs", "up", "down", "xT_dve")}
    sems = {}

    def S(name):
        if name.endswith("_psum"):
            name = "product_for_vector" if name in for_vector else "product_for_scalar"
        if name not in sems:
            sems[name] = ctx.enter_context(nc.semaphore(name))
        return sems[name]

    def give(e, *names):
        for name in names:
            e.sem_inc(S(name), 1)

    def bank(b, a=0, z=512):
        return PS[:, b * 512 + a:b * 512 + z]

    ENG = ["act", "dve", "pe", "pool"]

    def barrier(e, who):
        e.drain()
        for other in ENG:
            if other != who:
                give(e, f"end_{who}_{other}")
        for other in ENG:
            if other != who:
                e.wait_ge(S(f"end_{other}_{who}"), 1)
                e.sem_inc(S(f"end_{other}_{who}"), -1)

    def cst(at, w=P):
        return CST[:, at:at + w]

    ident, perm, mean = cst(C_ID), cst(C_PERM), cst(C_MEAN)

    def chunk(c):
        return slice(c * CW, (c + 1) * CW)

    r2flat = R2[:, :, :].rearrange("p a t -> p (a t)")
    tflat = TMP[:, :, :].rearrange("p a t -> p (a t)")
    PRAW = r2flat[:, 6 * T:6 * T + T + 2]
    r1tail = R1[:, 7, :]
    RT = r1tail[:, 0:768].rearrange("p (a t) -> p a t", t=P)
    SC = r2flat[:, 3 * T:3 * T + 2048].rearrange("p (h k) -> p h k", h=8)
    PT = tflat[:, 0:2048].rearrange("p (h k q) -> p h k q", h=8, k=2)
    RU = TMP[:, 2, 0:768].rearrange("p (a t) -> p a t", t=P)
    VST = TMP[:, 2, 768:896]
    KCR = TMP[:, 2, 896:1024]
    QR = R2[:, 5, 0:512].rearrange("p (a t) -> p a t", t=P)
    KR = R2[:, 5, 512:1024].rearrange("p (v s t) -> p v s t", v=2, s=2)
    VT = AUX[:, 0:256].rearrange("p (s t) -> p s t", s=2)
    OT = AUX[:, 256:768].rearrange("p (a t) -> p a t", t=P)
    KO = AUX[:, 768:896]
    COS, SIN = R2[:, 6, :], R2[:, 7, :]
    KK, RR, BB, KF, VV, GG, BON, YY = (R1[:, i, :] for i in range(8))
    TWA, SG1, SG2, DD2, DD, SEG = (R2[:, i, :] for i in range(6))
    LTM, XXF = r2flat[:, 3 * T:3 * T + 1536], r2flat[:, 3 * T + 1536:3 * T + 2560]
    T1F = r2flat[:, 3 * T + 2560:3 * T + 3072]
    ATM = AUX[:, 768:1024].rearrange("p (x t) -> p x t", x=2)
    QS = tflat[:, 2560:2816].rearrange("p (x t) -> p x t", x=2)
    w0 = 6 * T
    US = r2flat[:, w0:w0 + 256].rearrange("p (x t) -> p x t", x=2)
    MVS = r2flat[:, w0 + 256:w0 + 512].rearrange("p (x t) -> p x t", x=2)
    ELF = r2flat[:, w0 + 512:w0 + 1536]
    PTS = r2flat[:, w0 + 1536:w0 + 1792].rearrange("p (x t) -> p x t", x=2)

    def unit(u):
        return (u * 256, P, 2, 5) if u < UNITS else (SEQ, DEC_SEQ, 1, 4)

    def bkv(u):
        return tflat[:, (u % 2) * 768:(u % 2 + 1) * 768].rearrange("p (x a t) -> p x a t", x=2, a=3)

    def heads(buf, at, n, tiles):
        return buf[0:n, at:at + 2 * tiles * n].rearrange("p (g t) -> p g t", g=2 * tiles)

    SBD = AUX[:, 0:128]
    STMP = AUX[:, 128:256]
    SIO = AUX[:, 256:384]
    LW = AUX[:, 384:768]
    SAMPLE_IN, SAMPLE_OUT = AUX[:, 384:512], AUX[:, 512:640]
    SHC = AUX[:, 1024:1056]
    xq = r2flat[:, 4 * T:8 * T]
    CKT = xq[:, 0:1024].rearrange("p (h k) -> p h k", h=4)
    CV = xq[:, 1024:2048].rearrange("p (k d) -> p k d", k=2)
    CKR = xq[:, 2048:3072].rearrange("p (k d) -> p k d", k=2)
    CP = xq[:, 3072:4096].rearrange("p (h k) -> p h k", h=4)
    CPT = tflat[:, 0:1024].rearrange("p (h k q) -> p h k q", h=4, k=2)
    CQ = tflat[:, 1024:1536].rearrange("p (h q) -> p h q", h=4)

    HS = [0, 2, 4, 6, 1, 3, 5, 7]
    DOWN_BANKS = [6, 7, 0, 1, 2, 3, 4, 5]
    block = ctx.enter_context(nc.Block())

    def w_block(w, l, c0, cols=P, kb=DB):
        return w[bass.ds(l, 1)].rearrange("a (k p) n -> p (a k) n", p=P)[:, 0:kb, bass.ds(c0, cols)]

    @block.sync
    def _(e):
        def weight(slot, src, view=None):
            e.wait_ge(S(f"w_free{slot}"), 1)
            e.sem_inc(S(f"w_free{slot}"), -1)
            dst = WRAW[:, slot, :]
            e.dma_start(view(dst) if view else dst, src).then_inc(S(f"w_full{slot}"), 16)

        def w8(slot, w, l, c0):
            weight(slot, w_block(w, l, c0), view=lambda d: d.rearrange("p (k n) -> p k n", k=DB))

        def stream(w, l, pairs, c0=0):
            with e.Fori(0, pairs) as i:
                for s in range(2):
                    w8(s, w, l, (i * 2 + s) * P + c0)

        with e.Fori(0, DEPTH) as l:
            stream(io["w_mem_kv"], l, 4)
            stream(io["w_in"], l, 2)
            for s in range(2):
                e.wait_ge(S(f"w_free{s}"), 1)
                e.sem_inc(S(f"w_free{s}"), -1)
                for g in range(2):
                    done = "k_part" if g == 0 else f"w_full{s}"
                    e.dma_start(WRAW[:, s, :].rearrange("p (k g n) -> p k g n", k=DB, g=2)[:, :, g, :],
                                w_block(io["w_in"], l, A_WIDTH + s * HEAD, HEAD)).then_inc(S(done), 16)
                    if g == 0:
                        e.wait_ge(S("k_part"), 16)
                        e.sem_inc(S("k_part"), -16)
            w8(0, io["w_in"], l, A_WIDTH + KV_A)
            w8(1, io["w_in"], l, R0 + 3 * R_WIDTH)
            w8(0, io["w_in"], l, R0 + 3 * R_WIDTH + P)
            weight(1, w_block(io["w_in"], l, R0 + 3 * R_WIDTH + 2 * P, 32),
                   view=lambda d: d.rearrange("p (k n) -> p k n", k=DB)[:, :, 0:32])
            with e.Fori(0, PAIRS) as j:
                for b in range(3):
                    w8(b % 2, io["w_in"], l, j * P + R0 + b * R_WIDTH)
                e.wait_ge(S("w_free1"), 1)
                e.sem_inc(S("w_free1"), -1)
                lw = WRAW[:, 1, :]
                parts = ((lw[0:64, 0:P], io["rwkv_w2"][bass.ds(l, 1)]), (lw[64:128, 0:P], io["rwkv_a2"][bass.ds(l, 1)]),
                         (lw[:, P:2 * P], io["rwkv_g2"][bass.ds(l, 1), 0:P, :]),
                         (lw[0:32, 2 * P:3 * P], io["rwkv_g2"][bass.ds(l, 1), P:LORA_G, :]))
                for n, (dst, src) in enumerate(parts):
                    e.dma_start(dst, src.rearrange("a r n -> (a r) n")[:, bass.ds(j * P, P)]).then_inc(S("lw_part" if n < 3 else "w_full1"), 16)
                    if n == 2:
                        e.wait_ge(S("lw_part"), 48)
                        e.sem_inc(S("lw_part"), -48)
            stream(io["w_out"], l, 4)
            stream(io["w_mem_q"], l, 2)
            with e.Fori(0, 2) as i:
                for s in range(2):
                    weight(s, w_block(io["w_mem_o"], l, (i * 2 + s) * 2 * P, 2 * P, 4),
                           view=lambda d: d.rearrange("p (k n) -> p k n", k=4))
            with e.Fori(0, FB // 2) as i:
                for f in range(2):
                    w8(0, io["w_gate_up"], l, (i * 2 + f) * P)
                    w8(1, io["w_gate_up"], l, (i * 2 + f) * P + D_FF)
                for f in range(2):
                    weight(f, io["w_down"][bass.ds(l, 1), bass.ds((i * 2 + f) * P, P), :].rearrange("a p n -> p (a n)"))
        for s in range(2):
            weight(s, io["w_down"][0, 0:P, :])

    @block.gpsimd
    def _(e):
        due = e.alloc_register("moves_due")
        e.reg_mov(due, 0)

        def move(dst, src):
            e.dma_start(dst, src).then_inc(S("moves"), 16)

        def moved(n=1):
            e.reg_add(due, due, 16 * n)
            e.wait_ge(S("moves"), e.snap(due, min_val=16))
            give(e, "moves_seen")

        move(CST[:, :], io["consts"])
        moved()
        give(e, "cst_act", "cst_dve", "cst_pe")

        def tokens_in(src, rows):
            e.wait_ge(S("xin_free"), 1)
            e.sem_inc(S("xin_free"), -1)
            move(R2[0:rows, 0, 0:D_MODEL], src)
            moved()
            give(e, "xin_full")

        with e.Fori(0, MEM // P) as j:
            tokens_in(io["mem_prompt"][0, bass.ds(j * P, P), :], P)
        e.wait_ge(S("memT_ready"), 1)
        e.sem_inc(S("memT_ready"), -1)
        move(mem_dram, R1[:, :, 0:MEM])
        moved()
        give(e, "memT_saved_act", "memT_saved_dve")
        with e.Fori(0, TILES) as j:
            tokens_in(io["x_prompt"][0, bass.ds(j * P, P), :], P)
        tokens_in(io["x_sample"][0], DEC_SEQ)
        barrier(e, "pool")

        with e.Fori(0, DEPTH) as l:
            prow = TMP[:, 0, 0:P]

            def rows(at, src):
                move(prow[at:at + src.shape[0], 0:src.shape[1]], src)

            lay = lambda name: io[name][bass.ds(l, 1)]
            e.wait_ge(S("prow_clear"), 1)
            e.sem_inc(S("prow_clear"), -1)
            rows(G_AT, lay("norm_gains").rearrange("a n (b p) -> (a n b) p", p=P))
            for at, src in ((MU_AT, lay("shift_mu")), (SH_AT, lay("state_shift").rearrange("a b c n -> (a b c) n"))):
                rows(at, src[:, 0:14 * P].rearrange("a (b p) -> (a b) p", p=P))
                rows(at + 14, src[:, 14 * P:RWKV_PROJ])
            rows(RV_AT, lay("rwkv_vecs").rearrange("a n (b p) -> (a n b) p", p=P))
            rows(RK_AT, lay("rwkv_rk").rearrange("a (b g) p -> (a b) (g p)", g=2))
            move(SINK[:, :], lay("attn_sink").broadcast_to([P, 8]))
            moved(8)
            give(e, "prm_rows")
            move(R2[:, :, 0:MEM], mem_dram)
            moved()
            give(e, "memT_act", "memT_dve")
            move(x_spill, R1[:, :, :])
            moved()
            for k, out in ((0, "new_mem_k_prompt"), (1, "new_mem_v_prompt")):
                for tt in range(2):
                    e.wait_ge(S("memtok_ready"), 1)
                    e.sem_inc(S("memtok_ready"), -1)
                    move(lay(out).rearrange("a b m h d -> (a b m) (h d)")[tt * P:(tt + 1) * P, :], R2[:, 2 + 2 * k + tt, 512:1024])
            moved(4)
            barrier(e, "pool")
            e.wait_ge(S("cos_free"), 1)
            e.sem_inc(S("cos_free"), -1)
            move(COS, io["long"][0])
            move(SIN, io["long"][1])
            moved(2)
            give(e, "cos_ready")

            def store_att(n, c0):
                e.wait_ge(S("ot_ready"), 1)
                e.sem_inc(S("ot_ready"), -1)
                move(mix_dram[:, 0:4, bass.ds(c0, n)], OT[:, :, 0:n])
                moved()
                give(e, "ot_free")

            with e.Fori(0, TILES) as i:
                store_att(P, i * P)

            def store_kv(n, slot, okey, oval):
                e.wait_ge(S("ko_ready"), 1)
                e.sem_inc(S("ko_ready"), -1)
                move(lay(okey).rearrange("a b m h d -> (a b m) (h d)"), KO[0:n, :])
                move(lay(oval).rearrange("a b m h d -> (a b m) (h d)"), VT[0:n, slot, :])
                moved(2)

            store_kv(P, 1, "new_swa_k_prompt", "new_swa_v_prompt")
            for v in range(2):
                e.wait_ge(S("kcr_free"), 1)
                e.sem_inc(S("kcr_free"), -1)
                for g in range(2):
                    move(KCR[:, g * HEAD:(g + 1) * HEAD], lay("cache_swa_k").rearrange("a b m h d -> (a b m) h d")[:, v, :])
                moved(2)
                give(e, "kcr_ready")
            e.wait_ge(S("vt_free"), 1)
            e.sem_inc(S("vt_free"), -1)
            move(VT[:, 1, :], lay("cache_swa_v").rearrange("a b m h d -> (a b m) (h d)"))
            moved()
            give(e, "vcache_ready")
            store_att(DEC_SEQ, SEQ)
            store_kv(DEC_SEQ, 0, "new_swa_k_sample", "new_swa_v_sample")
            barrier(e, "pool")

            def level_masks(u):
                _, n, tiles, levels = unit(u)
                mask = lambda at: CST[0:n, at:at + n].unsqueeze(1).broadcast_to([n, 2 * tiles, n])
                lt, xt = heads(LTM, 0, n, tiles), heads(XXF, 512, n, tiles)
                e.wait_ge(S("lt_ready"), 1)
                e.sem_inc(S("lt_ready"), -1)
                for s in range(levels):
                    e.wait_ge(S("elt_free"), 1)
                    e.sem_inc(S("elt_free"), -1)
                    e.tensor_tensor(heads(ELF, (s % 2) * 512, n, tiles), lt, mask(C_LV + s * P), ALU.mult).then_inc(S("elt_ready"), 1)
                    if s == 0:
                        e.tensor_tensor(xt, lt, mask(C_NU), ALU.mult).then_inc(S("pool_done"), 1)
                        e.wait_ge(S("pool_done"), 1)
                        e.sem_inc(S("pool_done"), -1)
                        e.tensor_tensor(xt, xt, mask(C_ID), ALU.add).then_inc(S("xt_ready"), 1)

            with e.Fori(0, PAIRS) as j:
                def states(name, buf, store):
                    dram = lay(name).rearrange("a b h v k -> (a b h v) k")
                    for h in range(2):
                        d = dram[bass.ds(j * P + h * HEAD, HEAD), :]
                        t = buf[h * HEAD:(h + 1) * HEAD, h * HEAD:(h + 1) * HEAD]
                        move(d if store else t, t if store else d)

                e.wait_ge(S("sin_free"), 1)
                e.sem_inc(S("sin_free"), -1)
                states("state_rwkv", SAMPLE_IN, False)
                moved(2)
                give(e, "state_in")
                for u in range(UNITS + 1):
                    level_masks(u)
                e.wait_ge(S("state_out"), 1)
                e.sem_inc(S("state_out"), -1)
                states("new_state_rwkv_prompt", SIO, True)
                e.wait_ge(S("state_out"), 1)
                e.sem_inc(S("state_out"), -1)
                states("new_state_rwkv_sample", SAMPLE_OUT, True)
                moved(4)
                give(e, "states_saved")
                e.wait_ge(S("y_ready"), 1)
                e.sem_inc(S("y_ready"), -1)
                move(mix_dram[:, bass.ds(j + 4, 1), :].rearrange("p a t -> p (a t)"), YY)
                moved()
                give(e, "y_saved")
            e.wait_ge(S("shc_ready"), 1)
            e.sem_inc(S("shc_ready"), -1)
            for g, out in ((0, "new_state_shift_prompt"), (1, "new_state_shift_sample")):
                o = lay(out).rearrange("a b c n -> (a b c) n")
                at = g * 64
                move(o[:, 0:14 * P].rearrange("a (b p) -> (a b) p", p=P), AUX[at:at + 14, 256:384])
                move(o[:, 14 * P:RWKV_PROJ], AUX[at + 14:at + 15, 256:288])
            moved(4)
            barrier(e, "pool")
            move(R2[:, :, :], mix_dram)
            move(R1[:, :, :], x_spill)
            moved(2)
            give(e, "mix_act", "mix_dve")
            barrier(e, "pool")

            def mem_in(ksrc, vsrc):
                e.wait_ge(S("cv_free"), 1)
                e.sem_inc(S("cv_free"), -1)
                for dst, name in ((CKR, ksrc), (CV, vsrc)):
                    move(dst, lay(name).rearrange("a b (t m) h d -> m (a b t) (h d)", t=2))
                moved(2)
                give(e, "ckr_ready")

            mem_in("new_mem_k_prompt", "new_mem_v_prompt")
            mem_in("cache_mem_k", "cache_mem_v")
            barrier(e, "pool")
            barrier(e, "pool")

        def tokens_out(dst, n):
            e.wait_ge(S("xout_ready"), 1)
            e.sem_inc(S("xout_ready"), -1)
            move(dst, R2[0:n, 4, 0:D_MODEL])
            moved()
            give(e, "xout_free")

        with e.Fori(0, TILES) as j:
            tokens_out(io["y_prompt"][0, bass.ds(j * P, P), :], P)
        tokens_out(io["y_sample"][0], DEC_SEQ)

    @block.tensor
    def _(e):
        def claim(*banks):
            for b in banks:
                e.wait_ge(S(f"bank{b}"), 1)
                e.sem_inc(S(f"bank{b}"), -1)

        def transposes(items, b, name, base=0):
            claim(b)
            for n, (src, off) in enumerate(items):
                k, m = src.shape
                ins = e.matmul(PS[0:m, b * 512 + off:b * 512 + off + k], src, CST[0:k, C_ID:C_ID + k],
                               is_transpose=True, start=True, stop=True)
            ins.then_inc(S(name), 1)

        def products(out, lhs, rhs, slot_w, n):
            first = True
            for k in range(n):
                for wp, xp in ((0, 0), (1, 0), (0, 1)):
                    ins = e.matmul(out, lhs(k, wp), rhs(k, xp), start=first, stop=(k == n - 1 and xp == 1))
                    first = False
            return ins

        def dense8(slot, b0, name, m=P, n=T, cw=CW, ch=CH):
            e.wait_ge(S(f"w_ready{slot}"), 1)
            e.sem_inc(S(f"w_ready{slot}"), -1)
            W = [x[:, slot, :].rearrange("p (k n) -> p k n", k=DB) for x in (WH, WL)]
            H = [HH, HL]
            for c in range(ch):
                claim(b0 + c)
                products(PS[0:m, (b0 + c) * 512:(b0 + c) * 512 + cw], lambda k, p: W[p][:, k, 0:m],
                         lambda k, p: H[p][:, k, c * cw:(c + 1) * cw], slot, DB).then_inc(S(name), 1)

        def dense_pair(names=("dense_psum", "dense_psum")):
            e.wait_ge(S("w_ready0"), 1)
            e.sem_inc(S("w_ready0"), -1)
            e.wait_ge(S("w_ready1"), 1)
            e.sem_inc(S("w_ready1"), -1)
            claim(0, 1, 2, 3, 4, 5)
            for k in range(DB):
                e.wait_ge(S("h_ready"), 1)
                e.sem_inc(S("h_ready"), -1)
                for s in range(2):
                    for c in range(CH):
                        for w, h in ((WH, HH), (WL, HH), (WH, HL)):
                            ins = e.matmul(bank(3 * s + c, 0, CW), w[:, s, k * P:(k + 1) * P], h[:, k, chunk(c)],
                                           start=(k == 0 and w is WH and h is HH), stop=(k == DB - 1 and h is HL))
                        if k == DB - 1:
                            ins.then_inc(S(names[s]), 1)

        def block_stats():
            claim(0, 1, 2)
            for b in range(DB):
                e.wait_ge(S("r1sq_ready"), 1)
                e.sem_inc(S("r1sq_ready"), -1)
                for c in range(CH):
                    ins = e.matmul(bank(c, 0, CW), mean, R2[:, b, chunk(c)], start=(b == 0), stop=(b == DB - 1))
                    if b == DB - 1:
                        ins.then_inc(S("var_psum"), 1)

        def stats(n=T):
            e.wait_ge(S("sq_sum"), 1)
            e.sem_inc(S("sq_sum"), -1)
            cw = CW if n == T else n
            for c in range(n // cw):
                claim(c)
                e.matmul(bank(c, 0, cw), mean, TMP[:, 2, c * cw:(c + 1) * cw], start=True, stop=True).then_inc(S("var_psum"), 1)

        e.wait_ge(S("cst_pe"), 1)
        e.sem_inc(S("cst_pe"), -1)

        def tokens_in(n):
            e.wait_ge(S("xin_full"), 1)
            e.sem_inc(S("xin_full"), -1)
            for g in range(2):
                transposes([(R2[0:n, 0, (4 * g + b) * P:(4 * g + b + 1) * P], b * P) for b in range(4)], g, "xT_psum" if g == 0 else "xT_dve_psum")
            
        with e.Fori(0, MEM // P) as j:
            tokens_in(P)
        with e.Fori(0, TILES) as j:
            tokens_in(P)
        tokens_in(DEC_SEQ)
        barrier(e, "pe")
        with e.Fori(0, DEPTH) as l:
            e.wait_ge(S("prm_rows_pe"), 1)
            e.sem_inc(S("prm_rows_pe"), -1)
            transposes([(TMP[0:PRM_ROWS, 0, 0:P], 0)], 7, "prm_psum")
            stats(MEM)
            e.wait_ge(S("h_ready"), DB)
            e.sem_inc(S("h_ready"), -DB)
            with e.Fori(0, 4) as i:
                for s in range(2):
                    dense8(s, 3 * s, "dense_psum", n=MEM, cw=MEM, ch=1)
            e.wait_ge(S("kvT_ready"), 1)
            e.sem_inc(S("kvT_ready"), -1)
            for k in range(2):
                for tt in range(2):
                    transposes([(R2[:, k * 4 + b, MEM + tt * P:MEM + (tt + 1) * P], b * P) for b in range(4)], k * 2 + tt, "memtok_psum")
            stats()
            barrier(e, "pe")
            dense_pair()
            for n in range(8):
                dense8(n % 2, 3 * (n % 2), "dense_psum")
            e.wait_ge(S("cos_pe"), 1)
            e.sem_inc(S("cos_pe"), -1)

            def att(i, n, slot, parts):
                tok = bass.ds(i, n)
                claim(0, 1)
                e.matmul(PS[:, 0:4 * n].rearrange("p (a t) -> p a t", a=4), perm, R1[:, 0:4, tok], start=True, stop=True)
                e.matmul(PS[:, 512:512 + 2 * n].rearrange("p (a t) -> p a t", a=2), perm, R1[:, 4:6, tok], start=True, stop=True).then_inc(S("swap_psum"), 1)
                e.wait_ge(S("vst_ready"), 1)
                e.sem_inc(S("vst_ready"), -1)
                transposes([(VST[:, 0:n], 0)], 6, "v_psum")
                e.wait_ge(S("qk_ready"), 1)
                e.sem_inc(S("qk_ready"), -1)
                for hs, h in enumerate(HS):
                    p = (h % 2) * HEAD
                    if hs % 2 == 0:
                        claim(2 + hs // 2)
                    for ks, nk, col in parts:
                        at = 1024 + hs * 256 + col
                        ins = e.matmul(PS[0:n, at:at + nk], QR[p:p + HEAD, h // 2, 0:n], KR[p:p + HEAD, h // 4, ks, 0:nk] if not (len(parts) == 1)
                                       else KR[p:p + HEAD, h // 4, :, :].rearrange("p s t -> p (s t)"), start=True, stop=True)
                    if hs % 2 == 1:
                        ins.then_inc(S("score_psum"), 1)
                e.wait_ge(S("prob_ready"), 1)
                e.sem_inc(S("prob_ready"), -1)
                kparts = [(0, 0, P), (1, P, P)] if len(parts) == 1 else [(ks, col, nk) for ks, nk, col in parts]
                for g in range(4):
                    b = (0, 1, 6, 7)[g]
                    transposes([(SC[0:n, 2 * g + hh, col:col + nk], hh * 256 + kt * P) for hh in range(2)
                                for kt, (ks, col, nk) in enumerate(kparts)], b, "pT_psum")
                e.wait_ge(S("pT_ready"), 1)
                e.sem_inc(S("pT_ready"), -1)
                claim(2)
                for hs, h in enumerate(HS):
                    p, kv = (h % 2) * HEAD, h // 4
                    for kt, (ks, col, nk) in enumerate(kparts):
                        ins = e.matmul(PS[p:p + HEAD, 1024 + (h // 2) * n:1024 + (h // 2) * n + n],
                                       VT[0:nk, ks, kv * HEAD:(kv + 1) * HEAD], PT[0:nk, hs, kt, 0:n],
                                       start=(kt == 0), stop=(kt == 1))
                ins.then_inc(S("o_psum"), 1)

            def keys_out(n, slot):
                claim(0)
                for v in range(2):
                    ins = e.matmul(PS[0:n, v * HEAD:(v + 1) * HEAD], KR[0:HEAD, v, slot, 0:n], CST[0:HEAD, C_ID:C_ID + HEAD],
                                   is_transpose=True, start=True, stop=True)
                ins.then_inc(S("ko_psum"), 1)

            with e.Fori(0, TILES // 2) as i:
                for s in range(2):
                    att((i * 2 + s) * P, P, s, [(0, 256, 0)])
            keys_out(P, 1)
            for v in range(2):
                e.wait_ge(S("kcr_ready"), 1)
                e.sem_inc(S("kcr_ready"), -1)
                transposes([(KCR[:, :], 0)], v, "kc_psum")
            e.wait_ge(S("vcache_ready"), 1)
            e.sem_inc(S("vcache_ready"), -1)
            att(SEQ, DEC_SEQ, 0, [(0, DEC_SEQ, 0), (1, P, DEC_SEQ)])
            keys_out(DEC_SEQ, 0)
            barrier(e, "pe")

            def by_token(u):
                t0, n, tiles, _ = unit(u)
                for x in range(tiles):
                    transposes([(R1[:, a, t0 + x * n:t0 + (x + 1) * n], o * P) for o, a in enumerate((0, 2, 3, 4))], x, "tm_psum")

            def scores(u, x):
                t0, n, _, _ = unit(u)
                tok = slice(t0 + x * n, t0 + (x + 1) * n)
                for h in range(2):
                    p = slice(h * HEAD, (h + 1) * HEAD)
                    b = 2 + h - 2 * x
                    claim(b)
                    out = PS[0:n, b * 512:b * 512 + 4 * n].rearrange("p (a t) -> p a t", a=4)
                    e.matmul(out[:, 0:4:3, :], R1[p, 2, tok], R1[p, 0:2, tok], start=True, stop=True)
                    e.matmul(out[:, 1:3, :], R1[p, 3, tok], R1[p, 0:2, tok], start=True, stop=True).then_inc(S("sm_psum"), 1)

            def low(u):
                t0, n, tiles, _ = unit(u)
                for h in range(2):
                    p = slice(h * HEAD, (h + 1) * HEAD)
                    claim(2 + h)
                    for x in range(tiles):
                        tok = slice(t0 + x * n, t0 + (x + 1) * n)
                        at = (2 + h) * 512 + x * n
                        ins = e.matmul(PS[0:n, at:at + n], R1[p, 0, tok], R1[p, 2, tok], start=True, stop=True)
                    ins.then_inc(S("l_psum"), 1)

            def value_parts(u):
                _, n, tiles, _ = unit(u)
                e.wait_ge(S("tm_ready"), 1)
                e.sem_inc(S("tm_ready"), -1)
                e.wait_ge(S("sm_ready"), 1)
                e.sem_inc(S("sm_ready"), -1)
                yb = (4, 7)[u % 2]
                claim(yb)
                for x in range(tiles):
                    for h in range(2):
                        e.matmul(PS[h * HEAD:(h + 1) * HEAD, yb * 512 + x * n:yb * 512 + (x + 1) * n], bkv(u)[0:n, x, 2, h * HEAD:(h + 1) * HEAD],
                                 heads(LTM, 1024, n, tiles)[:, 2 * x + h, :], start=(x == 0), stop=False, skip_group_check=True)
                claim(3)
                for x in range(tiles):
                    for h in range(2):
                        at = 1536 + x * P + h * HEAD
                        ins = e.matmul(PS[0:n, at:at + HEAD], heads(LTM, 512, n, tiles)[:, 2 * x + h, :], bkv(u)[0:n, x, 2, h * HEAD:(h + 1) * HEAD],
                                       start=True, stop=True)
                ins.then_inc(S("mv_psum"), 1)

            def level_left(u, s):
                _, n, tiles, _ = unit(u)
                e.wait_ge(S("elt_ready"), 1)
                e.sem_inc(S("elt_ready"), -1)
                e.wait_ge(S("x_ready"), 1)
                e.sem_inc(S("x_ready"), -1)
                for x in range(tiles):
                    if s == 0:
                        claim(2 + x)
                    for h in range(2):
                        g, at = 2 * x + h, (2 + x) * 512 + h * n
                        ins = e.matmul(PS[0:n, at:at + n], heads(ELF, (s % 2) * 512, n, tiles)[:, g, :],
                                       heads(XXF, 0, n, tiles)[:, g, :], start=True, stop=True)
                    ins.then_inc(S("t1_psum"), 1)

            def level_right(u, s):
                _, n, tiles, levels = unit(u)
                xt, t1 = heads(XXF, 512, n, tiles), heads(T1F, 0, n, tiles)
                e.wait_ge(S("xt_ready"), 1)
                e.sem_inc(S("xt_ready"), -1)
                if s == 0:
                    claim(0, 1)
                if s < levels - 1:
                    for x in range(tiles):
                        e.wait_ge(S("t1_ready"), 1)
                        e.sem_inc(S("t1_ready"), -1)
                        for g in (2 * x, 2 * x + 1):
                            ins = e.matmul(PS[0:n, g * n:(g + 1) * n], xt[:, g, :], t1[:, g, :], start=True, stop=True)
                    ins.then_inc(S("dx_psum"), 1)
                else:
                    e.wait_ge(S("t1_ready"), tiles)
                    e.sem_inc(S("t1_ready"), -tiles)
                for g in range(2 * tiles):
                    ins = e.matmul(PS[0:n, 512 + g * n:512 + (g + 1) * n], t1[:, g, :], xt[:, g, :], start=True, stop=True)
                ins.then_inc(S("dx_psum"), 1)

            def solved(u):
                _, n, tiles, _ = unit(u)
                xt = heads(XXF, 512, n, tiles)
                e.wait_ge(S("xt_ready"), 1)
                e.sem_inc(S("xt_ready"), -1)
                give(e, "bank0", "bank1")
                for x in range(tiles):
                    for h in range(2):
                        ins = e.matmul(PS[h * HEAD:(h + 1) * HEAD, 1024 + x * n:1024 + (x + 1) * n], ATM[0:n, x, h * HEAD:(h + 1) * HEAD],
                                       xt[:, 2 * x + h, :], start=True, stop=True)
                ins.then_inc(S("pts_psum"), 1)
                e.wait_ge(S("mv_ready"), 1)
                e.sem_inc(S("mv_ready"), -1)
                if tiles == 1:
                    claim(3)
                for x in range(tiles):
                    for h in range(2):
                        at = 1536 + x * P + h * HEAD
                        ins = e.matmul(PS[0:n, at:at + HEAD], xt[:, 2 * x + h, :], MVS[0:n, x, h * HEAD:(h + 1) * HEAD], start=True, stop=True)
                ins.then_inc(S("q_psum"), 1)

            def chunk_u(u, c):
                t0, n, _, _ = unit(u)
                cn, x, yb = min(n, CHUNK), c // 2, (4, 7)[u % 2]
                a = (c % 2) * CHUNK
                if c == 0:
                    e.wait_ge(S("pq_ready"), 1)
                    e.sem_inc(S("pq_ready"), -1)
                e.wait_ge(S("state_ready"), 1)
                e.sem_inc(S("state_ready"), -1)
                e.matmul(PS[a:a + cn, 3072:3072 + P], PTS[:, x, a:a + cn], SBD, start=True, stop=True).then_inc(S("u_psum"), 1)
                e.matmul(PS[:, yb * 512 + c * CHUNK:yb * 512 + c * CHUNK + cn], SBD, RR[:, t0 + c * CHUNK:t0 + c * CHUNK + cn],
                         start=False, stop=False, skip_group_check=True)

            def chunk_state(u, c):
                _, n, _, _ = unit(u)
                r, x = slice((c % 2) * CHUNK, (c % 2) * CHUNK + min(n, CHUNK)), c // 2
                e.wait_ge(S("u_ready"), 1)
                e.sem_inc(S("u_ready"), -1)
                e.matmul(PS[:, 2560:2560 + P], bkv(u)[r, x, 1, :], bkv(u)[r, x, 2, :], start=True, stop=False)
                e.matmul(PS[:, 2560:2560 + P], bkv(u)[r, x, 0, :], US[r, x, :], start=False, stop=True).then_inc(S("ds_psum"), 1)

            def outputs(u):
                _, n, tiles, _ = unit(u)
                yb = (4, 7)[u % 2]
                for x in range(tiles):
                    for h in range(2):
                        ins = e.matmul(PS[h * HEAD:(h + 1) * HEAD, yb * 512 + x * n:yb * 512 + (x + 1) * n], US[0:n, x, h * HEAD:(h + 1) * HEAD],
                                       heads(tflat, 1536 + (u % 2) * 512, n, tiles)[:, 2 * x + h, :], start=False, stop=True, skip_group_check=True)
                ins.then_inc(S("y_psum"), 1)

            with e.Fori(0, PAIRS) as j:
                for s in (0, 1, 0):
                    dense8(s, 3 * s, "dense_psum")
                e.wait_ge(S("w_ready1"), 1)
                e.sem_inc(S("w_ready1"), -1)
                e.wait_ge(S("lw_ready"), 1)
                e.sem_inc(S("lw_ready"), -1)
                for c in range(CH):
                    claim(3 + c)
                    e.matmul(bank(3 + c, 0, CW), LW[0:64, 0:P], TWA[0:64, chunk(c)], start=True, stop=True).then_inc(S("z_psum"), 1)
                for c in range(CH):
                    claim(c)
                    e.matmul(bank(c, 0, CW), LW[64:128, 0:P], TWA[64:128, chunk(c)], start=True, stop=True).then_inc(S("z_psum"), 1)
                for c in range(CH):
                    claim(3 + c)
                    e.matmul(bank(3 + c, 0, CW), LW[:, P:2 * P], SG1[:, chunk(c)], start=True, stop=False)
                    e.matmul(bank(3 + c, 0, CW), LW[0:32, 2 * P:3 * P], SG2[0:32, chunk(c)], start=False, stop=True).then_inc(S("z_psum"), 1)
                e.wait_ge(S("kksq_ready"), 1)
                e.sem_inc(S("kksq_ready"), -1)
                for c in range(CH):
                    claim(c)
                    e.matmul(bank(c, 0, CW), cst(C_BD), TMP[:, 0, chunk(c)], start=True, stop=True).then_inc(S("kk_psum"), 1)
                e.wait_ge(S("rk_ready"), 1)
                e.sem_inc(S("rk_ready"), -1)
                for c in range(CH):
                    claim(3 + c)
                    e.matmul(bank(3 + c, 0, CW), cst(C_BD), TMP[:, 1, chunk(c)], start=True, stop=True).then_inc(S("rk_psum"), 1)
                e.wait_ge(S("til_ready"), 1)
                e.sem_inc(S("til_ready"), -1)
                claim(5, 6)
                for u in range(UNITS + 1):
                    _, _, tiles, levels = unit(u)
                    by_token(u)
                    if u > 0:
                        chunk_u(u - 1, 0)
                    scores(u, 0)
                    if u > 0:
                        chunk_state(u - 1, 0)
                    if tiles == 2:
                        scores(u, 1)
                    low(u)
                    value_parts(u)
                    for s in range(levels):
                        level_left(u, s)
                        if u > 0 and s < 3:
                            chunk_u(u - 1, s + 1)
                        level_right(u, s)
                        if u > 0 and s < 3:
                            chunk_state(u - 1, s + 1)
                    if u > 0:
                        outputs(u - 1)
                    solved(u)

                def state_out():
                    e.wait_ge(S("state_ready"), 1)
                    e.sem_inc(S("state_ready"), -1)
                    transposes([(SBD, 0)], 0, "sio_psum")

                state_out()
                e.wait_ge(S("state_in"), 1)
                e.sem_inc(S("state_in"), -1)
                transposes([(SAMPLE_IN, 0)], 1, "sin_psum")
                chunk_u(UNITS, 0)
                chunk_state(UNITS, 0)
                outputs(UNITS)
                state_out()
                give(e, "bank5", "bank6")
                e.wait_ge(S("yy_ready"), 1)
                e.sem_inc(S("yy_ready"), -1)
                for c in range(CH):
                    claim(c)
                    e.matmul(bank(c, 0, CW), cst(C_CEN), YY[:, chunk(c)], start=True, stop=True).then_inc(S("yc_psum"), 1)
                e.wait_ge(S("ysq_ready"), 1)
                e.sem_inc(S("ysq_ready"), -1)
                for c in range(CH):
                    claim(3 + c)
                    e.matmul(bank(3 + c, 0, CW), cst(C_BDM), TMP[:, 0, chunk(c)], start=True, stop=True).then_inc(S("var_psum"), 1)
            e.wait_ge(S("shc_full"), 1)
            e.sem_inc(S("shc_full"), -1)
            claim(0)
            for g in range(2):
                ins = e.matmul(PS[g * 64:g * 64 + 16, 0:P], SHC[:, g * 16:(g + 1) * 16], ident, start=True, stop=True)
            ins.then_inc(S("shc_psum"), 1)
            barrier(e, "pe")
            dense_pair()
            with e.Fori(0, 3) as i:
                for s in range(2):
                    dense8(s, 3 * s, "dense_psum")
            stats()
            barrier(e, "pe")
            block_stats()
            dense_pair()
            for s in range(2):
                dense8(s, 3 * s, "dense_psum")

            def mem_keys():
                e.wait_ge(S("ckr_ready"), 1)
                e.sem_inc(S("ckr_ready"), -1)
                for kt in range(2):
                    transposes([(CKR[:, kt, h * P:(h + 1) * P], h * P) for h in range(4)], 6 + kt, "ckt_psum")
                e.wait_ge(S("ckt_ready"), 1)
                e.sem_inc(S("ckt_ready"), -1)

            def cross(n):
                e.wait_ge(S("cq_ready"), 1)
                e.sem_inc(S("cq_ready"), -1)
                claim(0, 1)
                for h in range(4):
                    ins = e.matmul(PS[0:n, h * MEM:(h + 1) * MEM], CQ[:, h, 0:n], CKT[:, h, :], start=True, stop=True)
                ins.then_inc(S("cs_psum"), 1)
                e.wait_ge(S("cp_ready"), 1)
                e.sem_inc(S("cp_ready"), -1)
                for g in range(2):
                    transposes([(CP[0:n, 2 * g + hh, kt * P:(kt + 1) * P], (hh * 2 + kt) * P) for hh in range(2) for kt in range(2)], 2 + g, "cpt_psum")
                e.wait_ge(S("cpt_ready"), 1)
                e.sem_inc(S("cpt_ready"), -1)
                claim(4)
                for h in range(4):
                    for kt in range(2):
                        ins = e.matmul(PS[:, 2048 + h * n:2048 + (h + 1) * n], CV[:, kt, h * P:(h + 1) * P], CPT[:, h, kt, 0:n],
                                       start=(kt == 0), stop=(kt == 1))
                ins.then_inc(S("co_psum"), 1)

            mem_keys()
            with e.Fori(0, TILES) as t:
                cross(P)
            mem_keys()
            cross(DEC_SEQ)
            e.wait_ge(S("ch_ready"), 1)
            e.sem_inc(S("ch_ready"), -1)
            with e.Fori(0, 2) as i:
                for s in range(2):
                    e.wait_ge(S(f"w_ready{s}"), 1)
                    e.sem_inc(S(f"w_ready{s}"), -1)
                    W = [x[:, s, :].rearrange("p (k n) -> p k n", k=4) for x in (WH, WL)]
                    for o in range(2):
                        for c in range(CH):
                            claim(3 * o + c)
                            products(bank(3 * o + c, 0, CW), lambda k, p: W[p][:, k, o * P:(o + 1) * P],
                                     lambda k, p: (HH, HL)[p][:, k, chunk(c)], s, 4).then_inc(S("dense_psum"), 1)
            stats()
            barrier(e, "pe")
            block_stats()

            def gate_up():
                dense8(0, 0, "gate_psum")
                dense8(1, 3, "up_psum")

            def down():
                for c in range(CH):
                    e.wait_ge(S("g_ready"), 1)
                    e.sem_inc(S("g_ready"), -1)
                    for k in range(2):
                        if c == 0:
                            e.wait_ge(S(f"w_ready{k}"), 1)
                            e.sem_inc(S(f"w_ready{k}"), -1)
                        for m in range(DB):
                            b = DOWN_BANKS[m]
                            if k == 0:
                                claim(b)
                            for w, g in ((WH, GH), (WL, GH), (WH, GL)):
                                ins = e.matmul(bank(b, 0, CW), w[:, k, m * P:(m + 1) * P], g[:, k, chunk(c)],
                                               start=(k == 0 and w is WH and g is GH), stop=(k == 1 and g is GL))
                            if k == 1:
                                ins.then_inc(S("down_psum"), 1)
                            elif m == DB - 1 and c == CH - 1:
                                ins.then_inc(S("w0_used"), 1)

            dense_pair(("gate_psum", "up_psum"))
            gate_up()
            down()
            with e.Fori(1, FB // 2) as i:
                for f in range(2):
                    gate_up()
                down()
            stats()
            barrier(e, "pe")

        def tokens_out(n):
            e.wait_ge(S("xo_ready"), 1)
            e.sem_inc(S("xo_ready"), -1)
            for g in range(2):
                transposes([(R2[:, 0, 0:1024].rearrange("p (b t) -> p b t", b=8)[:, 4 * g + b, 0:n], b * P) for b in range(4)], g, "xo_psum")

        with e.Fori(0, TILES) as j:
            tokens_out(P)
        tokens_out(DEC_SEQ)

    @block.scalar
    def _(e):
        def copy(dst, src):
            return e.copy(dst, src)

        def split(slot):
            e.wait_ge(S(f"w_full{slot}"), 16)
            e.sem_inc(S(f"w_full{slot}"), -16)
            copy(WH[:, slot, :], WRAW[:, slot, :]).then_inc(S(f"wh_ready{slot}"), 1)

        def evac(slot, dst, m=P, cw=CW, ch=CH, name="dense_psum", b0=None, then=True):
            b0 = 3 * slot if b0 is None else b0
            for c in range(ch):
                e.wait_ge(S(name), 1)
                e.sem_inc(S(name), -1)
                for out, a, z in dst(c):
                    ins = copy(out, PS[0:m, (b0 + c) * 512 + a:(b0 + c) * 512 + z])
                ins.then_inc(S("act_done"), 1)
                e.wait_ge(S("act_done"), 1)
                e.sem_inc(S("act_done"), -1)
                give(e, f"bank{b0 + c}")
            if then:
                split(slot)

        def inverse_root(dst, b0, eps, n=T):
            cw = CW if n == T else n
            for c in range(n // cw):
                e.wait_ge(S("var_psum"), 1)
                e.sem_inc(S("var_psum"), -1)
                e.activation(dst[:, c * cw:(c + 1) * cw], bank(b0 + c, 0, cw), ACT.Ln, bias=CST[:, eps:eps + 1]).then_inc(S("act_done"), 1)
                e.wait_ge(S("act_done"), 1)
                e.sem_inc(S("act_done"), -1)
                give(e, f"bank{b0 + c}")
            e.activation(dst[:, 0:n], dst[:, 0:n], ACT.Exp, scale=-0.5).then_inc(S("rms_ready"), 1)

        def square(src, s, n=T):
            e.wait_ge(S("sq_free"), 1)
            e.sem_inc(S("sq_free"), -1)
            e.activation(TMP[:, s, 0:n], src, ACT.Square).then_inc(S("sq_ready"), 1)

        def squares(src, n=T):
            for b in range(DB):
                square(src[:, b, 0:n], b % 2, n)
            root_means(n)

        def root_means(n=T):
            inverse_root(TMP[:, 0, :], 0, C_EPS, n)

        def block_squares():
            for b in range(DB):
                e.wait_ge(S("r1_ready"), 1)
                e.sem_inc(S("r1_ready"), -1)
                e.activation(R2[:, b, :], R1[:, b, :], ACT.Square).then_inc(S("r1sq_ready"), 1)
            root_means()

        def highs(src, n=T):
            for b in range(DB):
                e.wait_ge(S("ht_ready"), 1)
                e.sem_inc(S("ht_ready"), -1)
                copy(HH[:, b, 0:n], src(b)[:, 0:n]).then_inc(S("hh_ready"), 1)

        in_tmp = lambda b: TMP[:, 1 + b % 2, :]
        in_r2 = lambda b: R2[:, b, :]

        e.wait_ge(S("cst_act"), 1)
        e.sem_inc(S("cst_act"), -1)
        for b in range(8):
            give(e, f"bank{b}")

        def tokens_in(n, dst):
            e.wait_ge(S("xT_psum"), 1)
            e.sem_inc(S("xT_psum"), -1)
            ins = copy(dst, PS[:, 0:512].rearrange("p (b t) -> p b t", b=4)[:, :, 0:n])
            ins.then_inc(S("act_done"), 1)
            e.wait_ge(S("act_done"), 1)
            e.sem_inc(S("act_done"), -1)
            give(e, "bank0", "xin_act")

        give(e, "sq_free", "sq_free", "ot_free", "elt_free", "elt_free")
        with e.Fori(0, MEM // P) as j:
            tokens_in(P, R1[:, 0:4, bass.ds(j * P, P)])
        e.wait_ge(S("memT_saved_act"), 1)
        e.sem_inc(S("memT_saved_act"), -1)
        with e.Fori(0, TILES) as j:
            tokens_in(P, R1[:, 0:4, bass.ds(j * P, P)])
        tokens_in(DEC_SEQ, R1[:, 0:4, SEQ:T])
        barrier(e, "act")
        split(0)
        split(1)
        with e.Fori(0, DEPTH) as l:
            e.wait_ge(S("prm_psum"), 1)
            e.sem_inc(S("prm_psum"), -1)
            ins = copy(PRM[:, :], PS[:, 3584:3584 + PRM_ROWS])
            ins.then_inc(S("act_done"), 1)
            e.wait_ge(S("act_done"), 1)
            e.sem_inc(S("act_done"), -1)
            give(e, "bank7", "prm_ready")
            e.wait_ge(S("memT_act"), 1)
            e.sem_inc(S("memT_act"), -1)
            squares(R2, MEM)
            highs(in_tmp, MEM)
            with e.Fori(0, 4) as i:
                for s in range(2):
                    evac(s, lambda c: [(R2[:, bass.ds(i * 2 + s, 1), MEM:2 * MEM].rearrange("p a m -> p (a m)"), 0, MEM)], cw=MEM, ch=1)
            give(e, "kvT_ready")
            for k in range(4):
                e.wait_ge(S("memtok_psum"), 1)
                e.sem_inc(S("memtok_psum"), -1)
                ins = copy(R2[:, 2 + k, 512:1024], bank(k))
                ins.then_inc(S("act_done"), 1)
                e.wait_ge(S("act_done"), 1)
                e.sem_inc(S("act_done"), -1)
                give(e, f"bank{k}", "memtok_ready")
            squares(R1)
            barrier(e, "act")
            highs(in_tmp)
            with e.Fori(0, 2) as i:
                for s in range(2):
                    evac(s, lambda c: [(R1[:, bass.ds(i * 2 + s, 1), chunk(c)].rearrange("p a t -> p (a t)"), 0, CW)])
            for s in range(2):
                evac(s, lambda c: [(R1[:, 4 + s, chunk(c)], 0, CW)])
            evac(0, lambda c: [(R1[:, 6, chunk(c)], 0, CW)])

            def raw(m=P):
                def dst(c):
                    if c < CH - 1:
                        return [(PRAW[0:m, 1 + c * CW:1 + (c + 1) * CW], 0, CW)]
                    w = SEQ - c * CW
                    return [(PRAW[0:m, 1 + c * CW:1 + SEQ], 0, w), (PRAW[0:m, SEQ + 2:T + 2], w, CW)]
                return dst

            for n, (s, m) in enumerate(((1, P), (0, P), (1, 32))):
                e.wait_ge(S("praw_free"), 1)
                e.sem_inc(S("praw_free"), -1)
                evac(s, raw(m), m=m)
                give(e, "praw_ready")
            e.wait_ge(S("lora_ready"), 1)
            e.sem_inc(S("lora_ready"), -1)
            e.activation(TWA[0:64, :], TWA[0:64, :], ACT.Tanh).then_inc(S("act_done"), 1)
            e.wait_ge(S("act_done"), 1)
            e.sem_inc(S("act_done"), -1)
            e.activation(SG1, SG1, ACT.Sigmoid).then_inc(S("act_done"), 1)
            e.wait_ge(S("act_done"), 1)
            e.sem_inc(S("act_done"), -1)
            e.activation(SG2[0:32, :], SG2[0:32, :], ACT.Sigmoid).then_inc(S("act_done"), 1)
            e.wait_ge(S("act_done"), 1)
            e.sem_inc(S("act_done"), -1)

            def att(i, n, slot, width, kts):
                copy(VST[:, 0:n], R1[:, 6, bass.ds(i, n)]).then_inc(S("vst_ready"), 1)
                e.wait_ge(S("v_psum"), 1)
                e.sem_inc(S("v_psum"), -1)
                copy(VT[0:n, slot, :], PS[0:n, 3072:3072 + P]).then_inc(S("act_done"), 1)
                e.wait_ge(S("act_done"), 1)
                e.sem_inc(S("act_done"), -1)
                give(e, "bank6")
                e.wait_ge(S("nm_ready"), 1)
                e.sem_inc(S("nm_ready"), -1)
                for hs in range(8):
                    ins = e.activation(SC[0:n, hs, 0:width], SC[0:n, hs, 0:width], ACT.Exp, bias=ST[0:n, 16 + hs:17 + hs], scale=1.0,
                                       accum_out=ST[0:n, 24 + hs:25 + hs])
                e.activation(ST[0:n, 32:40], ST[0:n, 32:40], ACT.Exp).then_inc(S("exp_ready"), 1)
                for g in range(4):
                    b = (0, 1, 6, 7)[g]
                    e.wait_ge(S("pT_psum"), 1)
                    e.sem_inc(S("pT_psum"), -1)
                    for kt, nk in enumerate(kts):
                        src = bank(b).rearrange("p (h k q) -> p h k q", h=2, k=2)
                        ins = copy(PT[0:nk, 2 * g:2 * g + 2, kt, 0:n], src[0:nk, :, kt, 0:n])
                    ins.then_inc(S("act_done"), 1)
                    e.wait_ge(S("act_done"), 1)
                    e.sem_inc(S("act_done"), -1)
                    give(e, f"bank{b}")
                give(e, "pT_ready")
                e.wait_ge(S("ot_free"), 1)
                e.sem_inc(S("ot_free"), -1)
                e.wait_ge(S("o_psum"), 1)
                e.sem_inc(S("o_psum"), -1)
                copy(OT[:, :, 0:n], PS[:, 1024:1024 + 4 * n].rearrange("p (a t) -> p a t", a=4)).then_inc(S("act_done"), 1)
                e.wait_ge(S("act_done"), 1)
                e.sem_inc(S("act_done"), -1)
                give(e, "bank2", "ot_ready")

            def keys_out(n):
                e.wait_ge(S("ko_psum"), 1)
                e.sem_inc(S("ko_psum"), -1)
                copy(KO[0:n, :], PS[0:n, 0:P]).then_inc(S("act_done"), 1)
                e.wait_ge(S("act_done"), 1)
                e.sem_inc(S("act_done"), -1)
                give(e, "bank0", "ko_ready")

            with e.Fori(0, TILES // 2) as i:
                for s in range(2):
                    att((i * 2 + s) * P, P, s, 256, (P, P))
            keys_out(P)
            give(e, "vt_free", "kcr_free")
            for v in range(2):
                e.wait_ge(S("kc_psum"), 1)
                e.sem_inc(S("kc_psum"), -1)
                copy(KR[:, v, 1, :], PS[:, v * 512:v * 512 + P]).then_inc(S("act_done"), 1)
                e.wait_ge(S("act_done"), 1)
                e.sem_inc(S("act_done"), -1)
                give(e, f"bank{v}")
                if v == 0:
                    give(e, "kcr_free")
            give(e, "kc_ready")
            att(SEQ, DEC_SEQ, 0, DEC_SEQ + P, (DEC_SEQ, P))
            keys_out(DEC_SEQ)
            barrier(e, "act")

            def by_token(u):
                _, n, tiles, _ = unit(u)
                for x in range(tiles):
                    e.wait_ge(S("tm_psum"), 1)
                    e.sem_inc(S("tm_psum"), -1)
                    copy(ATM[0:n, x, :], PS[0:n, x * 512:x * 512 + P])
                    copy(bkv(u)[0:n, x, :, :], PS[0:n, x * 512 + P:(x + 1) * 512].rearrange("p (a t) -> p a t", a=3)).then_inc(S("act_done"), 1)
                    e.wait_ge(S("act_done"), 1)
                    e.sem_inc(S("act_done"), -1)
                    give(e, f"bank{x}")
                give(e, "tm_ready")
                e.wait_ge(S("mv_psum"), 1)
                e.sem_inc(S("mv_psum"), -1)
                copy(MVS[0:n, 0:tiles, :], PS[0:n, 1536:1536 + tiles * P].rearrange("p (x t) -> p x t", x=tiles)).then_inc(S("act_done"), 1)
                e.wait_ge(S("act_done"), 1)
                e.sem_inc(S("act_done"), -1)
                give(e, "bank3", "mv_ready")

            def levels_left(u):
                _, n, tiles, levels = unit(u)
                for s in range(levels):
                    for x in range(tiles):
                        e.wait_ge(S("t1_psum"), 1)
                        e.sem_inc(S("t1_psum"), -1)
                        if x == tiles - 1:
                            give(e, "elt_free")
                        w = slice(2 * x * n, 2 * (x + 1) * n)
                        copy(T1F[0:n, w], PS[0:n, (2 + x) * 512:(2 + x) * 512 + 2 * n]).then_inc(S("t1_ready"), 1)

            def solved(u):
                _, n, tiles, _ = unit(u)
                e.wait_ge(S("pts_psum"), 1)
                e.sem_inc(S("pts_psum"), -1)
                copy(PTS[:, 0:tiles, 0:n], PS[:, 1024:1024 + tiles * n].rearrange("p (x t) -> p x t", x=tiles)).then_inc(S("act_done"), 1)
                e.wait_ge(S("act_done"), 1)
                e.sem_inc(S("act_done"), -1)
                give(e, "bank2")
                e.wait_ge(S("q_psum"), 1)
                e.sem_inc(S("q_psum"), -1)
                copy(QS[0:n, 0:tiles, :], PS[0:n, 1536:1536 + tiles * P].rearrange("p (x t) -> p x t", x=tiles)).then_inc(S("act_done"), 1)
                e.wait_ge(S("act_done"), 1)
                e.sem_inc(S("act_done"), -1)
                give(e, "bank3", "pq_ready", "q_ready")

            def outputs(u):
                t0, n, tiles, _ = unit(u)
                yb = (4, 7)[u % 2]
                e.wait_ge(S("y_psum"), 1)
                e.sem_inc(S("y_psum"), -1)
                copy(YY[:, t0:t0 + tiles * n], PS[:, yb * 512:yb * 512 + tiles * n]).then_inc(S("act_done"), 1)
                e.wait_ge(S("act_done"), 1)
                e.sem_inc(S("act_done"), -1)
                give(e, f"bank{yb}")

            with e.Fori(0, PAIRS) as j:
                for b, s in enumerate((0, 1, 0)):
                    e.wait_ge(S("praw_free"), 1)
                    e.sem_inc(S("praw_free"), -1)
                    evac(s, raw())
                    give(e, "praw_ready")
                e.wait_ge(S("pc_ready"), 1)
                e.sem_inc(S("pc_ready"), -1)
                for c in range(CH):
                    e.wait_ge(S("z_psum"), 1)
                    e.sem_inc(S("z_psum"), -1)
                    e.activation(DD2[:, chunk(c)], bank(3 + c, 0, CW), ACT.Sigmoid, bias=PC[:, 3:4]).then_inc(S("act_done"), 1)
                    e.wait_ge(S("act_done"), 1)
                    e.sem_inc(S("act_done"), -1)
                    give(e, f"bank{3 + c}")
                for c in range(CH):
                    e.wait_ge(S("z_psum"), 1)
                    e.sem_inc(S("z_psum"), -1)
                    e.activation(BB[:, chunk(c)], bank(c, 0, CW), ACT.Sigmoid, bias=PC[:, 4:5]).then_inc(S("act_done"), 1)
                    e.wait_ge(S("act_done"), 1)
                    e.sem_inc(S("act_done"), -1)
                    give(e, f"bank{c}")
                for c in range(CH):
                    e.wait_ge(S("z_psum"), 1)
                    e.sem_inc(S("z_psum"), -1)
                    copy(GG[:, chunk(c)], bank(3 + c, 0, CW)).then_inc(S("act_done"), 1)
                    e.wait_ge(S("act_done"), 1)
                    e.sem_inc(S("act_done"), -1)
                    give(e, f"bank{3 + c}")
                split(1)
                give(e, "sig_ready")
                e.wait_ge(S("kkr_ready"), 1)
                e.sem_inc(S("kkr_ready"), -1)
                e.activation(TMP[:, 0, :], KK, ACT.Square).then_inc(S("kksq_ready"), 1)
                e.wait_ge(S("kkn_ready"), 1)
                e.sem_inc(S("kkn_ready"), -1)
                e.activation(TMP[:, 2, :], TMP[:, 2, :], ACT.Ln).then_inc(S("act_done"), 1)
                e.wait_ge(S("act_done"), 1)
                e.sem_inc(S("act_done"), -1)
                e.activation(TMP[:, 2, :], TMP[:, 2, :], ACT.Exp, scale=-0.5).then_inc(S("kks_ready"), 1)
                e.wait_ge(S("dd_ready"), 1)
                e.sem_inc(S("dd_ready"), -1)
                e.activation(TMP[:, 0, :], DD, ACT.Exp, scale=-DECAY)
                e.activation(TMP[:, 1, :], DD2, ACT.Exp, scale=-DECAY)
                e.activation(TMP[:, 2, :], DD, ACT.Exp, scale=DECAY)
                e.activation(EC[:, 20:38], EC[:, 0:18], ACT.Exp, scale=-DECAY).then_inc(S("e_ready"), 1)
                for u in range(UNITS + 1):
                    by_token(u)
                    levels_left(u)
                    if u > 0:
                        outputs(u - 1)
                    solved(u)

                def state_out(dst):
                    e.wait_ge(S("sio_psum"), 1)
                    e.sem_inc(S("sio_psum"), -1)
                    copy(dst, PS[:, 0:P]).then_inc(S("act_done"), 1)
                    e.wait_ge(S("act_done"), 1)
                    e.sem_inc(S("act_done"), -1)
                    give(e, "bank0", "state_out")

                state_out(SIO)
                outputs(UNITS)
                state_out(SAMPLE_OUT)
                give(e, "yy_ready")
                for c in range(CH):
                    e.wait_ge(S("yc_psum"), 1)
                    e.sem_inc(S("yc_psum"), -1)
                    copy(TMP[:, 1, chunk(c)], bank(c, 0, CW)).then_inc(S("act_done"), 1)
                    e.wait_ge(S("act_done"), 1)
                    e.sem_inc(S("act_done"), -1)
                    give(e, f"bank{c}")
                e.activation(TMP[:, 0, :], TMP[:, 1, :], ACT.Square).then_inc(S("act_done"), 1)
                e.wait_ge(S("act_done"), 1)
                e.sem_inc(S("act_done"), -1)
                give(e, "ysq_ready")
                inverse_root(TMP[:, 2, :], 3, C_EPS + 1)
            e.wait_ge(S("shc_psum"), 1)
            e.sem_inc(S("shc_psum"), -1)
            for g in range(2):
                ins = copy(AUX[g * 64:g * 64 + 16, 256:384], PS[g * 64:g * 64 + 16, 0:P])
            ins.then_inc(S("act_done"), 1)
            e.wait_ge(S("act_done"), 1)
            e.sem_inc(S("act_done"), -1)
            give(e, "bank0", "shc_ready")
            barrier(e, "act")
            e.wait_ge(S("mix_act"), 1)
            e.sem_inc(S("mix_act"), -1)
            for b in range(DB):
                copy(HH[:, b, :], R2[:, b, :]).then_inc(S("hh_ready"), 1)
            e.wait_ge(S("r2_free"), 1)
            e.sem_inc(S("r2_free"), -1)

            def out8():
                with e.Fori(0, 4) as i:
                    for s in range(2):
                        evac(s, lambda c: [(R2[:, bass.ds(i * 2 + s, 1), chunk(c)].rearrange("p a t -> p (a t)"), 0, CW)])
                        square(R2[:, bass.ds(i * 2 + s, 1), :].rearrange("p a t -> p (a t)"), s)

            out8()
            root_means()
            barrier(e, "act")
            block_squares()
            highs(in_r2)
            with e.Fori(0, 2) as i:
                for s in range(2):
                    evac(s, lambda c: [(R2[:, bass.ds(i * 2 + s, 1), chunk(c)].rearrange("p a t -> p (a t)"), 0, CW)])

            def mem_keys():
                for kt in range(2):
                    e.wait_ge(S("ckt_psum"), 1)
                    e.sem_inc(S("ckt_psum"), -1)
                    copy(CKT[:, :, kt * P:(kt + 1) * P], bank(6 + kt).rearrange("p (h k) -> p h k", h=4)).then_inc(S("act_done"), 1)
                    e.wait_ge(S("act_done"), 1)
                    e.sem_inc(S("act_done"), -1)
                    give(e, f"bank{6 + kt}")
                give(e, "ckt_ready")

            def cross(i, n):
                copy(CQ[:, :, 0:n], R2[:, 0:4, bass.ds(i, n)]).then_inc(S("cq_ready"), 1)
                e.wait_ge(S("cnm_ready"), 1)
                e.sem_inc(S("cnm_ready"), -1)
                for h in range(4):
                    ins = e.activation(CP[0:n, h, :], PS[0:n, h * MEM:(h + 1) * MEM], ACT.Exp, bias=ST[0:n, 4 + h:5 + h], scale=float(P) ** -0.5,
                                       accum_out=ST[0:n, 8 + h:9 + h])
                ins.then_inc(S("act_done"), 1)
                e.wait_ge(S("act_done"), 1)
                e.sem_inc(S("act_done"), -1)
                give(e, "bank0", "bank1", "cexp_ready")
                for g in range(2):
                    e.wait_ge(S("cpt_psum"), 1)
                    e.sem_inc(S("cpt_psum"), -1)
                    copy(CPT[:, 2 * g:2 * g + 2, :, 0:n], bank(2 + g).rearrange("p (h k q) -> p h k q", h=2, k=2)[:, :, :, 0:n]).then_inc(S("act_done"), 1)
                    e.wait_ge(S("act_done"), 1)
                    e.sem_inc(S("act_done"), -1)
                    give(e, f"bank{2 + g}")
                give(e, "cpt_ready")
                e.wait_ge(S("co_psum"), 1)
                e.sem_inc(S("co_psum"), -1)
                copy(HH[:, 0:4, bass.ds(i, n)], PS[:, 2048:2048 + 4 * n].rearrange("p (h q) -> p h q", h=4)).then_inc(S("coh_ready"), 1)

            mem_keys()
            with e.Fori(0, TILES) as t:
                cross(t * P, P)
            mem_keys()
            cross(SEQ, DEC_SEQ)
            with e.Fori(0, 2) as i:
                for s in range(2):
                    for o in range(2):
                        evac(s, lambda c: [(R2[:, bass.ds((i * 2 + s) * 2 + o, 1), chunk(c)].rearrange("p a t -> p (a t)"), 0, CW)],
                             b0=3 * o, then=(o == 1))
                        square(R2[:, bass.ds((i * 2 + s) * 2 + o, 1), :].rearrange("p a t -> p (a t)"), o)
            root_means()
            barrier(e, "act")
            block_squares()
            highs(in_r2)

            def group():
                for f in range(2):
                    for c in range(CH):
                        e.wait_ge(S("gate_psum"), 1)
                        e.sem_inc(S("gate_psum"), -1)
                        e.wait_ge(S("silu_free"), 1)
                        e.sem_inc(S("silu_free"), -1)
                        e.activation(TMP[:, 0, chunk(c)], bank(c, 0, CW), ACT.Silu).then_inc(S("act_done"), 1)
                        e.wait_ge(S("act_done"), 1)
                        e.sem_inc(S("act_done"), -1)
                        give(e, f"bank{c}", "silu_ready")
                    split(0)
                    for c in range(CH):
                        if c == CH - 1:
                            e.wait_ge(S("w1_used"), 1)
                            e.sem_inc(S("w1_used"), -1)
                            split(1)
                        e.wait_ge(S("gu_ready"), 1)
                        e.sem_inc(S("gu_ready"), -1)
                        copy(GH[:, f, chunk(c)], TMP[:, 1, chunk(c)]).then_inc(S("gh_ready"), 1)
                e.wait_ge(S("w0_used"), 1)
                e.sem_inc(S("w0_used"), -1)
                split(0)
                e.wait_ge(S("w1_used"), 1)
                e.sem_inc(S("w1_used"), -1)
                split(1)

            with e.Fori(0, FB // 2) as i:
                group()
            e.wait_ge(S("r2_ready"), 1)
            e.sem_inc(S("r2_ready"), -1)
            squares(R2)
            barrier(e, "act")

        def tokens_out(i, n):
            e.wait_ge(S("xo_free"), 1)
            e.sem_inc(S("xo_free"), -1)
            copy(R2[:, 0, 0:1024].rearrange("p (b t) -> p b t", b=8)[:, :, 0:n], R1[:, :, bass.ds(i, n)]).then_inc(S("xo_ready"), 1)
            e.wait_ge(S("xout_free"), 1)
            e.sem_inc(S("xout_free"), -1)
            for g in range(2):
                e.wait_ge(S("xo_psum"), 1)
                e.sem_inc(S("xo_psum"), -1)
                copy(R2[0:n, 4, g * 512:(g + 1) * 512], PS[0:n, g * 512:(g + 1) * 512]).then_inc(S("act_done"), 1)
                e.wait_ge(S("act_done"), 1)
                e.sem_inc(S("act_done"), -1)
                give(e, f"bank{g}")
            give(e, "xout_ready", "xo_free")

        give(e, "xo_free", "xout_free")
        with e.Fori(0, TILES) as j:
            tokens_out(j * P, P)
        tokens_out(SEQ, DEC_SEQ)

    @block.vector
    def _(e):
        def lo(slot):
            e.wait_ge(S(f"wh_ready{slot}"), 1)
            e.sem_inc(S(f"wh_ready{slot}"), -1)
            e.tensor_tensor(WL[:, slot, :], WRAW[:, slot, :], WH[:, slot, :].bitcast(F32), ALU.subtract).then_inc(S("dve_done"), 1)
            e.wait_ge(S("dve_done"), 1)
            e.sem_inc(S("dve_done"), -1)
            give(e, f"w_ready{slot}", f"w_free{slot}")

        def los(n):
            with e.Fori(0, n) as i:
                lo(0)
                lo(1)

        def add_square(s, n=T):
            e.wait_ge(S("sq_ready"), 1)
            e.sem_inc(S("sq_ready"), -1)
            e.tensor_tensor(TMP[:, 2, 0:n], TMP[:, 2, 0:n], TMP[:, s, 0:n], ALU.add).then_inc(S("dve_done"), 1)
            e.wait_ge(S("dve_done"), 1)
            e.sem_inc(S("dve_done"), -1)
            give(e, "sq_free")

        def sum_squares(n=T):
            e.memset(TMP[:, 2, 0:n], 0.0).then_inc(S("dve_done"), 1)
            e.wait_ge(S("dve_done"), 1)
            e.sem_inc(S("dve_done"), -1)
            for b in range(DB):
                add_square(b % 2, n)
            give(e, "sq_sum")
            e.wait_ge(S("rms_ready"), 1)
            e.sem_inc(S("rms_ready"), -1)

        def scaled(dst, src, gain, n=T):
            return e.scalar_tensor_tensor(out=dst, in0=src, scalar=PRM[:, gain:gain + 1], in1=TMP[:, 0, 0:n], op0=ALU.mult, op1=ALU.mult)

        in_tmp = lambda b: TMP[:, 1 + b % 2, :]
        in_r2 = lambda b: R2[:, b, :]

        def normed(src, which, t, n=T):
            g = G_AT + which * DB
            scaled(t(0)[:, 0:n], src[:, 0, 0:n], g, n).then_inc(S("ht_ready"), 1)
            for b in range(DB):
                if b < DB - 1:
                    scaled(t(b + 1)[:, 0:n], src[:, b + 1, 0:n], g + b + 1, n).then_inc(S("ht_ready"), 1)
                e.wait_ge(S("hh_ready"), 1)
                e.sem_inc(S("hh_ready"), -1)
                e.tensor_tensor(HL[:, b, 0:n], t(b)[:, 0:n], HH[:, b, 0:n].bitcast(F32), ALU.subtract).then_inc(S("dve_done"), 1)
                e.wait_ge(S("dve_done"), 1)
                e.sem_inc(S("dve_done"), -1)
                give(e, "h_ready")

        def add_normed(which, then=True):
            for b in range(DB):
                scaled(R2[:, b, :], R2[:, b, :], G_AT + which * DB + b).then_inc(S("dve_done"), 1)
                e.wait_ge(S("dve_done"), 1)
                e.sem_inc(S("dve_done"), -1)
                e.tensor_tensor(R1[:, b, :], R1[:, b, :], R2[:, b, :], ALU.add).then_inc(S("dve_done"), 1)
                e.wait_ge(S("dve_done"), 1)
                e.sem_inc(S("dve_done"), -1)
                if then:
                    give(e, "r1_ready")

        def add_and_norm(post, pre):
            add_normed(post)
            e.wait_ge(S("rms_ready"), 1)
            e.sem_inc(S("rms_ready"), -1)
            normed(R1, pre, in_r2)

        e.wait_ge(S("cst_dve"), 1)
        e.sem_inc(S("cst_dve"), -1)
        give(e, "xin_free", "w_free0", "w_free1", "praw_free")
        e.memset(SHC, 0.0).then_inc(S("dve_done"), 1)
        e.wait_ge(S("dve_done"), 1)
        e.sem_inc(S("dve_done"), -1)

        def tokens_in(n, dst):
            e.wait_ge(S("xT_dve_psum"), 1)
            e.sem_inc(S("xT_dve_psum"), -1)
            e.tensor_copy(dst, PS[:, 512:1024].rearrange("p (b t) -> p b t", b=4)[:, :, 0:n]).then_inc(S("dve_done"), 1)
            e.wait_ge(S("dve_done"), 1)
            e.sem_inc(S("dve_done"), -1)
            give(e, "bank1")
            e.wait_ge(S("xin_act"), 1)
            e.sem_inc(S("xin_act"), -1)
            give(e, "xin_free")

        with e.Fori(0, MEM // P) as j:
            tokens_in(P, R1[:, 4:8, bass.ds(j * P, P)])
        give(e, "memT_ready")
        e.wait_ge(S("memT_saved_dve"), 1)
        e.sem_inc(S("memT_saved_dve"), -1)
        with e.Fori(0, TILES) as j:
            tokens_in(P, R1[:, 4:8, bass.ds(j * P, P)])
        tokens_in(DEC_SEQ, R1[:, 4:8, SEQ:T])
        barrier(e, "dve")
        lo(0)
        lo(1)
        with e.Fori(0, DEPTH) as l:
            e.memset(TMP[:, 0, 0:P], 0.0).then_inc(S("dve_done"), 1)
            e.wait_ge(S("dve_done"), 1)
            e.sem_inc(S("dve_done"), -1)
            give(e, "prow_clear")
            e.wait_ge(S("prm_rows"), 1)
            e.sem_inc(S("prm_rows"), -1)
            give(e, "prm_rows_pe")
            e.wait_ge(S("prm_ready"), 1)
            e.sem_inc(S("prm_ready"), -1)
            e.wait_ge(S("memT_dve"), 1)
            e.sem_inc(S("memT_dve"), -1)
            sum_squares(MEM)
            normed(R2, N_MEM, in_tmp, MEM)
            los(4)
            sum_squares()
            barrier(e, "dve")
            normed(R1, MIX_PRE, in_tmp)
            los(3)
            lo(0)

            def shifted(dst, mu, sh, m=P):
                e.memset(PRAW[0:m, 0:1], 0.0).then_inc(S("dve_done"), 1)
                e.wait_ge(S("dve_done"), 1)
                e.sem_inc(S("dve_done"), -1)
                e.tensor_copy(PRAW[0:m, SEQ + 1:SEQ + 2], sh).then_inc(S("dve_done"), 1)
                e.wait_ge(S("dve_done"), 1)
                e.sem_inc(S("dve_done"), -1)
                e.wait_ge(S("praw_ready"), 1)
                e.sem_inc(S("praw_ready"), -1)
                e.tensor_tensor(dst[:, 0:SEQ], PRAW[0:m, 0:SEQ], PRAW[0:m, 1:SEQ + 1], ALU.subtract).then_inc(S("dve_done"), 1)
                e.wait_ge(S("dve_done"), 1)
                e.sem_inc(S("dve_done"), -1)
                e.tensor_tensor(dst[:, SEQ:T], PRAW[0:m, SEQ + 1:T + 1], PRAW[0:m, SEQ + 2:T + 2], ALU.subtract).then_inc(S("dve_done"), 1)
                e.wait_ge(S("dve_done"), 1)
                e.sem_inc(S("dve_done"), -1)
                e.scalar_tensor_tensor(out=dst[:, 0:SEQ], in0=dst[:, 0:SEQ], scalar=mu, in1=PRAW[0:m, 1:SEQ + 1], op0=ALU.mult, op1=ALU.add).then_inc(S("dve_done"), 1)
                e.wait_ge(S("dve_done"), 1)
                e.sem_inc(S("dve_done"), -1)
                e.scalar_tensor_tensor(out=dst[:, SEQ:T], in0=dst[:, SEQ:T], scalar=mu, in1=PRAW[0:m, SEQ + 2:T + 2], op0=ALU.mult, op1=ALU.add).then_inc(S("dve_done"), 1)
                e.wait_ge(S("dve_done"), 1)
                e.sem_inc(S("dve_done"), -1)

            def kept(at, m=P):
                for g, col in ((0, SEQ), (16, T + 1)):
                    e.tensor_copy(at(g), PRAW[0:m, col:col + 1]).then_inc(S("dve_done"), 1)
                    e.wait_ge(S("dve_done"), 1)
                    e.sem_inc(S("dve_done"), -1)
                give(e, "praw_free")

            for b, (dst, m) in enumerate(((TWA, P), (SG1, P), (SG2[0:32, :], 32))):
                shifted(dst, PRM[0:m, MU_AT + 12 + b:MU_AT + 13 + b], PRM[0:m, SH_AT + 12 + b:SH_AT + 13 + b], m)
                kept(lambda g: SHC[0:m, 12 + b + g:13 + b + g], m)
                lo(1 - b % 2)
            give(e, "lora_ready", "cos_free")
            e.wait_ge(S("cos_ready"), 1)
            e.sem_inc(S("cos_ready"), -1)
            give(e, "cos_pe")
            e.memset(KR[:, :, 1, :], 0.0).then_inc(S("dve_done"), 1)
            e.wait_ge(S("dve_done"), 1)
            e.sem_inc(S("dve_done"), -1)
            e.memset(VT[:, 1, :], 0.0).then_inc(S("dve_done"), 1)
            e.wait_ge(S("dve_done"), 1)
            e.sem_inc(S("dve_done"), -1)

            def att(i, n, slot, width, mask):
                tok = bass.ds(i, n)
                cs, sn = (x[:, tok].unsqueeze(1).broadcast_to([P, 6, n]) for x in (COS, SIN))
                e.tensor_tensor(RT[:, :, 0:n], R1[:, 0:6, tok], cs, ALU.mult).then_inc(S("dve_done"), 1)
                e.wait_ge(S("dve_done"), 1)
                e.sem_inc(S("dve_done"), -1)
                e.wait_ge(S("swap_psum"), 1)
                e.sem_inc(S("swap_psum"), -1)
                e.tensor_tensor(RU[:, 0:4, 0:n], PS[:, 0:4 * n].rearrange("p (a t) -> p a t", a=4), sn[:, 0:4, :], ALU.mult).then_inc(S("dve_done"), 1)
                e.wait_ge(S("dve_done"), 1)
                e.sem_inc(S("dve_done"), -1)
                e.tensor_tensor(RU[:, 4:6, 0:n], PS[:, 512:512 + 2 * n].rearrange("p (a t) -> p a t", a=2), sn[:, 0:2, :], ALU.mult).then_inc(S("dve_done"), 1)
                e.wait_ge(S("dve_done"), 1)
                e.sem_inc(S("dve_done"), -1)
                give(e, "bank0", "bank1")
                e.tensor_tensor(QR[:, :, 0:n], RT[:, 0:4, 0:n], RU[:, 0:4, 0:n], ALU.add).then_inc(S("dve_done"), 1)
                e.wait_ge(S("dve_done"), 1)
                e.sem_inc(S("dve_done"), -1)
                e.tensor_tensor(KR[:, :, slot, 0:n], RT[:, 4:6, 0:n], RU[:, 4:6, 0:n], ALU.add).then_inc(S("dve_done"), 1)
                e.wait_ge(S("dve_done"), 1)
                e.sem_inc(S("dve_done"), -1)
                if mask is None:
                    e.wait_ge(S("kc_ready"), 1)
                    e.sem_inc(S("kc_ready"), -1)
                give(e, "qk_ready")
                s = SC[0:n, :, 0:width]
                for g in range(4):
                    e.wait_ge(S("score_psum"), 1)
                    e.sem_inc(S("score_psum"), -1)
                    src = PS[0:n, 1024 + g * 512:1536 + g * 512].rearrange("p (h k) -> p h k", h=2)[:, :, 0:width]
                    dst = SC[0:n, 2 * g:2 * g + 2, 0:width]
                    if mask is None:
                        e.tensor_scalar(dst, src, HEAD ** -0.5, None, ALU.mult).then_inc(S("dve_done"), 1)
                        e.wait_ge(S("dve_done"), 1)
                        e.sem_inc(S("dve_done"), -1)
                        give(e, f"bank{2 + g}")
                    else:
                        e.scalar_tensor_tensor(out=dst, in0=src, scalar=HEAD ** -0.5, in1=mask.unsqueeze(1).broadcast_to([n, 2, width]),
                                                    op0=ALU.mult, op1=ALU.add).then_inc(S("dve_done"), 1)
                        e.wait_ge(S("dve_done"), 1)
                        e.sem_inc(S("dve_done"), -1)
                        give(e, f"bank{2 + g}")
                e.tensor_reduce(ST[0:n, 0:8], s, AX.X, ALU.max).then_inc(S("dve_done"), 1)
                e.wait_ge(S("dve_done"), 1)
                e.sem_inc(S("dve_done"), -1)
                e.tensor_tensor(ST[0:n, 8:16], ST[0:n, 0:8], ST[0:n, 40:48], ALU.max).then_inc(S("dve_done"), 1)
                e.wait_ge(S("dve_done"), 1)
                e.sem_inc(S("dve_done"), -1)
                e.tensor_scalar(ST[0:n, 16:24], ST[0:n, 8:16], -1.0, None, ALU.mult).then_inc(S("dve_done"), 1)
                e.wait_ge(S("dve_done"), 1)
                e.sem_inc(S("dve_done"), -1)
                e.tensor_tensor(ST[0:n, 32:40], ST[0:n, 40:48], ST[0:n, 8:16], ALU.subtract).then_inc(S("dve_done"), 1)
                e.wait_ge(S("dve_done"), 1)
                e.sem_inc(S("dve_done"), -1)
                give(e, "nm_ready")
                e.wait_ge(S("exp_ready"), 1)
                e.sem_inc(S("exp_ready"), -1)
                e.tensor_tensor(ST[0:n, 0:8], ST[0:n, 24:32], ST[0:n, 32:40], ALU.add).then_inc(S("dve_done"), 1)
                e.wait_ge(S("dve_done"), 1)
                e.sem_inc(S("dve_done"), -1)
                e.reciprocal(ST[0:n, 0:8], ST[0:n, 0:8]).then_inc(S("dve_done"), 1)
                e.wait_ge(S("dve_done"), 1)
                e.sem_inc(S("dve_done"), -1)
                e.tensor_tensor(s, s, ST[0:n, 0:8].unsqueeze(2).broadcast_to([n, 8, width]), ALU.mult).then_inc(S("dve_done"), 1)
                e.wait_ge(S("dve_done"), 1)
                e.sem_inc(S("dve_done"), -1)
                give(e, "prob_ready")

            e.tensor_copy(ST[:, 40:44], SINK[:, 0:8:2]).then_inc(S("dve_done"), 1)
            e.wait_ge(S("dve_done"), 1)
            e.sem_inc(S("dve_done"), -1)
            e.tensor_copy(ST[:, 44:48], SINK[:, 1:8:2]).then_inc(S("dve_done"), 1)
            e.wait_ge(S("dve_done"), 1)
            e.sem_inc(S("dve_done"), -1)
            with e.Fori(0, TILES // 2) as i:
                att((i * 2) * P, P, 0, 256, CST[:, bass.ds(C_AE + i * 256, 256)])
                att((i * 2 + 1) * P, P, 1, 256, CST[:, C_AO:C_AO + 256])
            att(SEQ, DEC_SEQ, 0, DEC_SEQ + P, None)
            barrier(e, "dve")

            def scores(u, x):
                _, n, tiles, _ = unit(u)
                e.wait_ge(S("sm_psum"), 2)
                e.sem_inc(S("sm_psum"), -2)
                src = PS[0:n, 1024 * (1 - x):1024 * (2 - x)].rearrange("p (h c) -> p h c", h=2)
                dst = LTM[0:n, :].rearrange("p (a c) -> p a c", a=3)[:, :, 0:2 * tiles * n].rearrange("p a (g t) -> p g a t", t=n)
                m3 = CST[0:n, C_M3:C_M3 + 3 * P].rearrange("p (a t) -> p a t", a=3)[:, :, 0:n]
                e.tensor_tensor(dst[:, 2 * x:2 * x + 2, :, :], src[:, :, 0:3 * n].rearrange("p h (a t) -> p h a t", a=3),
                                m3.unsqueeze(1).broadcast_to([n, 2, 3, n]), ALU.mult)
                e.tensor_tensor(heads(tflat, 1536 + (u % 2) * 512, n, tiles)[:, 2 * x:2 * x + 2, :], src[:, :, 3 * n:4 * n],
                                     m3[:, 2, :].unsqueeze(1).broadcast_to([n, 2, n]), ALU.mult).then_inc(S("dve_done"), 1)
                e.wait_ge(S("dve_done"), 1)
                e.sem_inc(S("dve_done"), -1)
                give(e, f"bank{2 - 2 * x}", f"bank{3 - 2 * x}")
                if x == tiles - 1:
                    give(e, "lt_ready", "sm_ready")

            def low(u):
                _, n, tiles, _ = unit(u)
                e.wait_ge(S("l_psum"), 2)
                e.sem_inc(S("l_psum"), -2)
                mask = lambda at: CST[0:n, at:at + n].unsqueeze(1).broadcast_to([n, 2 * tiles, n])
                src = PS[0:n, 1024:2048].rearrange("p (h c) -> p h c", h=2)[:, :, 0:tiles * n].rearrange("p h (x t) -> p x h t", x=tiles)
                dst = heads(XXF, 0, n, tiles)
                e.tensor_tensor(dst.rearrange("p (x h) t -> p x h t", h=2), src,
                                     mask(C_NL).rearrange("p (x h) t -> p x h t", h=2), ALU.mult).then_inc(S("dve_done"), 1)
                e.wait_ge(S("dve_done"), 1)
                e.sem_inc(S("dve_done"), -1)
                give(e, "bank2", "bank3")
                e.tensor_tensor(dst, dst, mask(C_ID), ALU.add).then_inc(S("x_ready"), 1)

            def level_right(u, s):
                _, n, tiles, levels = unit(u)
                w = 2 * tiles * n
                for k in range(0 if s < levels - 1 else 1, 2):
                    xx = XXF[0:n, k * 512:k * 512 + w]
                    e.wait_ge(S("dx_psum"), 1)
                    e.sem_inc(S("dx_psum"), -1)
                    e.tensor_tensor(xx, xx, PS[0:n, k * 512:k * 512 + w], ALU.subtract).then_inc(S(("x_ready", "xt_ready")[k]), 1)

            def chunk_u(u, c):
                _, n, _, _ = unit(u)
                r, x = slice((c % 2) * CHUNK, (c % 2) * CHUNK + min(n, CHUNK)), c // 2
                if c == 0:
                    e.wait_ge(S("q_ready"), 1)
                    e.sem_inc(S("q_ready"), -1)
                e.wait_ge(S("u_psum"), 1)
                e.sem_inc(S("u_psum"), -1)
                e.scalar_tensor_tensor(out=US[r, x, :], in0=PS[r, 3072:3072 + P], scalar=-1.0, in1=QS[r, x, :],
                                       op0=ALU.mult, op1=ALU.subtract).then_inc(S("u_ready"), 1)
                ec = 20 + 4 * u + c
                e.tensor_scalar(STMP, SBD, EC[:, ec:ec + 1], None, ALU.mult).then_inc(S("dve_done"), 1)
                e.wait_ge(S("dve_done"), 1)
                e.sem_inc(S("dve_done"), -1)

            def chunk_state(u, c):
                ec = 20 + 4 * u + c
                e.wait_ge(S("ds_psum"), 1)
                e.sem_inc(S("ds_psum"), -1)
                for h in range(2):
                    p, q = slice(h * HEAD, (h + 1) * HEAD), 2560 + h * HEAD
                    ins = e.scalar_tensor_tensor(out=SBD[p, h * HEAD:(h + 1) * HEAD], in0=PS[p, q:q + HEAD], scalar=EC[p, ec:ec + 1],
                                                 in1=STMP[p, h * HEAD:(h + 1) * HEAD], op0=ALU.mult, op1=ALU.add)
                ins.then_inc(S("state_ready"), 1)

            give(e, "y_saved", "states_saved")
            with e.Fori(0, PAIRS) as j:
                e.wait_ge(S("y_saved"), 1)
                e.sem_inc(S("y_saved"), -1)
                e.tensor_copy(PC[:, 0:3], PRM[:, bass.ds(MU_AT + j, 9)][:, 0:9:4]).then_inc(S("dve_done"), 1)
                e.wait_ge(S("dve_done"), 1)
                e.sem_inc(S("dve_done"), -1)
                e.tensor_copy(PC[:, 3:9], PRM[:, bass.ds(RV_AT + j, 21)][:, 0:21:4]).then_inc(S("dve_done"), 1)
                e.wait_ge(S("dve_done"), 1)
                e.sem_inc(S("dve_done"), -1)
                e.tensor_copy(PC[:, 9:12], PRM[:, bass.ds(SH_AT + j, 9)][:, 0:9:4]).then_inc(S("dve_done"), 1)
                e.wait_ge(S("dve_done"), 1)
                e.sem_inc(S("dve_done"), -1)
                e.tensor_copy(PC[:, 12:13], PRM[:, bass.ds(RK_AT + j, 1)]).then_inc(S("dve_done"), 1)
                e.wait_ge(S("dve_done"), 1)
                e.sem_inc(S("dve_done"), -1)
                e.tensor_scalar(PC[:, 13:14], PC[:, 6:7], -1.0, 1.0, ALU.mult, ALU.add).then_inc(S("dve_done"), 1)
                e.wait_ge(S("dve_done"), 1)
                e.sem_inc(S("dve_done"), -1)
                give(e, "pc_ready")
                for b, dst in enumerate((RR, KF, VV)):
                    shifted(dst, PC[:, b:b + 1], PC[:, 9 + b:10 + b])
                    kept(lambda g: SHC[:, bass.ds(j + (b * 4 + g), 1)])
                    if b == 1:
                        e.wait_ge(S("states_saved"), 1)
                        e.sem_inc(S("states_saved"), -1)
                        e.wait_ge(S("wh_ready1"), 1)
                        e.sem_inc(S("wh_ready1"), -1)
                        e.tensor_copy(LW, WRAW[:, 1, 0:3 * P]).then_inc(S("dve_done"), 1)
                        e.wait_ge(S("dve_done"), 1)
                        e.sem_inc(S("dve_done"), -1)
                        give(e, "lw_ready")
                        give(e, "wh_ready1")
                    lo(b % 2)
                e.memset(SEG, 1.0).then_inc(S("dve_done"), 1)
                e.wait_ge(S("dve_done"), 1)
                e.sem_inc(S("dve_done"), -1)
                e.memset(SEG[:, 0:T:CHUNK], 0.0).then_inc(S("dve_done"), 1)
                e.wait_ge(S("dve_done"), 1)
                e.sem_inc(S("dve_done"), -1)
                e.wait_ge(S("sig_ready"), 1)
                e.sem_inc(S("sig_ready"), -1)
                lo(1)
                e.tensor_tensor_scan(DD, SEG, DD2, 0.0, ALU.mult, ALU.add).then_inc(S("dve_done"), 1)
                e.wait_ge(S("dve_done"), 1)
                e.sem_inc(S("dve_done"), -1)
                d = DD[:, 0:SEQ].rearrange("p (c t) -> p c t", t=CHUNK)
                e.tensor_copy(ST[:, 0:16], d[:, :, 31]).then_inc(S("dve_done"), 1)
                e.wait_ge(S("dve_done"), 1)
                e.sem_inc(S("dve_done"), -1)
                e.tensor_copy(ST[:, 16:17], DD[:, SEQ + 15:SEQ + 16]).then_inc(S("dve_done"), 1)
                e.wait_ge(S("dve_done"), 1)
                e.sem_inc(S("dve_done"), -1)
                e.tensor_tensor(EC[:, 0:16], d[:, :, 63], ST[:, 0:16], ALU.subtract).then_inc(S("dve_done"), 1)
                e.wait_ge(S("dve_done"), 1)
                e.sem_inc(S("dve_done"), -1)
                e.tensor_tensor(EC[:, 0:15], EC[:, 0:15], ST[:, 1:16], ALU.add).then_inc(S("dve_done"), 1)
                e.wait_ge(S("dve_done"), 1)
                e.sem_inc(S("dve_done"), -1)
                e.tensor_tensor(EC[:, 16:17], DD[:, T - 1:T], ST[:, 16:17], ALU.subtract).then_inc(S("dve_done"), 1)
                e.wait_ge(S("dve_done"), 1)
                e.sem_inc(S("dve_done"), -1)
                e.tensor_copy(EC[:, 17:18], ST[:, 16:17]).then_inc(S("dve_done"), 1)
                e.wait_ge(S("dve_done"), 1)
                e.sem_inc(S("dve_done"), -1)
                e.tensor_tensor(d, d, ST[:, 0:16].unsqueeze(2).broadcast_to([P, 16, CHUNK]), ALU.subtract).then_inc(S("dve_done"), 1)
                e.wait_ge(S("dve_done"), 1)
                e.sem_inc(S("dve_done"), -1)
                e.tensor_scalar(DD[:, SEQ:T], DD[:, SEQ:T], ST[:, 16:17], None, ALU.subtract).then_inc(S("dve_done"), 1)
                e.wait_ge(S("dve_done"), 1)
                e.sem_inc(S("dve_done"), -1)
                e.tensor_tensor(DD2, DD, DD2, ALU.subtract).then_inc(S("dve_done"), 1)
                e.wait_ge(S("dve_done"), 1)
                e.sem_inc(S("dve_done"), -1)
                e.tensor_scalar(KK, KF, PC[:, 5:6], None, ALU.mult).then_inc(S("dve_done"), 1)
                e.wait_ge(S("dve_done"), 1)
                e.sem_inc(S("dve_done"), -1)
                give(e, "kkr_ready")
                e.tensor_scalar(TMP[:, 1, :], BB, PC[:, 6:7], PC[:, 13:14], ALU.mult, ALU.add).then_inc(S("dve_done"), 1)
                e.wait_ge(S("dve_done"), 1)
                e.sem_inc(S("dve_done"), -1)
                e.tensor_tensor(KF, KF, TMP[:, 1, :], ALU.mult).then_inc(S("dve_done"), 1)
                e.wait_ge(S("dve_done"), 1)
                e.sem_inc(S("dve_done"), -1)
                e.scalar_tensor_tensor(out=TMP[:, 1, :], in0=RR, scalar=PC[:, 12:13], in1=KF, op0=ALU.mult, op1=ALU.mult).then_inc(S("dve_done"), 1)
                e.wait_ge(S("dve_done"), 1)
                e.sem_inc(S("dve_done"), -1)
                give(e, "rk_ready")
                for c in range(CH):
                    e.wait_ge(S("kk_psum"), 1)
                    e.sem_inc(S("kk_psum"), -1)
                    e.tensor_scalar(TMP[:, 2, chunk(c)], bank(c, 0, CW), 1e-24, None, ALU.max).then_inc(S("dve_done"), 1)
                    e.wait_ge(S("dve_done"), 1)
                    e.sem_inc(S("dve_done"), -1)
                    give(e, f"bank{c}")
                give(e, "kkn_ready")
                for c in range(CH):
                    e.wait_ge(S("rk_psum"), 1)
                    e.sem_inc(S("rk_psum"), -1)
                    e.tensor_tensor(BON[:, chunk(c)], VV[:, chunk(c)], bank(3 + c, 0, CW), ALU.mult).then_inc(S("dve_done"), 1)
                    e.wait_ge(S("dve_done"), 1)
                    e.sem_inc(S("dve_done"), -1)
                    give(e, f"bank{3 + c}")
                e.wait_ge(S("kks_ready"), 1)
                e.sem_inc(S("kks_ready"), -1)
                e.tensor_tensor(KK, KK, TMP[:, 2, :], ALU.mult).then_inc(S("dve_done"), 1)
                e.wait_ge(S("dve_done"), 1)
                e.sem_inc(S("dve_done"), -1)
                e.tensor_tensor(BB, BB, KK, ALU.mult).then_inc(S("dve_done"), 1)
                e.wait_ge(S("dve_done"), 1)
                e.sem_inc(S("dve_done"), -1)
                give(e, "dd_ready")
                e.wait_ge(S("e_ready"), 1)
                e.sem_inc(S("e_ready"), -1)
                e.tensor_tensor(RR, RR, TMP[:, 0, :], ALU.mult).then_inc(S("dve_done"), 1)
                e.wait_ge(S("dve_done"), 1)
                e.sem_inc(S("dve_done"), -1)
                e.tensor_tensor(KK, KK, TMP[:, 1, :], ALU.mult).then_inc(S("dve_done"), 1)
                e.wait_ge(S("dve_done"), 1)
                e.sem_inc(S("dve_done"), -1)
                e.tensor_tensor(BB, BB, TMP[:, 2, :], ALU.mult).then_inc(S("dve_done"), 1)
                e.wait_ge(S("dve_done"), 1)
                e.sem_inc(S("dve_done"), -1)
                e.tensor_tensor(KF, KF, TMP[:, 2, :], ALU.mult).then_inc(S("dve_done"), 1)
                e.wait_ge(S("dve_done"), 1)
                e.sem_inc(S("dve_done"), -1)
                e.memset(SAMPLE_IN, 0.0).then_inc(S("dve_done"), 1)
                e.wait_ge(S("dve_done"), 1)
                e.sem_inc(S("dve_done"), -1)
                give(e, "sin_free")
                e.memset(SBD, 0.0).then_inc(S("dve_done"), 1)
                e.wait_ge(S("dve_done"), 1)
                e.sem_inc(S("dve_done"), -1)
                give(e, "state_ready", "til_ready")
                for u in range(UNITS + 1):
                    _, _, tiles, levels = unit(u)
                    if u > 0:
                        chunk_u(u - 1, 0)
                    scores(u, 0)
                    if u > 0:
                        chunk_state(u - 1, 0)
                    if tiles == 2:
                        scores(u, 1)
                    low(u)
                    for s in range(levels):
                        if u > 0 and s < 3:
                            chunk_u(u - 1, s + 1)
                        level_right(u, s)
                        if u > 0 and s < 3:
                            chunk_state(u - 1, s + 1)
                e.wait_ge(S("sin_psum"), 1)
                e.sem_inc(S("sin_psum"), -1)
                e.tensor_scalar(SBD, PS[:, 512:512 + P], EC[:, 37:38], None, ALU.mult).then_inc(S("dve_done"), 1)
                e.wait_ge(S("dve_done"), 1)
                e.sem_inc(S("dve_done"), -1)
                give(e, "bank1", "state_ready")
                chunk_u(UNITS, 0)
                chunk_state(UNITS, 0)
                e.wait_ge(S("rms_ready"), 1)
                e.sem_inc(S("rms_ready"), -1)
                e.tensor_tensor(YY, TMP[:, 1, :], TMP[:, 2, :], ALU.mult).then_inc(S("dve_done"), 1)
                e.wait_ge(S("dve_done"), 1)
                e.sem_inc(S("dve_done"), -1)
                e.tensor_scalar(YY, YY, PC[:, 7:8], PC[:, 8:9], ALU.mult, ALU.add).then_inc(S("dve_done"), 1)
                e.wait_ge(S("dve_done"), 1)
                e.sem_inc(S("dve_done"), -1)
                e.tensor_tensor(YY, YY, BON, ALU.add).then_inc(S("dve_done"), 1)
                e.wait_ge(S("dve_done"), 1)
                e.sem_inc(S("dve_done"), -1)
                e.tensor_tensor(YY, YY, GG, ALU.mult).then_inc(S("dve_done"), 1)
                e.wait_ge(S("dve_done"), 1)
                e.sem_inc(S("dve_done"), -1)
                give(e, "y_ready")
            e.wait_ge(S("y_saved"), 1)
            e.sem_inc(S("y_saved"), -1)
            e.wait_ge(S("states_saved"), 1)
            e.sem_inc(S("states_saved"), -1)
            give(e, "shc_full")
            barrier(e, "dve")
            e.wait_ge(S("mix_dve"), 1)
            e.sem_inc(S("mix_dve"), -1)
            for b in range(DB):
                e.wait_ge(S("hh_ready"), 1)
                e.sem_inc(S("hh_ready"), -1)
                e.tensor_tensor(HL[:, b, :], R2[:, b, :], HH[:, b, :].bitcast(F32), ALU.subtract).then_inc(S("dve_done"), 1)
                e.wait_ge(S("dve_done"), 1)
                e.sem_inc(S("dve_done"), -1)
                give(e, "h_ready")
            give(e, "r2_free")
            e.memset(TMP[:, 2, :], 0.0).then_inc(S("dve_done"), 1)
            e.wait_ge(S("dve_done"), 1)
            e.sem_inc(S("dve_done"), -1)
            with e.Fori(0, 4) as i:
                for s in range(2):
                    lo(s)
                    add_square(s)
            give(e, "sq_sum")
            e.wait_ge(S("rms_ready"), 1)
            e.sem_inc(S("rms_ready"), -1)
            barrier(e, "dve")
            add_and_norm(MIX_POST, X_PRE)
            give(e, "cv_free")
            los(2)

            def cross(i, n):
                e.wait_ge(S("cs_psum"), 1)
                e.sem_inc(S("cs_psum"), -1)
                e.tensor_reduce(ST[0:n, 0:4], PS[0:n, 0:1024].rearrange("p (h k) -> p h k", h=4), AX.X, ALU.max).then_inc(S("dve_done"), 1)
                e.wait_ge(S("dve_done"), 1)
                e.sem_inc(S("dve_done"), -1)
                e.tensor_scalar(ST[0:n, 4:8], ST[0:n, 0:4], -float(P) ** -0.5, None, ALU.mult).then_inc(S("dve_done"), 1)
                e.wait_ge(S("dve_done"), 1)
                e.sem_inc(S("dve_done"), -1)
                give(e, "cnm_ready")
                e.wait_ge(S("cexp_ready"), 1)
                e.sem_inc(S("cexp_ready"), -1)
                e.reciprocal(ST[0:n, 0:4], ST[0:n, 8:12]).then_inc(S("dve_done"), 1)
                e.wait_ge(S("dve_done"), 1)
                e.sem_inc(S("dve_done"), -1)
                e.tensor_tensor(CP[0:n, :, :], CP[0:n, :, :], ST[0:n, 0:4].unsqueeze(2).broadcast_to([n, 4, MEM]), ALU.mult).then_inc(S("dve_done"), 1)
                e.wait_ge(S("dve_done"), 1)
                e.sem_inc(S("dve_done"), -1)
                give(e, "cp_ready")
                e.wait_ge(S("coh_ready"), 1)
                e.sem_inc(S("coh_ready"), -1)
                e.tensor_tensor(HL[:, 0:4, bass.ds(i, n)], PS[:, 2048:2048 + 4 * n].rearrange("p (h q) -> p h q", h=4),
                                     HH[:, 0:4, bass.ds(i, n)].bitcast(F32), ALU.subtract).then_inc(S("dve_done"), 1)
                e.wait_ge(S("dve_done"), 1)
                e.sem_inc(S("dve_done"), -1)
                give(e, "bank4")

            with e.Fori(0, TILES) as t:
                cross(t * P, P)
            give(e, "cv_free")
            cross(SEQ, DEC_SEQ)
            give(e, "ch_ready")
            e.memset(TMP[:, 2, :], 0.0).then_inc(S("dve_done"), 1)
            e.wait_ge(S("dve_done"), 1)
            e.sem_inc(S("dve_done"), -1)
            with e.Fori(0, 2) as i:
                for s in range(2):
                    add_square(0)
                    lo(s)
                    add_square(1)
            give(e, "sq_sum")
            e.wait_ge(S("rms_ready"), 1)
            e.sem_inc(S("rms_ready"), -1)
            barrier(e, "dve")
            add_and_norm(X_POST, FFN_PRE)
            give(e, "silu_free", "silu_free", "silu_free")

            def group(first):
                for f in range(2):
                    lo(0)
                    for c in range(CH):
                        e.wait_ge(S("silu_ready"), 1)
                        e.sem_inc(S("silu_ready"), -1)
                        e.wait_ge(S("up_psum"), 1)
                        e.sem_inc(S("up_psum"), -1)
                        if c == CH - 1:
                            give(e, "w1_used")
                        e.tensor_tensor(TMP[:, 1, chunk(c)], TMP[:, 0, chunk(c)], bank(3 + c, 0, CW), ALU.mult).then_inc(S("dve_done"), 1)
                        e.wait_ge(S("dve_done"), 1)
                        e.sem_inc(S("dve_done"), -1)
                        give(e, f"bank{3 + c}", "gu_ready", "silu_free")
                    lo(1)
                    for c in range(CH):
                        e.wait_ge(S("gh_ready"), 1)
                        e.sem_inc(S("gh_ready"), -1)
                        e.tensor_tensor(GL[:, f, chunk(c)], TMP[:, 1, chunk(c)], GH[:, f, chunk(c)].bitcast(F32), ALU.subtract).then_inc(S("dve_done"), 1)
                        e.wait_ge(S("dve_done"), 1)
                        e.sem_inc(S("dve_done"), -1)
                        if f == 1:
                            give(e, "g_ready")
                for c in range(CH):
                    for m in range(DB):
                        if c == CH - 1 and m == 3:
                            lo(0)
                        b = DOWN_BANKS[m]
                        e.wait_ge(S("down_psum"), 1)
                        e.sem_inc(S("down_psum"), -1)
                        if c == CH - 1 and m == DB - 1:
                            give(e, "w1_used")
                        if first:
                            e.tensor_copy(R2[:, m, chunk(c)], bank(b, 0, CW)).then_inc(S(f"bank{b}"), 1)
                        else:
                            e.tensor_tensor(R2[:, m, chunk(c)], R2[:, m, chunk(c)], bank(b, 0, CW), ALU.add).then_inc(S(f"bank{b}"), 1)
                lo(1)

            group(True)
            with e.Fori(1, FB // 2) as i:
                group(False)
            e.wait_ge(S("silu_free"), 3)
            e.sem_inc(S("silu_free"), -3)
            give(e, "r2_ready")
            sum_squares()
            add_normed(FFN_POST, False)
            barrier(e, "dve")


INPUTS = ["x_prompt", "mem_prompt", "x_sample", "cache_swa_k", "cache_swa_v", "cache_mem_k", "cache_mem_v", "state_rwkv",
          "state_shift", "norm_gains", "w_in", "attn_sink", "shift_mu", "rwkv_vecs", "rwkv_rk", "rwkv_w2", "rwkv_a2",
          "rwkv_g2", "w_out", "w_mem_q", "w_mem_kv", "w_mem_o", "w_gate_up", "w_down"]
OUTPUTS = [("y_prompt", (1, SEQ, D_MODEL)), ("y_sample", (1, DEC_SEQ, D_MODEL)),
           ("new_swa_k_prompt", (DEPTH, 1, WINDOW, 2, HEAD)), ("new_swa_v_prompt", (DEPTH, 1, WINDOW, 2, HEAD)),
           ("new_mem_k_prompt", (DEPTH, 1, MEM, MEM_HEADS, P)), ("new_mem_v_prompt", (DEPTH, 1, MEM, MEM_HEADS, P)),
           ("new_state_rwkv_prompt", (DEPTH, 1, 8, HEAD, HEAD)), ("new_state_shift_prompt", (DEPTH, 1, 1, RWKV_PROJ)),
           ("new_swa_k_sample", (DEPTH, 1, DEC_SEQ, 2, HEAD)), ("new_swa_v_sample", (DEPTH, 1, DEC_SEQ, 2, HEAD)),
           ("new_state_rwkv_sample", (DEPTH, 1, 8, HEAD, HEAD)), ("new_state_shift_sample", (DEPTH, 1, 1, RWKV_PROJ))]


def kernel(**inputs):
    import concourse.bacc as bacc
    from concourse.bass_utils import run_bass_kernel_spmd

    nc = bacc.Bacc("TRN2", target_bir_lowering=False, num_devices=1)
    arrays, io = {}, {}
    c, long = constants()
    for name, a in [(n, inputs[n]) for n in INPUTS] + [("consts", c), ("long", long)]:
        arrays[f"in_{name}"] = np.ascontiguousarray(a)
        io[name] = nc.dram_tensor(f"in_{name}", arrays[f"in_{name}"].shape, F32, kind="ExternalInput").ap()
    for name, shape in OUTPUTS:
        io[name] = nc.dram_tensor(f"out_{name}", shape, F32, kind="ExternalOutput").ap()
    program(nc, io)
    r = run_bass_kernel_spmd(nc, [arrays], core_ids=[0])
    return tuple(r.results[0][f"out_{name}"] for name, _ in OUTPUTS)
```

```python
from contextlib import ExitStack

import numpy as np

import concourse.bass as bass
from concourse import mybir

F32 = mybir.dt.float32
F32R = mybir.dt.float32r
ALU = mybir.AluOpType
ACT = mybir.ActivationFunctionType
AX = mybir.AxisListType

P = 128
D_MODEL, SEQ, DEC_SEQ, DEPTH, PAST_LEN = 1024, 1024, 32, 2, 512
T = SEQ + DEC_SEQ
CH = 3
CW = T // CH
DB = D_MODEL // P
HEAD, CHUNK, WINDOW = 64, 64, 128
A_WIDTH, KV_A, R_WIDTH = 512, 128, 512
PAIRS = R_WIDTH // P
UNITS = SEQ // 256
LORA_W, LORA_A, LORA_G = 64, 64, 160
RWKV_PROJ = 3 * R_WIDTH + LORA_W + LORA_A + LORA_G
R0 = A_WIDTH + 2 * KV_A
MEM, MEM_HEADS = 256, 4
D_FF = 2816
FB = D_FF // P
TILES = SEQ // P
RMS_EPS, GN_EPS = 1e-6, 6.4e-4
NEG = -1e30
DECAY = float(np.exp(-0.5))
MIX_PRE, MIX_POST, X_PRE, X_POST, N_MEM, FFN_PRE, FFN_POST = range(7)

G_AT, MU_AT, SH_AT, RV_AT, RK_AT, PRM_ROWS = 0, 56, 71, 86, 110, 114
C_ID, C_PERM, C_MEAN, C_BD, C_BDM, C_CEN = (i * P for i in range(6))
C_M3 = 6 * P
C_NL = 9 * P
C_NU = 10 * P
C_LV = 11 * P
C_AE = 16 * P
C_AO = C_AE + 4 * 256
C_EPS = C_AO + 256
C_COLS = C_EPS + 2


def constants():
    c = np.zeros((P, C_COLS), np.float32)
    i, j = np.arange(P)[:, None], np.arange(P)[None, :]
    same = (i // 64) == (j // 64)
    c[:, C_ID:C_ID + P] = i == j
    c[:, C_PERM:C_PERM + P] = np.where((j % 64 < 32) & (i == j + 32), -1.0, 0.0) + ((j % 64 >= 32) & (i == j - 32))
    c[:, C_MEAN:C_MEAN + P] = 1.0 / D_MODEL
    c[:, C_BD:C_BD + P] = same
    c[:, C_BDM:C_BDM + P] = same / 64.0
    c[:, C_CEN:C_CEN + P] = (i == j) - same / 64.0
    c[:, C_M3:C_M3 + 2 * P] = np.tile(same & (i < j), (1, 2))
    c[:, C_M3 + 2 * P:C_M3 + 3 * P] = same & (i <= j)
    c[:, C_NL:C_NL + P] = -1.0 * ((i // 2 == j // 2) & (i > j))
    c[:, C_NU:C_NU + P] = -1.0 * ((i // 2 == j // 2) & (i < j))
    for n in range(5):
        s = 2 << n
        c[:, C_LV + n * P:C_LV + (n + 1) * P] = (i // (2 * s) == j // (2 * s)) & (i // s < j // s)
    cur = np.where((i < 64) & (j >= 64), NEG, 0.0)
    prev = np.where((i >= 64) & (j < 64), NEG, 0.0)
    for it in range(4):
        at = C_AE + it * 256
        c[:, at:at + P] = cur
        c[:, at + P:at + 2 * P] = NEG if it == 0 else prev
    c[:, C_AO:C_AO + P] = prev
    c[:, C_AO + P:C_AO + 2 * P] = cur
    c[:, C_EPS] = RMS_EPS
    c[:, C_EPS + 1] = GN_EPS
    pos = np.concatenate([np.arange(SEQ), PAST_LEN + np.arange(DEC_SEQ)]).astype(np.float32)
    inv = np.float32(10000.0) ** (-np.arange(32, dtype=np.float32) / np.float32(32))
    ang = (pos[None, :] * inv[:, None]).astype(np.float32)
    long = np.zeros((2, P, T), np.float32)
    long[0] = np.tile(np.cos(ang), (4, 1))
    long[1] = np.tile(np.sin(ang), (4, 1))
    return c, long


def program(nc, io):
    with ExitStack() as ctx:
        build(nc, io, ctx)


def build(nc, io, ctx):
    def sb(name, shape, dt=F32):
        return ctx.enter_context(nc.sbuf_tensor(name, shape, dt))

    R1 = sb("R1", [P, DB, T])
    R2 = sb("R2", [P, DB, T])
    HH, HL = sb("HH", [P, DB, T], F32R), sb("HL", [P, DB, T], F32R)
    GH, GL = sb("GH", [P, 2, T], F32R), sb("GL", [P, 2, T], F32R)
    TMP = sb("TMP", [P, 3, T])
    WRAW = sb("WRAW", [P, 2, 1024])
    WH, WL = sb("WH", [P, 2, 1024], F32R), sb("WL", [P, 2, 1024], F32R)
    CST = sb("CST", [P, C_COLS])
    PRM = sb("PRM", [P, PRM_ROWS])
    PC = sb("PC", [P, 16])
    SINK = sb("SINK", [P, 8])
    ST = sb("ST", [P, 64])
    EC = sb("EC", [P, 40])
    AUX = sb("AUX", [P, 1088])
    PS = ctx.enter_context(nc.psum_tensor("PS", [P, 8 * 512], F32))

    x_spill = nc.dram_tensor("x_spill", [P, DB, T], F32, kind="Internal").ap()
    mix_dram = nc.dram_tensor("mix_dram", [P, DB, T], F32, kind="Internal").ap()
    mem_dram = nc.dram_tensor("mem_dram", [P, DB, MEM], F32, kind="Internal").ap()

    for_vector = {n + "_psum" for n in ("swap", "score", "sm", "l", "dx", "u", "ds", "kk", "rk", "sin",
                                      "cs", "up", "down", "xT_dve")}
    sems = {}

    def S(name):
        if name.endswith("_psum"):
            name = "product_for_vector" if name in for_vector else "product_for_scalar"
        if name not in sems:
            sems[name] = ctx.enter_context(nc.semaphore(name))
        return sems[name]

    def give(e, *names):
        for name in names:
            e.sem_inc(S(name), 1)

    def bank(b, a=0, z=512):
        return PS[:, b * 512 + a:b * 512 + z]

    ENG = ["act", "dve", "pe", "pool"]

    def barrier(e, who):
        e.drain()
        for other in ENG:
            if other != who:
                give(e, f"end_{who}_{other}")
        for other in ENG:
            if other != who:
                e.wait_ge(S(f"end_{other}_{who}"), 1)
                e.sem_inc(S(f"end_{other}_{who}"), -1)

    def cst(at, w=P):
        return CST[:, at:at + w]

    ident, perm, mean = cst(C_ID), cst(C_PERM), cst(C_MEAN)

    def chunk(c):
        return slice(c * CW, (c + 1) * CW)

    r2flat = R2[:, :, :].rearrange("p a t -> p (a t)")
    tflat = TMP[:, :, :].rearrange("p a t -> p (a t)")
    PRAW = r2flat[:, 6 * T:6 * T + T + 2]
    r1tail = R1[:, 7, :]
    RT = r1tail[:, 0:768].rearrange("p (a t) -> p a t", t=P)
    SC = r2flat[:, 3 * T:3 * T + 2048].rearrange("p (h k) -> p h k", h=8)
    PT = tflat[:, 0:2048].rearrange("p (h k q) -> p h k q", h=8, k=2)
    RU = TMP[:, 2, 0:768].rearrange("p (a t) -> p a t", t=P)
    VST = TMP[:, 2, 768:896]
    KCR = (TMP[:, 2, 896:1024], AUX[:, 896:1024])
    VCR = r1tail[:, 768:896]
    QR = R2[:, 5, 0:512].rearrange("p (a t) -> p a t", t=P)
    KR = R2[:, 5, 512:1024].rearrange("p (v s t) -> p v s t", v=2, s=2)
    VT = AUX[:, 0:256].rearrange("p (s t) -> p s t", s=2)
    OT = AUX[:, 256:768].rearrange("p (a t) -> p a t", t=P)
    KO = AUX[:, 768:896]
    COS, SIN = R2[:, 6, :], R2[:, 7, :]
    KK, RR, BB, KF, VV, GG, BON, YY = (R1[:, i, :] for i in range(8))
    TWA, SG1, SG2, DD2, DD, SEG = (R2[:, i, :] for i in range(6))
    LTM, XXF = r2flat[:, 3 * T:3 * T + 1536], r2flat[:, 3 * T + 1536:3 * T + 2560]
    T1F = r2flat[:, 3 * T + 2560:3 * T + 3072]
    ATM = AUX[:, 768:1024].rearrange("p (x t) -> p x t", x=2)
    QS = tflat[:, 2560:2816].rearrange("p (x t) -> p x t", x=2)
    w0 = 6 * T
    US = r2flat[:, w0:w0 + 256].rearrange("p (x t) -> p x t", x=2)
    MVS = r2flat[:, w0 + 256:w0 + 512].rearrange("p (x t) -> p x t", x=2)
    ELF = r2flat[:, w0 + 512:w0 + 1536]
    PTS = r2flat[:, w0 + 1536:w0 + 1792].rearrange("p (x t) -> p x t", x=2)

    def unit(u):
        return (u * 256, P, 2, 5) if u < UNITS else (SEQ, DEC_SEQ, 1, 4)

    def bkv(u):
        return tflat[:, (u % 2) * 768:(u % 2 + 1) * 768].rearrange("p (x a t) -> p x a t", x=2, a=3)

    def heads(buf, at, n, tiles):
        return buf[0:n, at:at + 2 * tiles * n].rearrange("p (g t) -> p g t", g=2 * tiles)

    PROW = AUX[:, 0:128]
    SBD = AUX[:, 0:128]
    STMP = AUX[:, 128:256]
    SIO = AUX[:, 256:384]
    LW = AUX[:, 384:768]
    SAMPLE_IN, SAMPLE_OUT = AUX[:, 384:512], AUX[:, 512:640]
    SHC = AUX[:, 1024:1056]
    xq = r2flat[:, 4 * T:8 * T]
    CKT = xq[:, 0:1024].rearrange("p (h k) -> p h k", h=4)
    CV = [x.rearrange("p (k d) -> p k d", k=2) for x in (xq[:, 1024:2048], tflat[:, 1536:2560])]
    CKR = xq[:, 2048:3072].rearrange("p (k d) -> p k d", k=2)
    CP = xq[:, 3072:4096].rearrange("p (h k) -> p h k", h=4)
    CPT = tflat[:, 0:1024].rearrange("p (h k q) -> p h k q", h=4, k=2)
    CQ = tflat[:, 1024:1536].rearrange("p (h q) -> p h q", h=4)

    MEMT = r2flat[:, 2 * T:2 * T + DB * MEM].rearrange("p (b t) -> p b t", b=DB)
    DOWN_BANKS = [6, 7, 0, 1, 2, 3, 4, 5]
    block = ctx.enter_context(nc.Block())

    def w_block(w, l, c0, cols=P, kb=DB):
        return w[bass.ds(l, 1)].rearrange("a (k p) n -> p (a k) n", p=P)[:, 0:kb, bass.ds(c0, cols)]

    @block.sync
    def _(e):
        def weight(slot, src, view=None):
            e.wait_ge(S(f"w_free{slot}"), 1)
            e.sem_inc(S(f"w_free{slot}"), -1)
            dst = WRAW[:, slot, :]
            e.dma_start(view(dst) if view else dst, src).then_inc(S(f"w_full{slot}"), 16)

        def w8(slot, w, l, c0):
            weight(slot, w_block(w, l, c0), view=lambda d: d.rearrange("p (k n) -> p k n", k=DB))

        def stream(w, l, pairs, c0=0):
            with e.Fori(0, pairs) as i:
                for s in range(2):
                    w8(s, w, l, (i * 2 + s) * P + c0)

        def tokens_in(s, src, rows):
            e.wait_ge(S(f"xin_free{s}"), 1)
            e.sem_inc(S(f"xin_free{s}"), -1)
            e.dma_start(R2[0:rows, s, 0:D_MODEL], src).then_inc(S(f"xin_full{s}"), 16)

        for s in range(2):
            tokens_in(s, io["mem_prompt"][0, s * P:(s + 1) * P, :], P)
        with e.Fori(0, TILES // 2) as j:
            for s in range(2):
                tokens_in(s, io["x_prompt"][0, bass.ds((j * 2 + s) * P, P), :], P)
        tokens_in(0, io["x_sample"][0], DEC_SEQ)
        with e.Fori(0, DEPTH) as l:
            stream(io["w_mem_kv"], l, 4)
            stream(io["w_in"], l, 2)
            for s in range(2):
                e.wait_ge(S(f"w_free{s}"), 1)
                e.sem_inc(S(f"w_free{s}"), -1)
                for g in range(2):
                    done = "k_part" if g == 0 else f"w_full{s}"
                    e.dma_start(WRAW[:, s, :].rearrange("p (k g n) -> p k g n", k=DB, g=2)[:, :, g, :],
                                w_block(io["w_in"], l, A_WIDTH + s * HEAD, HEAD)).then_inc(S(done), 16)
                    if g == 0:
                        e.wait_ge(S("k_part"), 16)
                        e.sem_inc(S("k_part"), -16)
            w8(0, io["w_in"], l, A_WIDTH + KV_A)
            w8(1, io["w_in"], l, R0 + 3 * R_WIDTH)
            w8(0, io["w_in"], l, R0 + 3 * R_WIDTH + P)
            weight(1, w_block(io["w_in"], l, R0 + 3 * R_WIDTH + 2 * P, 32),
                   view=lambda d: d.rearrange("p (k n) -> p k n", k=DB)[:, :, 0:32])
            with e.Fori(0, PAIRS) as j:
                w8(0, io["w_in"], l, j * P + R0)
                e.wait_ge(S("w_free1"), 1)
                e.sem_inc(S("w_free1"), -1)
                lw = WRAW[:, 1, :]
                parts = ((lw[0:64, 0:P], io["rwkv_w2"][bass.ds(l, 1)]), (lw[64:128, 0:P], io["rwkv_a2"][bass.ds(l, 1)]),
                         (lw[:, P:2 * P], io["rwkv_g2"][bass.ds(l, 1), 0:P, :]),
                         (lw[0:32, 2 * P:3 * P], io["rwkv_g2"][bass.ds(l, 1), P:LORA_G, :]))
                for n, (dst, src) in enumerate(parts):
                    e.dma_start(dst, src.rearrange("a r n -> (a r) n")[:, bass.ds(j * P, P)]).then_inc(S("lw_part" if n < 3 else "w_full1"), 16)
                    if n == 2:
                        e.wait_ge(S("lw_part"), 48)
                        e.sem_inc(S("lw_part"), -48)
                for b in range(1, 3):
                    w8(b - 1, io["w_in"], l, j * P + R0 + b * R_WIDTH)
            stream(io["w_out"], l, 4)
            stream(io["w_mem_q"], l, 2)
            with e.Fori(0, 2) as i:
                for s in range(2):
                    weight(s, w_block(io["w_mem_o"], l, (i * 2 + s) * 2 * P, 2 * P, 4),
                           view=lambda d: d.rearrange("p (k n) -> p k n", k=4))
            with e.Fori(0, FB // 2) as i:
                for f in range(2):
                    w8(0, io["w_gate_up"], l, (i * 2 + f) * P)
                    w8(1, io["w_gate_up"], l, (i * 2 + f) * P + D_FF)
                for f in range(2):
                    weight(f, io["w_down"][bass.ds(l, 1), bass.ds((i * 2 + f) * P, P), :].rearrange("a p n -> p (a n)"))
        for s in range(2):
            weight(s, io["w_down"][0, 0:P, :])

        def tokens_out(s, dst, n):
            e.wait_ge(S(f"xout_ready{s}"), 1)
            e.sem_inc(S(f"xout_ready{s}"), -1)
            e.dma_start(dst, R2[0:n, 4 + s, 0:D_MODEL]).then_inc(S(f"xout_done{s}"), 16)

        with e.Fori(0, TILES // 2) as j:
            for s in range(2):
                tokens_out(s, io["y_prompt"][0, bass.ds((j * 2 + s) * P, P), :], P)
        tokens_out(0, io["y_sample"][0], DEC_SEQ)

    @block.gpsimd
    def _(e):
        due = e.alloc_register("moves_due")
        e.reg_mov(due, 0)
        mix_due = e.alloc_register("mix_due")
        e.reg_mov(mix_due, 0)

        def move(dst, src):
            e.dma_start(dst, src).then_inc(S("moves"), 16)

        def moved(n=1):
            e.reg_add(due, due, 16 * n)
            e.wait_ge(S("moves"), e.snap(due, min_val=16))
            give(e, "moves_seen")

        move(CST[:, :], io["consts"])
        moved()
        give(e, "cst_act", "cst_dve", "cst_pe")

        e.wait_ge(S("memT_ready"), 1)
        e.sem_inc(S("memT_ready"), -1)
        e.wait_ge(S("memT_ready_act"), 1)
        e.sem_inc(S("memT_ready_act"), -1)
        move(mem_dram, MEMT)
        moved()
        with e.Fori(0, DEPTH) as l:

            def rows(at, src):
                move(PROW[at:at + src.shape[0], 0:src.shape[1]], src)

            lay = lambda name: io[name][bass.ds(l, 1)]
            e.wait_ge(S("prow_clear"), 1)
            e.sem_inc(S("prow_clear"), -1)
            rows(G_AT, lay("norm_gains").rearrange("a n (b p) -> (a n b) p", p=P))
            for at, src in ((MU_AT, lay("shift_mu")), (SH_AT, lay("state_shift").rearrange("a b c n -> (a b c) n"))):
                rows(at, src[:, 0:14 * P].rearrange("a (b p) -> (a b) p", p=P))
                rows(at + 14, src[:, 14 * P:RWKV_PROJ])
            rows(RV_AT, lay("rwkv_vecs").rearrange("a n (b p) -> (a n b) p", p=P))
            rows(RK_AT, lay("rwkv_rk").rearrange("a (b g) p -> (a b) (g p)", g=2))
            move(SINK[:, :], lay("attn_sink").broadcast_to([P, 8]))
            moved(8)
            give(e, "prm_rows")
            barrier(e, "pool")
            move(R2[:, :, 0:MEM], mem_dram)
            moved()
            give(e, "memT_act", "memT_dve")
            move(x_spill, R1[:, :, :])
            moved()
            for k, out in ((0, "new_mem_k_prompt"), (1, "new_mem_v_prompt")):
                for tt in range(2):
                    e.wait_ge(S("memtok_ready"), 1)
                    e.sem_inc(S("memtok_ready"), -1)
                    move(lay(out).rearrange("a b m h d -> (a b m) (h d)")[tt * P:(tt + 1) * P, :], R2[:, 2 + 2 * k + tt, 512:1024])
            moved(4)
            barrier(e, "pool")
            e.wait_ge(S("cos_free"), 1)
            e.sem_inc(S("cos_free"), -1)
            move(COS, io["long"][0])
            move(SIN, io["long"][1])
            moved(2)
            give(e, "cos_ready")

            def store_att(n, c0, beside=None):
                e.wait_ge(S("ot_ready"), 1)
                e.sem_inc(S("ot_ready"), -1)
                move(mix_dram[:, 0:4, bass.ds(c0, n)], OT[:, :, 0:n])
                if beside is not None:
                    rotary(n, beside)
                moved()
                give(e, "ot_free")

            def rotary(n, c0):
                tok = bass.ds(c0, n)
                e.wait_ge(S("rt_free"), 1)
                e.sem_inc(S("rt_free"), -1)
                e.tensor_tensor(RT[:, :, 0:n], R1[:, 0:6, tok], COS[:, tok].unsqueeze(1).broadcast_to([P, 6, n]), ALU.mult).then_inc(S("rt_ready"), 1)

            rotary(P, 0)
            rotary(P, P)
            for v in range(2):
                for g in range(2):
                    move(KCR[v][:, g * HEAD:(g + 1) * HEAD], lay("cache_swa_k").rearrange("a b m h d -> (a b m) h d")[:, v, :])
            move(VCR, lay("cache_swa_v").rearrange("a b m h d -> (a b m) (h d)"))
            moved(5)
            give(e, "cached_ready")
            with e.Fori(0, TILES - 2) as i:
                store_att(P, i * P, beside=i * P + 2 * P)
            store_att(P, SEQ - 2 * P)
            rotary(DEC_SEQ, SEQ)
            store_att(P, SEQ - P)

            def store_kv(n, slot, okey, oval):
                e.wait_ge(S("ko_ready"), 1)
                e.sem_inc(S("ko_ready"), -1)
                move(lay(okey).rearrange("a b m h d -> (a b m) (h d)"), KO[0:n, :])
                move(lay(oval).rearrange("a b m h d -> (a b m) (h d)"), VT[0:n, slot, :])
                moved(2)

            store_kv(P, 1, "new_swa_k_prompt", "new_swa_v_prompt")
            give(e, "ko_free")
            store_att(DEC_SEQ, SEQ)
            store_kv(DEC_SEQ, 0, "new_swa_k_sample", "new_swa_v_sample")
            barrier(e, "pool")

            def level_masks(u):
                _, n, tiles, levels = unit(u)
                mask = lambda at: CST[0:n, at:at + n].unsqueeze(1).broadcast_to([n, 2 * tiles, n])
                lt, xt = heads(LTM, 0, n, tiles), heads(XXF, 512, n, tiles)
                e.wait_ge(S("lt_ready"), 1)
                e.sem_inc(S("lt_ready"), -1)
                for s in range(levels):
                    e.wait_ge(S("elt_free"), 1)
                    e.sem_inc(S("elt_free"), -1)
                    e.tensor_tensor(heads(ELF, (s % 2) * 512, n, tiles), lt, mask(C_LV + s * P), ALU.mult).then_inc(S("elt_ready"), 1)
                    if s == 0:
                        e.tensor_tensor(xt, lt, mask(C_NU), ALU.mult).then_inc(S("pool_done"), 1)
                        e.wait_ge(S("pool_done"), 1)
                        e.sem_inc(S("pool_done"), -1)
                        e.tensor_tensor(xt, xt, mask(C_ID), ALU.add).then_inc(S("xt_ready"), 1)

            with e.Fori(0, PAIRS) as j:
                def states(name, buf, store):
                    dram = lay(name).rearrange("a b h v k -> (a b h v) k")
                    for h in range(2):
                        d = dram[bass.ds(j * P + h * HEAD, HEAD), :]
                        t = buf[h * HEAD:(h + 1) * HEAD, h * HEAD:(h + 1) * HEAD]
                        move(d if store else t, t if store else d)

                e.wait_ge(S("rk_formed"), 1)
                e.sem_inc(S("rk_formed"), -1)
                e.wait_ge(S("e_pool"), 1)
                e.sem_inc(S("e_pool"), -1)
                e.tensor_tensor(RR, RR, SEG, ALU.mult)
                e.tensor_tensor(KF, KF, DD, ALU.mult).then_inc(S("pool_done"), 1)
                e.wait_ge(S("pool_done"), 1)
                e.sem_inc(S("pool_done"), -1)
                give(e, "rk_scaled")
                e.wait_ge(S("sin_free"), 1)
                e.sem_inc(S("sin_free"), -1)
                states("state_rwkv", SAMPLE_IN, False)
                moved(2)
                give(e, "state_in")
                for u in range(UNITS + 1):
                    level_masks(u)
                e.wait_ge(S("state_out"), 1)
                e.sem_inc(S("state_out"), -1)
                states("new_state_rwkv_prompt", SIO, True)
                e.wait_ge(S("state_out"), 1)
                e.sem_inc(S("state_out"), -1)
                states("new_state_rwkv_sample", SAMPLE_OUT, True)
                moved(4)
                give(e, "states_saved")
                e.wait_ge(S("y_ready"), 1)
                e.sem_inc(S("y_ready"), -1)
                move(mix_dram[:, bass.ds(j + 4, 1), :].rearrange("p a t -> p (a t)"), YY)
                moved()
                give(e, "y_saved")
            e.wait_ge(S("shc_ready"), 1)
            e.sem_inc(S("shc_ready"), -1)
            for g, out in ((0, "new_state_shift_prompt"), (1, "new_state_shift_sample")):
                o = lay(out).rearrange("a b c n -> (a b c) n")
                at = g * 64
                move(o[:, 0:14 * P].rearrange("a (b p) -> (a b) p", p=P), AUX[at:at + 14, 256:384])
                move(o[:, 14 * P:RWKV_PROJ], AUX[at + 14:at + 15, 256:288])
            moved(4)
            barrier(e, "pool")
            for b in range(DB):
                e.dma_start(R2[:, b, :], mix_dram[:, b, :]).then_inc(S(f"mix_in{b}"), 16)
            move(R1[:, :, :], x_spill)
            e.reg_add(mix_due, mix_due, 16)
            mixed = e.snap(mix_due, min_val=16)
            for b in range(DB):
                e.wait_ge(S(f"mix_in{b}"), mixed)
                give(e, "mix_act")
            moved()
            barrier(e, "pool")

            def mem_in(g, ksrc, vsrc):
                e.wait_ge(S("ckr_free"), 1)
                e.sem_inc(S("ckr_free"), -1)
                for dst, name in ((CKR, ksrc), (CV[g], vsrc)):
                    move(dst, lay(name).rearrange("a b (t m) h d -> m (a b t) (h d)", t=2))
                moved(2)
                give(e, "ckr_ready")

            mem_in(0, "new_mem_k_prompt", "new_mem_v_prompt")
            mem_in(1, "cache_mem_k", "cache_mem_v")
            barrier(e, "pool")
        barrier(e, "pool")

    @block.tensor
    def _(e):
        def claim(*banks):
            for b in banks:
                e.wait_ge(S(f"bank{b}"), 1)
                e.sem_inc(S(f"bank{b}"), -1)

        def transposes(items, b, name, base=0):
            claim(b)
            for n, (src, off) in enumerate(items):
                k, m = src.shape
                ins = e.matmul(PS[0:m, b * 512 + off:b * 512 + off + k], src, CST[0:k, C_ID:C_ID + k],
                               is_transpose=True, start=True, stop=True)
            ins.then_inc(S(name), 1)

        def products(out, lhs, rhs, n):
            first = True
            for k in range(n):
                for wp, xp in ((0, 0), (1, 0), (0, 1)):
                    ins = e.matmul(out, lhs(k, wp), rhs(k, xp), start=first, stop=(k == n - 1 and xp == 1))
                    first = False
            return ins

        def dense8(slot, b0, name, m=P, cw=CW, chunks=range(CH), first=True):
            if first:
                e.wait_ge(S(f"w_ready{slot}"), 1)
                e.sem_inc(S(f"w_ready{slot}"), -1)
            W = [x[:, slot, :].rearrange("p (k n) -> p k n", k=DB) for x in (WH, WL)]
            H = [HH, HL]
            for c in chunks:
                claim(b0 + c)
                products(PS[0:m, (b0 + c) * 512:(b0 + c) * 512 + cw], lambda k, p: W[p][:, k, 0:m],
                         lambda k, p: H[p][:, k, c * cw:(c + 1) * cw], DB).then_inc(S(name), 1)

        def dense_pair(names=("dense_psum", "dense_psum")):
            e.wait_ge(S("w_ready0"), 1)
            e.sem_inc(S("w_ready0"), -1)
            e.wait_ge(S("w_ready1"), 1)
            e.sem_inc(S("w_ready1"), -1)
            claim(0, 1, 2, 3, 4, 5)
            for k in range(DB):
                e.wait_ge(S("h_ready"), 1)
                e.sem_inc(S("h_ready"), -1)
                for s in range(2):
                    for c in range(CH):
                        for w, h in ((WH, HH), (WL, HH), (WH, HL)):
                            ins = e.matmul(bank(3 * s + c, 0, CW), w[:, s, k * P:(k + 1) * P], h[:, k, chunk(c)],
                                           start=(k == 0 and w is WH and h is HH), stop=(k == DB - 1 and h is HL))
                        if k == DB - 1:
                            ins.then_inc(S(names[s]), 1)

        def block_stats():
            claim(0, 1, 2)
            for b in range(DB):
                e.wait_ge(S("r1sq_ready"), 1)
                e.sem_inc(S("r1sq_ready"), -1)
                for c in range(CH):
                    ins = e.matmul(bank(c, 0, CW), mean, R2[:, b, chunk(c)], start=(b == 0), stop=(b == DB - 1))
                    if b == DB - 1:
                        ins.then_inc(S("var_psum"), 1)

        def stats(n=T):
            e.wait_ge(S("sq_sum"), 1)
            e.sem_inc(S("sq_sum"), -1)
            cw = CW if n == T else n
            for c in range(n // cw):
                claim(c)
                e.matmul(bank(c, 0, cw), mean, TMP[:, 2, c * cw:(c + 1) * cw], start=True, stop=True).then_inc(S("var_psum"), 1)

        e.wait_ge(S("cst_pe"), 1)
        e.sem_inc(S("cst_pe"), -1)

        def tokens_in(s, n):
            e.wait_ge(S(f"xin_full{s}"), 16)
            e.sem_inc(S(f"xin_full{s}"), -16)
            for g in range(2):
                transposes([(R2[0:n, s, (4 * g + b) * P:(4 * g + b + 1) * P], b * P) for b in range(4)], 2 * s + g, "xT_psum" if g == 0 else "xT_dve_psum")

        for s in range(2):
            tokens_in(s, P)
        with e.Fori(0, TILES // 2) as j:
            for s in range(2):
                tokens_in(s, P)
        tokens_in(0, DEC_SEQ)
        barrier(e, "pe")
        with e.Fori(0, DEPTH) as l:
            e.wait_ge(S("prm_rows_pe"), 1)
            e.sem_inc(S("prm_rows_pe"), -1)
            transposes([(PROW[0:PRM_ROWS, :], 0)], 7, "prm_psum")
            stats(MEM)
            e.wait_ge(S("h_ready"), DB)
            e.sem_inc(S("h_ready"), -DB)
            with e.Fori(0, 4) as i:
                for s in range(2):
                    dense8(s, 3 * s, "dense_psum", cw=MEM, chunks=(0,))
            e.wait_ge(S("kvT_ready"), 1)
            e.sem_inc(S("kvT_ready"), -1)
            for k in range(2):
                for tt in range(2):
                    transposes([(R2[:, k * 4 + b, MEM + tt * P:MEM + (tt + 1) * P], b * P) for b in range(4)], k * 2 + tt, "memtok_psum")
            stats()
            barrier(e, "pe")
            dense_pair()
            for n in range(8):
                dense8(n % 2, 3 * (n % 2), "dense_psum")
            e.wait_ge(S("cos_pe"), 1)
            e.sem_inc(S("cos_pe"), -1)

            def swapped(i, n):
                tok = bass.ds(i, n)
                claim(5, 6)
                e.matmul(PS[:, 2560:2560 + 4 * n].rearrange("p (a t) -> p a t", a=4), perm, R1[:, 0:4, tok], start=True, stop=True)
                e.matmul(PS[:, 3072:3072 + 2 * n].rearrange("p (a t) -> p a t", a=2), perm, R1[:, 4:6, tok], start=True, stop=True).then_inc(S("swap_psum"), 1)

            def scores(g, n, parts):
                if g == 0:
                    e.wait_ge(S("qk_ready"), 1)
                    e.sem_inc(S("qk_ready"), -1)
                p = slice(g * HEAD, (g + 1) * HEAD)
                for q in range(4):
                    if q % 2 == 0:
                        claim(2 + 3 * g + q // 2)
                    for ks, nk, col in parts:
                        keys = KR[p, q // 2, :, :].rearrange("p s t -> p (s t)") if len(parts) == 1 else KR[p, q // 2, ks, 0:nk]
                        at = 1024 + g * 1536 + q * 256 + col
                        ins = e.matmul(PS[0:n, at:at + nk], QR[p, q, 0:n], keys, start=True, stop=True)
                ins.then_inc(S("score_psum"), 1)

            def values(n):
                e.wait_ge(S("vst_ready"), 1)
                e.sem_inc(S("vst_ready"), -1)
                transposes([(VST[:, 0:n], 0)], 7, "v_psum")

            def by_key(g, n, parts):
                e.wait_ge(S("prob_ready"), 1)
                e.sem_inc(S("prob_ready"), -1)
                kparts = [(0, 0, P), (1, P, P)] if len(parts) == 1 else [(ks, col, nk) for ks, nk, col in parts]
                for b in range(2):
                    transposes([(SC[0:n, 4 * g + 2 * b + hh, col:col + nk], hh * 256 + kt * P) for hh in range(2)
                                for kt, (ks, col, nk) in enumerate(kparts)], b, "pT_psum")

            def weighted(g, n, parts):
                kparts = [(0, 0, P), (1, P, P)] if len(parts) == 1 else [(ks, col, nk) for ks, nk, col in parts]
                e.wait_ge(S("pT_ready"), 1)
                e.sem_inc(S("pT_ready"), -1)
                claim(4)
                for q in range(4):
                    for kt, (ks, col, nk) in enumerate(kparts):
                        vals = VCR if len(parts) == 2 and ks == 1 else VT[:, ks, :]
                        ins = e.matmul(PS[g * HEAD:(g + 1) * HEAD, 2048 + q * n:2048 + (q + 1) * n], vals[0:nk, (q // 2) * HEAD:(q // 2 + 1) * HEAD],
                                       PT[0:nk, 4 * g + q, kt, 0:n], start=(kt == 0), stop=(kt == 1))
                ins.then_inc(S("o_psum"), 1)

            def keys_out(n, slot):
                claim(0)
                for v in range(2):
                    ins = e.matmul(PS[0:n, v * HEAD:(v + 1) * HEAD], KR[0:HEAD, v, slot, 0:n], CST[0:HEAD, C_ID:C_ID + HEAD],
                                   is_transpose=True, start=True, stop=True)
                ins.then_inc(S("ko_psum"), 1)

            both = [(0, 256, 0)]

            def tile(i, last):
                if not last:
                    swapped(i, P)
                for g in range(2):
                    by_key(g, P, both)
                    if not last:
                        scores(g, P, both)
                for g in range(2):
                    weighted(g, P, both)
                if not last:
                    values(P)

            swapped(0, P)
            scores(0, P, both)
            scores(1, P, both)
            values(P)
            with e.Fori(0, TILES - 1) as i:
                tile(i * P + P, False)
            tile(None, True)
            keys_out(P, 1)
            e.wait_ge(S("cached_ready"), 1)
            e.sem_inc(S("cached_ready"), -1)
            for v in range(2):
                transposes([(KCR[v], 0)], v, "kc_psum")
            cached = [(0, DEC_SEQ, 0), (1, P, DEC_SEQ)]
            swapped(SEQ, DEC_SEQ)
            values(DEC_SEQ)
            for g in range(2):
                scores(g, DEC_SEQ, cached)
                by_key(g, DEC_SEQ, cached)
                weighted(g, DEC_SEQ, cached)
            keys_out(DEC_SEQ, 0)
            barrier(e, "pe")

            def by_token(u):
                t0, n, tiles, _ = unit(u)
                for x in range(tiles):
                    transposes([(R1[:, a, t0 + x * n:t0 + (x + 1) * n], o * P) for o, a in enumerate((0, 2, 3, 4))], x, "tm_psum")

            def scores(u, x):
                t0, n, _, _ = unit(u)
                tok = slice(t0 + x * n, t0 + (x + 1) * n)
                for h in range(2):
                    p = slice(h * HEAD, (h + 1) * HEAD)
                    b = 2 + h - 2 * x
                    claim(b)
                    out = PS[0:n, b * 512:b * 512 + 4 * n].rearrange("p (a t) -> p a t", a=4)
                    e.matmul(out[:, 0:4:3, :], R1[p, 2, tok], R1[p, 0:2, tok], start=True, stop=True)
                    e.matmul(out[:, 1:3, :], R1[p, 3, tok], R1[p, 0:2, tok], start=True, stop=True).then_inc(S("sm_psum"), 1)

            def low(u):
                t0, n, tiles, _ = unit(u)
                for h in range(2):
                    p = slice(h * HEAD, (h + 1) * HEAD)
                    claim(2 + h)
                    for x in range(tiles):
                        tok = slice(t0 + x * n, t0 + (x + 1) * n)
                        at = (2 + h) * 512 + x * n
                        ins = e.matmul(PS[0:n, at:at + n], R1[p, 0, tok], R1[p, 2, tok], start=True, stop=True)
                    ins.then_inc(S("l_psum"), 1)

            def value_parts(u):
                _, n, tiles, _ = unit(u)
                e.wait_ge(S("tm_ready"), 1)
                e.sem_inc(S("tm_ready"), -1)
                e.wait_ge(S("sm_ready"), 1)
                e.sem_inc(S("sm_ready"), -1)
                yb = (4, 7)[u % 2]
                claim(yb)
                for x in range(tiles):
                    for h in range(2):
                        e.matmul(PS[h * HEAD:(h + 1) * HEAD, yb * 512 + x * n:yb * 512 + (x + 1) * n], bkv(u)[0:n, x, 2, h * HEAD:(h + 1) * HEAD],
                                 heads(LTM, 1024, n, tiles)[:, 2 * x + h, :], start=(x == 0), stop=False, skip_group_check=True)
                claim(3)
                for x in range(tiles):
                    for h in range(2):
                        at = 1536 + x * P + h * HEAD
                        ins = e.matmul(PS[0:n, at:at + HEAD], heads(LTM, 512, n, tiles)[:, 2 * x + h, :], bkv(u)[0:n, x, 2, h * HEAD:(h + 1) * HEAD],
                                       start=True, stop=True)
                ins.then_inc(S("mv_psum"), 1)

            def level_left(u, s):
                _, n, tiles, _ = unit(u)
                e.wait_ge(S("elt_ready"), 1)
                e.sem_inc(S("elt_ready"), -1)
                e.wait_ge(S("x_ready"), 1)
                e.sem_inc(S("x_ready"), -1)
                for x in range(tiles):
                    if s == 0:
                        claim(2 + x)
                    for h in range(2):
                        g, at = 2 * x + h, (2 + x) * 512 + h * n
                        ins = e.matmul(PS[0:n, at:at + n], heads(ELF, (s % 2) * 512, n, tiles)[:, g, :],
                                       heads(XXF, 0, n, tiles)[:, g, :], start=True, stop=True)
                    ins.then_inc(S("t1_psum"), 1)

            def level_right(u, s):
                _, n, tiles, levels = unit(u)
                xt, t1 = heads(XXF, 512, n, tiles), heads(T1F, 0, n, tiles)
                e.wait_ge(S("xt_ready"), 1)
                e.sem_inc(S("xt_ready"), -1)
                if s == 0:
                    claim(0, 1)
                if s < levels - 1:
                    for x in range(tiles):
                        e.wait_ge(S("t1_ready"), 1)
                        e.sem_inc(S("t1_ready"), -1)
                        for g in (2 * x, 2 * x + 1):
                            ins = e.matmul(PS[0:n, g * n:(g + 1) * n], xt[:, g, :], t1[:, g, :], start=True, stop=True)
                    ins.then_inc(S("dx_psum"), 1)
                else:
                    e.wait_ge(S("t1_ready"), tiles)
                    e.sem_inc(S("t1_ready"), -tiles)
                for g in range(2 * tiles):
                    ins = e.matmul(PS[0:n, 512 + g * n:512 + (g + 1) * n], t1[:, g, :], xt[:, g, :], start=True, stop=True)
                ins.then_inc(S("dx_psum"), 1)

            def solved(u):
                _, n, tiles, _ = unit(u)
                xt = heads(XXF, 512, n, tiles)
                e.wait_ge(S("xt_ready"), 1)
                e.sem_inc(S("xt_ready"), -1)
                give(e, "bank0", "bank1")
                for x in range(tiles):
                    for h in range(2):
                        ins = e.matmul(PS[h * HEAD:(h + 1) * HEAD, 1024 + x * n:1024 + (x + 1) * n], ATM[0:n, x, h * HEAD:(h + 1) * HEAD],
                                       xt[:, 2 * x + h, :], start=True, stop=True)
                ins.then_inc(S("pts_psum"), 1)
                e.wait_ge(S("mv_ready"), 1)
                e.sem_inc(S("mv_ready"), -1)
                if tiles == 1:
                    claim(3)
                for x in range(tiles):
                    for h in range(2):
                        at = 1536 + x * P + h * HEAD
                        ins = e.matmul(PS[0:n, at:at + HEAD], xt[:, 2 * x + h, :], MVS[0:n, x, h * HEAD:(h + 1) * HEAD], start=True, stop=True)
                ins.then_inc(S("q_psum"), 1)

            def chunk_u(u, c):
                t0, n, _, _ = unit(u)
                cn, x, yb = min(n, CHUNK), c // 2, (4, 7)[u % 2]
                a = (c % 2) * CHUNK
                if c == 0:
                    e.wait_ge(S("pq_ready"), 1)
                    e.sem_inc(S("pq_ready"), -1)
                e.wait_ge(S("state_ready"), 1)
                e.sem_inc(S("state_ready"), -1)
                e.matmul(PS[a:a + cn, 3072:3072 + P], PTS[:, x, a:a + cn], SBD, start=True, stop=True).then_inc(S("u_psum"), 1)
                e.matmul(PS[:, yb * 512 + c * CHUNK:yb * 512 + c * CHUNK + cn], SBD, RR[:, t0 + c * CHUNK:t0 + c * CHUNK + cn],
                         start=False, stop=False, skip_group_check=True)

            def chunk_state(u, c):
                _, n, _, _ = unit(u)
                r, x = slice((c % 2) * CHUNK, (c % 2) * CHUNK + min(n, CHUNK)), c // 2
                e.wait_ge(S("u_ready"), 1)
                e.sem_inc(S("u_ready"), -1)
                e.matmul(PS[:, 2560:2560 + P], bkv(u)[r, x, 1, :], bkv(u)[r, x, 2, :], start=True, stop=False)
                e.matmul(PS[:, 2560:2560 + P], bkv(u)[r, x, 0, :], US[r, x, :], start=False, stop=True).then_inc(S("ds_psum"), 1)

            def outputs(u):
                _, n, tiles, _ = unit(u)
                yb = (4, 7)[u % 2]
                for x in range(tiles):
                    for h in range(2):
                        ins = e.matmul(PS[h * HEAD:(h + 1) * HEAD, yb * 512 + x * n:yb * 512 + (x + 1) * n], US[0:n, x, h * HEAD:(h + 1) * HEAD],
                                       heads(tflat, 1536 + (u % 2) * 512, n, tiles)[:, 2 * x + h, :], start=False, stop=True, skip_group_check=True)
                ins.then_inc(S("y_psum"), 1)

            with e.Fori(0, PAIRS) as j:
                dense8(0, 0, "dense_psum")
                e.wait_ge(S("lw_ready"), 1)
                e.sem_inc(S("lw_ready"), -1)
                for c in range(CH):
                    claim(3 + c)
                    e.matmul(bank(3 + c, 0, CW), LW[0:64, 0:P], TWA[0:64, chunk(c)], start=True, stop=True).then_inc(S("z_psum"), 1)
                for c in range(CH):
                    claim(c)
                    e.matmul(bank(c, 0, CW), LW[64:128, 0:P], TWA[64:128, chunk(c)], start=True, stop=True).then_inc(S("z_psum"), 1)
                for c in range(CH):
                    claim(3 + c)
                    e.matmul(bank(3 + c, 0, CW), LW[:, P:2 * P], SG1[:, chunk(c)], start=True, stop=False)
                    e.matmul(bank(3 + c, 0, CW), LW[0:32, 2 * P:3 * P], SG2[0:32, chunk(c)], start=False, stop=True).then_inc(S("z_psum"), 1)
                dense8(0, 0, "dense_psum")
                dense8(1, 3, "dense_psum", chunks=(0, 1))
                e.wait_ge(S("kksq_ready"), 1)
                e.sem_inc(S("kksq_ready"), -1)
                for c in range(CH):
                    claim(c)
                    e.matmul(bank(c, 0, CW), cst(C_BD), TMP[:, 0, chunk(c)], start=True, stop=True).then_inc(S("kk_psum"), 1)
                dense8(1, 3, "dense_psum", chunks=(2,), first=False)
                e.wait_ge(S("rk_ready"), 1)
                e.sem_inc(S("rk_ready"), -1)
                for c in range(CH):
                    claim(3 + c)
                    e.matmul(bank(3 + c, 0, CW), cst(C_BD), TMP[:, 1, chunk(c)], start=True, stop=True).then_inc(S("rk_psum"), 1)
                e.wait_ge(S("til_ready"), 1)
                e.sem_inc(S("til_ready"), -1)
                claim(5, 6)
                for u in range(UNITS + 1):
                    _, _, tiles, levels = unit(u)
                    by_token(u)
                    if u > 0:
                        chunk_u(u - 1, 0)
                    scores(u, 0)
                    if u > 0:
                        chunk_state(u - 1, 0)
                    if tiles == 2:
                        scores(u, 1)
                    low(u)
                    value_parts(u)
                    for s in range(levels):
                        level_left(u, s)
                        if u > 0 and s < 3:
                            chunk_u(u - 1, s + 1)
                        level_right(u, s)
                        if u > 0 and s < 3:
                            chunk_state(u - 1, s + 1)
                    if u > 0:
                        outputs(u - 1)
                    solved(u)

                def state_out():
                    e.wait_ge(S("state_ready"), 1)
                    e.sem_inc(S("state_ready"), -1)
                    transposes([(SBD, 0)], 0, "sio_psum")

                state_out()
                e.wait_ge(S("state_in"), 1)
                e.sem_inc(S("state_in"), -1)
                transposes([(SAMPLE_IN, 0)], 1, "sin_psum")
                chunk_u(UNITS, 0)
                chunk_state(UNITS, 0)
                outputs(UNITS)
                state_out()
                give(e, "bank5", "bank6")
                e.wait_ge(S("yy_ready"), 1)
                e.sem_inc(S("yy_ready"), -1)
                for c in range(CH):
                    claim(c)
                    e.matmul(bank(c, 0, CW), cst(C_CEN), YY[:, chunk(c)], start=True, stop=True).then_inc(S("yc_psum"), 1)
                e.wait_ge(S("ysq_ready"), 1)
                e.sem_inc(S("ysq_ready"), -1)
                for c in range(CH):
                    claim(3 + c)
                    e.matmul(bank(3 + c, 0, CW), cst(C_BDM), TMP[:, 0, chunk(c)], start=True, stop=True).then_inc(S("var_psum"), 1)
            e.wait_ge(S("shc_full"), 1)
            e.sem_inc(S("shc_full"), -1)
            claim(0)
            for g in range(2):
                ins = e.matmul(PS[g * 64:g * 64 + 16, 0:P], SHC[:, g * 16:(g + 1) * 16], ident, start=True, stop=True)
            ins.then_inc(S("shc_psum"), 1)
            barrier(e, "pe")
            dense_pair()
            with e.Fori(0, 3) as i:
                for s in range(2):
                    dense8(s, 3 * s, "dense_psum")
            stats()
            barrier(e, "pe")
            block_stats()
            dense_pair()
            for s in range(2):
                dense8(s, 3 * s, "dense_psum")

            def mem_keys():
                e.wait_ge(S("ckr_ready"), 1)
                e.sem_inc(S("ckr_ready"), -1)
                for kt in range(2):
                    transposes([(CKR[:, kt, h * P:(h + 1) * P], h * P) for h in range(4)], 6 + kt, "ckt_psum")
                e.wait_ge(S("ckt_ready"), 1)
                e.sem_inc(S("ckt_ready"), -1)

            def cross_scores(n):
                e.wait_ge(S("cq_ready"), 1)
                e.sem_inc(S("cq_ready"), -1)
                claim(0, 1)
                for h in range(4):
                    ins = e.matmul(PS[0:n, h * MEM:(h + 1) * MEM], CQ[:, h, 0:n], CKT[:, h, :], start=True, stop=True)
                ins.then_inc(S("cs_psum"), 1)

            def cross_sums(n, group=0):
                e.wait_ge(S("cp_ready"), 1)
                e.sem_inc(S("cp_ready"), -1)
                for g in range(2):
                    transposes([(CP[0:n, 2 * g + hh, kt * P:(kt + 1) * P], (hh * 2 + kt) * P) for hh in range(2) for kt in range(2)], 2 + g, "cpt_psum")
                e.wait_ge(S("cpt_ready"), 1)
                e.sem_inc(S("cpt_ready"), -1)
                claim(4)
                for h in range(4):
                    for kt in range(2):
                        ins = e.matmul(PS[:, 2048 + h * n:2048 + (h + 1) * n], CV[group][:, kt, h * P:(h + 1) * P], CPT[:, h, kt, 0:n],
                                       start=(kt == 0), stop=(kt == 1))
                ins.then_inc(S("co_psum"), 1)

            mem_keys()
            cross_scores(P)
            with e.Fori(0, TILES - 1) as t:
                cross_scores(P)
                cross_sums(P)
            cross_sums(P)
            mem_keys()
            cross_scores(DEC_SEQ)
            cross_sums(DEC_SEQ, 1)
            e.wait_ge(S("ch_ready"), 1)
            e.sem_inc(S("ch_ready"), -1)
            with e.Fori(0, 2) as i:
                for s in range(2):
                    e.wait_ge(S(f"w_ready{s}"), 1)
                    e.sem_inc(S(f"w_ready{s}"), -1)
                    W = [x[:, s, :].rearrange("p (k n) -> p k n", k=4) for x in (WH, WL)]
                    for o in range(2):
                        for c in range(CH):
                            claim(3 * o + c)
                            products(bank(3 * o + c, 0, CW), lambda k, p: W[p][:, k, o * P:(o + 1) * P],
                                     lambda k, p: (HH, HL)[p][:, k, chunk(c)], 4).then_inc(S("dense_psum"), 1)
            stats()
            barrier(e, "pe")
            block_stats()

            def gate_up():
                dense8(0, 0, "gate_psum")
                dense8(1, 3, "up_psum")

            def down():
                for c in range(CH):
                    e.wait_ge(S("g_ready"), 1)
                    e.sem_inc(S("g_ready"), -1)
                    for k in range(2):
                        if c == 0:
                            e.wait_ge(S(f"w_ready{k}"), 1)
                            e.sem_inc(S(f"w_ready{k}"), -1)
                        for m in range(DB):
                            b = DOWN_BANKS[m]
                            if k == 0:
                                claim(b)
                            for w, g in ((WH, GH), (WL, GH), (WH, GL)):
                                ins = e.matmul(bank(b, 0, CW), w[:, k, m * P:(m + 1) * P], g[:, k, chunk(c)],
                                               start=(k == 0 and w is WH and g is GH), stop=(k == 1 and g is GL))
                            if k == 1:
                                ins.then_inc(S("down_psum"), 1)
                            elif m == DB - 1 and c == CH - 1:
                                ins.then_inc(S("w0_used"), 1)

            dense_pair(("gate_psum", "up_psum"))
            gate_up()
            down()
            with e.Fori(1, FB // 2) as i:
                for f in range(2):
                    gate_up()
                down()
            stats()
            barrier(e, "pe")

        def tokens_out(s, n):
            e.wait_ge(S("xo_ready"), 1)
            e.sem_inc(S("xo_ready"), -1)
            for g in range(2):
                transposes([(R2[:, s, 0:1024].rearrange("p (b t) -> p b t", b=8)[:, 4 * g + b, 0:n], b * P) for b in range(4)], 2 * s + g, "xo_psum")

        with e.Fori(0, TILES // 2) as j:
            for s in range(2):
                tokens_out(s, P)
        tokens_out(0, DEC_SEQ)

    @block.scalar
    def _(e):
        def copy(dst, src):
            return e.copy(dst, src)

        def split(slot):
            e.wait_ge(S(f"w_full{slot}"), 16)
            e.sem_inc(S(f"w_full{slot}"), -16)
            copy(WH[:, slot, :], WRAW[:, slot, :]).then_inc(S(f"wh_ready{slot}"), 1)

        def evac(slot, dst, m=P, cw=CW, ch=CH, name="dense_psum", b0=None, then=True):
            b0 = 3 * slot if b0 is None else b0
            for c in range(ch):
                e.wait_ge(S(name), 1)
                e.sem_inc(S(name), -1)
                for out, a, z in dst(c):
                    ins = copy(out, PS[0:m, (b0 + c) * 512 + a:(b0 + c) * 512 + z])
                ins.then_inc(S("act_done"), 1)
                e.wait_ge(S("act_done"), 1)
                e.sem_inc(S("act_done"), -1)
                give(e, f"bank{b0 + c}")
            if then:
                split(slot)

        def inverse_root(dst, b0, eps, n=T):
            cw = CW if n == T else n
            for c in range(n // cw):
                e.wait_ge(S("var_psum"), 1)
                e.sem_inc(S("var_psum"), -1)
                e.activation(dst[:, c * cw:(c + 1) * cw], bank(b0 + c, 0, cw), ACT.Ln, bias=CST[:, eps:eps + 1]).then_inc(S("act_done"), 1)
                e.wait_ge(S("act_done"), 1)
                e.sem_inc(S("act_done"), -1)
                give(e, f"bank{b0 + c}")
            e.activation(dst[:, 0:n], dst[:, 0:n], ACT.Exp, scale=-0.5).then_inc(S("rms_ready"), 1)

        def square(src, s, n=T):
            e.wait_ge(S("sq_free"), 1)
            e.sem_inc(S("sq_free"), -1)
            e.activation(TMP[:, s, 0:n], src, ACT.Square).then_inc(S("sq_ready"), 1)

        def squares(src, n=T):
            for b in range(DB):
                square(src[:, b, 0:n], b % 2, n)
            root_means(n)

        def root_means(n=T):
            inverse_root(TMP[:, 0, :], 0, C_EPS, n)

        def block_squares():
            for b in range(DB):
                e.wait_ge(S("r1_ready"), 1)
                e.sem_inc(S("r1_ready"), -1)
                e.activation(R2[:, b, :], R1[:, b, :], ACT.Square).then_inc(S("r1sq_ready"), 1)
            root_means()

        def highs(src, n=T):
            for b in range(DB):
                e.wait_ge(S("ht_ready"), 1)
                e.sem_inc(S("ht_ready"), -1)
                copy(HH[:, b, 0:n], src(b)[:, 0:n]).then_inc(S("hh_ready"), 1)

        in_tmp = lambda b: TMP[:, 1 + b % 2, :]
        in_r2 = lambda b: R2[:, b, :]

        e.wait_ge(S("cst_act"), 1)
        e.sem_inc(S("cst_act"), -1)
        for b in range(8):
            give(e, f"bank{b}")

        def tokens_in(s, n, dst):
            e.wait_ge(S("xT_psum"), 1)
            e.sem_inc(S("xT_psum"), -1)
            copy(dst, bank(2 * s).rearrange("p (b t) -> p b t", b=4)[:, :, 0:n]).then_inc(S("act_done"), 1)
            e.wait_ge(S("act_done"), 1)
            e.sem_inc(S("act_done"), -1)
            give(e, f"bank{2 * s}", "xin_act")

        give(e, "sq_free", "sq_free", "ot_free", "elt_free", "elt_free", "sc_free", "sc_free")
        for s in range(2):
            tokens_in(s, P, MEMT[:, 0:4, s * P:(s + 1) * P])
        give(e, "memT_ready_act")
        with e.Fori(0, TILES // 2) as j:
            for s in range(2):
                tokens_in(s, P, R1[:, 0:4, bass.ds((j * 2 + s) * P, P)])
        tokens_in(0, DEC_SEQ, R1[:, 0:4, SEQ:T])
        barrier(e, "act")
        split(0)
        split(1)
        with e.Fori(0, DEPTH) as l:
            e.wait_ge(S("prm_psum"), 1)
            e.sem_inc(S("prm_psum"), -1)
            ins = copy(PRM[:, :], PS[:, 3584:3584 + PRM_ROWS])
            ins.then_inc(S("act_done"), 1)
            e.wait_ge(S("act_done"), 1)
            e.sem_inc(S("act_done"), -1)
            give(e, "bank7", "prm_ready")
            e.wait_ge(S("memT_act"), 1)
            e.sem_inc(S("memT_act"), -1)
            squares(R2, MEM)
            highs(in_tmp, MEM)
            with e.Fori(0, 4) as i:
                for s in range(2):
                    evac(s, lambda c: [(R2[:, bass.ds(i * 2 + s, 1), MEM:2 * MEM].rearrange("p a m -> p (a m)"), 0, MEM)], cw=MEM, ch=1)
                    square(R1[:, bass.ds(i * 2 + s, 1), :].rearrange("p a t -> p (a t)"), s)
            give(e, "kvT_ready")
            for k in range(4):
                e.wait_ge(S("memtok_psum"), 1)
                e.sem_inc(S("memtok_psum"), -1)
                ins = copy(R2[:, 2 + k, 512:1024], bank(k))
                ins.then_inc(S("act_done"), 1)
                e.wait_ge(S("act_done"), 1)
                e.sem_inc(S("act_done"), -1)
                give(e, f"bank{k}", "memtok_ready")
            root_means()
            barrier(e, "act")
            highs(in_tmp)
            with e.Fori(0, 2) as i:
                for s in range(2):
                    evac(s, lambda c: [(R1[:, bass.ds(i * 2 + s, 1), chunk(c)].rearrange("p a t -> p (a t)"), 0, CW)])
            for s in range(2):
                evac(s, lambda c: [(R1[:, 4 + s, chunk(c)], 0, CW)])
            evac(0, lambda c: [(R1[:, 6, chunk(c)], 0, CW)])

            def raw(m=P):
                def dst(c):
                    if c < CH - 1:
                        return [(PRAW[0:m, 1 + c * CW:1 + (c + 1) * CW], 0, CW)]
                    w = SEQ - c * CW
                    return [(PRAW[0:m, 1 + c * CW:1 + SEQ], 0, w), (PRAW[0:m, SEQ + 2:T + 2], w, CW)]
                return dst

            for n, (s, m) in enumerate(((1, P), (0, P), (1, 32))):
                e.wait_ge(S("praw_free"), 1)
                e.sem_inc(S("praw_free"), -1)
                evac(s, raw(m), m=m)
                give(e, "praw_ready")
            e.wait_ge(S("lora_ready"), 1)
            e.sem_inc(S("lora_ready"), -1)
            e.activation(TWA[0:64, :], TWA[0:64, :], ACT.Tanh).then_inc(S("act_done"), 1)
            e.wait_ge(S("act_done"), 1)
            e.sem_inc(S("act_done"), -1)
            e.activation(SG1, SG1, ACT.Sigmoid).then_inc(S("act_done"), 1)
            e.wait_ge(S("act_done"), 1)
            e.sem_inc(S("act_done"), -1)
            e.activation(SG2[0:32, :], SG2[0:32, :], ACT.Sigmoid).then_inc(S("act_done"), 1)
            e.wait_ge(S("act_done"), 1)
            e.sem_inc(S("act_done"), -1)

            def exps(g, n, width):
                at = g * 20
                e.wait_ge(S("nm_ready"), 1)
                e.sem_inc(S("nm_ready"), -1)
                for q in range(4):
                    h = 4 * g + q
                    e.activation(SC[0:n, h, 0:width], SC[0:n, h, 0:width], ACT.Exp, bias=ST[0:n, at + 4 + q:at + 5 + q], scale=1.0,
                                 accum_out=ST[0:n, at + 8 + q:at + 9 + q])
                e.activation(ST[0:n, at + 12:at + 16], ST[0:n, at + 12:at + 16], ACT.Exp).then_inc(S("exp_ready"), 1)

            def value_stage(i, n):
                copy(VST[:, 0:n], R1[:, 6, bass.ds(i, n)]).then_inc(S("vst_ready"), 1)

            def values(n, slot):
                e.wait_ge(S("v_psum"), 1)
                e.sem_inc(S("v_psum"), -1)
                copy(VT[0:n, slot, :], PS[0:n, 3584:3584 + P]).then_inc(S("act_done"), 1)
                e.wait_ge(S("act_done"), 1)
                e.sem_inc(S("act_done"), -1)
                give(e, "bank7")

            def by_key(g, n, kts):
                for b in range(2):
                    e.wait_ge(S("pT_psum"), 1)
                    e.sem_inc(S("pT_psum"), -1)
                    for kt, nk in enumerate(kts):
                        src = bank(b).rearrange("p (h k q) -> p h k q", h=2, k=2)
                        at = 4 * g + 2 * b
                        ins = copy(PT[0:nk, at:at + 2, kt, 0:n], src[0:nk, :, kt, 0:n])
                    ins.then_inc(S("act_done"), 1)
                    e.wait_ge(S("act_done"), 1)
                    e.sem_inc(S("act_done"), -1)
                    give(e, f"bank{b}")
                give(e, "pT_ready", "sc_free")

            def weighted(g, n):
                if g == 0:
                    e.wait_ge(S("ot_free"), 1)
                    e.sem_inc(S("ot_free"), -1)
                e.wait_ge(S("o_psum"), 1)
                e.sem_inc(S("o_psum"), -1)
                p = slice(g * HEAD, (g + 1) * HEAD)
                copy(OT[p, :, 0:n], PS[p, 2048:2048 + 4 * n].rearrange("p (a t) -> p a t", a=4)).then_inc(S("act_done"), 1)
                e.wait_ge(S("act_done"), 1)
                e.sem_inc(S("act_done"), -1)
                give(e, "bank4")
                if g == 1:
                    give(e, "ot_ready")

            def keys_out(n):
                e.wait_ge(S("ko_psum"), 1)
                e.sem_inc(S("ko_psum"), -1)
                copy(KO[0:n, :], PS[0:n, 0:P]).then_inc(S("act_done"), 1)
                e.wait_ge(S("act_done"), 1)
                e.sem_inc(S("act_done"), -1)
                give(e, "bank0", "ko_ready")

            def tile(i, slot, last):
                if not last:
                    value_stage(i, P)
                for g in range(2):
                    by_key(g, P, (P, P))
                for g in range(2):
                    if not last:
                        exps(g, P, 256)
                    weighted(g, P)
                if not last:
                    values(P, slot)

            value_stage(0, P)
            values(P, 0)
            exps(0, P, 256)
            exps(1, P, 256)
            with e.Fori(0, TILES // 2 - 1) as i:
                tile((i * 2 + 1) * P, 1, False)
                tile((i * 2 + 2) * P, 0, False)
            tile(SEQ - P, 1, False)
            tile(None, None, True)
            keys_out(P)
            for v in range(2):
                e.wait_ge(S("kc_psum"), 1)
                e.sem_inc(S("kc_psum"), -1)
                copy(KR[:, v, 1, :], PS[:, v * 512:v * 512 + P]).then_inc(S("act_done"), 1)
                e.wait_ge(S("act_done"), 1)
                e.sem_inc(S("act_done"), -1)
                give(e, f"bank{v}")
            give(e, "kc_ready")
            value_stage(SEQ, DEC_SEQ)
            values(DEC_SEQ, 0)
            for g in range(2):
                exps(g, DEC_SEQ, DEC_SEQ + P)
                by_key(g, DEC_SEQ, (DEC_SEQ, P))
                weighted(g, DEC_SEQ)
            e.wait_ge(S("ko_free"), 1)
            e.sem_inc(S("ko_free"), -1)
            keys_out(DEC_SEQ)
            barrier(e, "act")

            def by_token(u):
                _, n, tiles, _ = unit(u)
                for x in range(tiles):
                    e.wait_ge(S("tm_psum"), 1)
                    e.sem_inc(S("tm_psum"), -1)
                    copy(ATM[0:n, x, :], PS[0:n, x * 512:x * 512 + P])
                    copy(bkv(u)[0:n, x, :, :], PS[0:n, x * 512 + P:(x + 1) * 512].rearrange("p (a t) -> p a t", a=3)).then_inc(S("act_done"), 1)
                    e.wait_ge(S("act_done"), 1)
                    e.sem_inc(S("act_done"), -1)
                    give(e, f"bank{x}")
                give(e, "tm_ready")
                e.wait_ge(S("mv_psum"), 1)
                e.sem_inc(S("mv_psum"), -1)
                copy(MVS[0:n, 0:tiles, :], PS[0:n, 1536:1536 + tiles * P].rearrange("p (x t) -> p x t", x=tiles)).then_inc(S("act_done"), 1)
                e.wait_ge(S("act_done"), 1)
                e.sem_inc(S("act_done"), -1)
                give(e, "bank3", "mv_ready")

            def levels_left(u):
                _, n, tiles, levels = unit(u)
                for s in range(levels):
                    for x in range(tiles):
                        e.wait_ge(S("t1_psum"), 1)
                        e.sem_inc(S("t1_psum"), -1)
                        if x == tiles - 1:
                            give(e, "elt_free")
                        w = slice(2 * x * n, 2 * (x + 1) * n)
                        copy(T1F[0:n, w], PS[0:n, (2 + x) * 512:(2 + x) * 512 + 2 * n]).then_inc(S("t1_ready"), 1)

            def solved(u):
                _, n, tiles, _ = unit(u)
                e.wait_ge(S("pts_psum"), 1)
                e.sem_inc(S("pts_psum"), -1)
                copy(PTS[:, 0:tiles, 0:n], PS[:, 1024:1024 + tiles * n].rearrange("p (x t) -> p x t", x=tiles)).then_inc(S("act_done"), 1)
                e.wait_ge(S("act_done"), 1)
                e.sem_inc(S("act_done"), -1)
                give(e, "bank2")
                e.wait_ge(S("q_psum"), 1)
                e.sem_inc(S("q_psum"), -1)
                copy(QS[0:n, 0:tiles, :], PS[0:n, 1536:1536 + tiles * P].rearrange("p (x t) -> p x t", x=tiles)).then_inc(S("act_done"), 1)
                e.wait_ge(S("act_done"), 1)
                e.sem_inc(S("act_done"), -1)
                give(e, "bank3", "pq_ready", "q_ready")

            def outputs(u):
                t0, n, tiles, _ = unit(u)
                yb = (4, 7)[u % 2]
                e.wait_ge(S("y_psum"), 1)
                e.sem_inc(S("y_psum"), -1)
                copy(YY[:, t0:t0 + tiles * n], PS[:, yb * 512:yb * 512 + tiles * n]).then_inc(S("act_done"), 1)
                e.wait_ge(S("act_done"), 1)
                e.sem_inc(S("act_done"), -1)
                give(e, f"bank{yb}")

            with e.Fori(0, PAIRS) as j:
                def raw_out(slot, then=True):
                    e.wait_ge(S("praw_free"), 1)
                    e.sem_inc(S("praw_free"), -1)
                    evac(slot, raw(), then=then)
                    give(e, "praw_ready")

                raw_out(0)
                e.wait_ge(S("pc_ready"), 1)
                e.sem_inc(S("pc_ready"), -1)
                for c in range(CH):
                    e.wait_ge(S("z_psum"), 1)
                    e.sem_inc(S("z_psum"), -1)
                    e.activation(DD2[:, chunk(c)], bank(3 + c, 0, CW), ACT.Sigmoid, bias=PC[:, 3:4]).then_inc(S("act_done"), 1)
                    e.wait_ge(S("act_done"), 1)
                    e.sem_inc(S("act_done"), -1)
                    give(e, f"bank{3 + c}")
                for c in range(CH):
                    e.wait_ge(S("z_psum"), 1)
                    e.sem_inc(S("z_psum"), -1)
                    e.activation(BB[:, chunk(c)], bank(c, 0, CW), ACT.Sigmoid, bias=PC[:, 4:5]).then_inc(S("act_done"), 1)
                    e.wait_ge(S("act_done"), 1)
                    e.sem_inc(S("act_done"), -1)
                    give(e, f"bank{c}")
                give(e, "sig_ready")
                for c in range(CH):
                    e.wait_ge(S("z_psum"), 1)
                    e.sem_inc(S("z_psum"), -1)
                    copy(GG[:, chunk(c)], bank(3 + c, 0, CW)).then_inc(S("act_done"), 1)
                    e.wait_ge(S("act_done"), 1)
                    e.sem_inc(S("act_done"), -1)
                    give(e, f"bank{3 + c}")
                split(1)
                e.wait_ge(S("dd_ready"), 1)
                e.sem_inc(S("dd_ready"), -1)
                e.activation(SEG, DD, ACT.Exp, scale=-DECAY)
                e.activation(DD2, DD2, ACT.Exp, scale=-DECAY)
                e.activation(DD, DD, ACT.Exp, scale=DECAY)
                e.activation(EC[:, 20:38], EC[:, 0:18], ACT.Exp, scale=-DECAY).then_inc(S("act_done"), 1)
                e.wait_ge(S("act_done"), 1)
                e.sem_inc(S("act_done"), -1)
                give(e, "e_ready", "e_pool")
                raw_out(0)
                e.wait_ge(S("kkr_ready"), 1)
                e.sem_inc(S("kkr_ready"), -1)
                e.activation(TMP[:, 0, :], KK, ACT.Square).then_inc(S("kksq_ready"), 1)
                raw_out(1, then=False)
                e.wait_ge(S("kkn_ready"), 1)
                e.sem_inc(S("kkn_ready"), -1)
                e.activation(TMP[:, 2, :], TMP[:, 2, :], ACT.Ln).then_inc(S("act_done"), 1)
                e.wait_ge(S("act_done"), 1)
                e.sem_inc(S("act_done"), -1)
                e.activation(TMP[:, 2, :], TMP[:, 2, :], ACT.Exp, scale=-0.5).then_inc(S("kks_ready"), 1)
                split(1)
                for u in range(UNITS + 1):
                    by_token(u)
                    levels_left(u)
                    if u > 0:
                        outputs(u - 1)
                    solved(u)

                def state_out(dst):
                    e.wait_ge(S("sio_psum"), 1)
                    e.sem_inc(S("sio_psum"), -1)
                    copy(dst, PS[:, 0:P]).then_inc(S("act_done"), 1)
                    e.wait_ge(S("act_done"), 1)
                    e.sem_inc(S("act_done"), -1)
                    give(e, "bank0", "state_out")

                state_out(SIO)
                outputs(UNITS)
                state_out(SAMPLE_OUT)
                give(e, "yy_ready")
                for c in range(CH):
                    e.wait_ge(S("yc_psum"), 1)
                    e.sem_inc(S("yc_psum"), -1)
                    copy(TMP[:, 1, chunk(c)], bank(c, 0, CW)).then_inc(S("act_done"), 1)
                    e.wait_ge(S("act_done"), 1)
                    e.sem_inc(S("act_done"), -1)
                    give(e, f"bank{c}")
                e.activation(TMP[:, 0, :], TMP[:, 1, :], ACT.Square).then_inc(S("act_done"), 1)
                e.wait_ge(S("act_done"), 1)
                e.sem_inc(S("act_done"), -1)
                give(e, "ysq_ready")
                inverse_root(TMP[:, 2, :], 3, C_EPS + 1)
            e.wait_ge(S("shc_psum"), 1)
            e.sem_inc(S("shc_psum"), -1)
            for g in range(2):
                ins = copy(AUX[g * 64:g * 64 + 16, 256:384], PS[g * 64:g * 64 + 16, 0:P])
            ins.then_inc(S("act_done"), 1)
            e.wait_ge(S("act_done"), 1)
            e.sem_inc(S("act_done"), -1)
            give(e, "bank0", "shc_ready")
            barrier(e, "act")
            for b in range(DB):
                e.wait_ge(S("mix_act"), 1)
                e.sem_inc(S("mix_act"), -1)
                copy(HH[:, b, :], R2[:, b, :]).then_inc(S("hh_ready"), 1)
            e.wait_ge(S("r2_free"), 1)
            e.sem_inc(S("r2_free"), -1)

            def out8():
                with e.Fori(0, 4) as i:
                    for s in range(2):
                        evac(s, lambda c: [(R2[:, bass.ds(i * 2 + s, 1), chunk(c)].rearrange("p a t -> p (a t)"), 0, CW)])
                        square(R2[:, bass.ds(i * 2 + s, 1), :].rearrange("p a t -> p (a t)"), s)

            out8()
            root_means()
            barrier(e, "act")
            block_squares()
            highs(in_r2)
            with e.Fori(0, 2) as i:
                for s in range(2):
                    evac(s, lambda c: [(R2[:, bass.ds(i * 2 + s, 1), chunk(c)].rearrange("p a t -> p (a t)"), 0, CW)])

            def mem_keys():
                for kt in range(2):
                    e.wait_ge(S("ckt_psum"), 1)
                    e.sem_inc(S("ckt_psum"), -1)
                    copy(CKT[:, :, kt * P:(kt + 1) * P], bank(6 + kt).rearrange("p (h k) -> p h k", h=4)).then_inc(S("act_done"), 1)
                    e.wait_ge(S("act_done"), 1)
                    e.sem_inc(S("act_done"), -1)
                    give(e, f"bank{6 + kt}")
                give(e, "ckt_ready")

            def cross_query(i, n):
                copy(CQ[:, :, 0:n], R2[:, 0:4, bass.ds(i, n)]).then_inc(S("cq_ready"), 1)

            def cross_exps(n):
                e.wait_ge(S("cnm_ready"), 1)
                e.sem_inc(S("cnm_ready"), -1)
                for h in range(4):
                    ins = e.activation(CP[0:n, h, :], PS[0:n, h * MEM:(h + 1) * MEM], ACT.Exp, bias=ST[0:n, 4 + h:5 + h], scale=float(P) ** -0.5,
                                       accum_out=ST[0:n, 8 + h:9 + h])
                ins.then_inc(S("act_done"), 1)
                e.wait_ge(S("act_done"), 1)
                e.sem_inc(S("act_done"), -1)
                give(e, "bank0", "bank1", "cexp_ready")

            def cross_by_key(n):
                for g in range(2):
                    e.wait_ge(S("cpt_psum"), 1)
                    e.sem_inc(S("cpt_psum"), -1)
                    copy(CPT[:, 2 * g:2 * g + 2, :, 0:n], bank(2 + g).rearrange("p (h k q) -> p h k q", h=2, k=2)[:, :, :, 0:n]).then_inc(S("act_done"), 1)
                    e.wait_ge(S("act_done"), 1)
                    e.sem_inc(S("act_done"), -1)
                    give(e, f"bank{2 + g}")
                give(e, "cpt_ready")

            def cross_out(i, n):
                e.wait_ge(S("co_psum"), 1)
                e.sem_inc(S("co_psum"), -1)
                copy(HH[:, 0:4, bass.ds(i, n)], PS[:, 2048:2048 + 4 * n].rearrange("p (h q) -> p h q", h=4)).then_inc(S("coh_ready"), 1)

            mem_keys()
            give(e, "ckr_free")
            cross_query(0, P)
            cross_exps(P)
            with e.Fori(0, TILES - 1) as t:
                cross_query(t * P + P, P)
                cross_by_key(P)
                cross_exps(P)
                cross_out(t * P, P)
            cross_by_key(P)
            cross_out(SEQ - P, P)
            mem_keys()
            cross_query(SEQ, DEC_SEQ)
            cross_exps(DEC_SEQ)
            cross_by_key(DEC_SEQ)
            cross_out(SEQ, DEC_SEQ)
            with e.Fori(0, 2) as i:
                for s in range(2):
                    for o in range(2):
                        evac(s, lambda c: [(R2[:, bass.ds((i * 2 + s) * 2 + o, 1), chunk(c)].rearrange("p a t -> p (a t)"), 0, CW)],
                             b0=3 * o, then=(o == 1))
                        square(R2[:, bass.ds((i * 2 + s) * 2 + o, 1), :].rearrange("p a t -> p (a t)"), o)
            root_means()
            barrier(e, "act")
            block_squares()
            highs(in_r2)

            def group():
                for f in range(2):
                    for c in range(CH):
                        e.wait_ge(S("gate_psum"), 1)
                        e.sem_inc(S("gate_psum"), -1)
                        e.wait_ge(S("silu_free"), 1)
                        e.sem_inc(S("silu_free"), -1)
                        e.activation(TMP[:, 0, chunk(c)], bank(c, 0, CW), ACT.Silu).then_inc(S("act_done"), 1)
                        e.wait_ge(S("act_done"), 1)
                        e.sem_inc(S("act_done"), -1)
                        give(e, f"bank{c}", "silu_ready")
                    split(0)
                    for c in range(CH):
                        if c == CH - 1:
                            e.wait_ge(S("w1_used"), 1)
                            e.sem_inc(S("w1_used"), -1)
                            split(1)
                        e.wait_ge(S("gu_ready"), 1)
                        e.sem_inc(S("gu_ready"), -1)
                        copy(GH[:, f, chunk(c)], TMP[:, 1, chunk(c)]).then_inc(S("gh_ready"), 1)
                e.wait_ge(S("w0_used"), 1)
                e.sem_inc(S("w0_used"), -1)
                split(0)
                e.wait_ge(S("w1_used"), 1)
                e.sem_inc(S("w1_used"), -1)
                split(1)

            with e.Fori(0, FB // 2) as i:
                group()
            e.wait_ge(S("r2_ready"), 1)
            e.sem_inc(S("r2_ready"), -1)
            squares(R2)
            barrier(e, "act")

        def stage(s, i, n):
            copy(R2[:, s, 0:1024].rearrange("p (b t) -> p b t", b=8)[:, :, 0:n], R1[:, :, bass.ds(i, n)]).then_inc(S("xo_ready"), 1)

        def tokens_out(s, n, first=False):
            if not first:
                e.wait_ge(S(f"xout_done{s}"), 16)
                e.sem_inc(S(f"xout_done{s}"), -16)
            for g in range(2):
                e.wait_ge(S("xo_psum"), 1)
                e.sem_inc(S("xo_psum"), -1)
                copy(R2[0:n, 4 + s, g * 512:(g + 1) * 512], PS[0:n, (2 * s + g) * 512:(2 * s + g + 1) * 512]).then_inc(S("act_done"), 1)
                e.wait_ge(S("act_done"), 1)
                e.sem_inc(S("act_done"), -1)
                give(e, f"bank{2 * s + g}")
            give(e, f"xout_ready{s}")

        stage(0, 0, P)
        stage(1, P, P)
        tokens_out(0, P, True)
        stage(0, 2 * P, P)
        tokens_out(1, P, True)
        with e.Fori(1, TILES // 2 - 1) as j:
            stage(1, (j * 2 + 1) * P, P)
            tokens_out(0, P)
            stage(0, (j * 2 + 2) * P, P)
            tokens_out(1, P)
        stage(1, SEQ - P, P)
        tokens_out(0, P)
        stage(0, SEQ, DEC_SEQ)
        tokens_out(1, P)
        tokens_out(0, DEC_SEQ)
        for s in range(2):
            e.wait_ge(S(f"xout_done{s}"), 16)
            e.sem_inc(S(f"xout_done{s}"), -16)

    @block.vector
    def _(e):
        def lo(slot):
            e.wait_ge(S(f"wh_ready{slot}"), 1)
            e.sem_inc(S(f"wh_ready{slot}"), -1)
            e.tensor_tensor(WL[:, slot, :], WRAW[:, slot, :], WH[:, slot, :].bitcast(F32), ALU.subtract).then_inc(S("dve_done"), 1)
            e.wait_ge(S("dve_done"), 1)
            e.sem_inc(S("dve_done"), -1)
            give(e, f"w_ready{slot}", f"w_free{slot}")

        def los(n):
            with e.Fori(0, n) as i:
                lo(0)
                lo(1)

        def add_square(s, n=T):
            e.wait_ge(S("sq_ready"), 1)
            e.sem_inc(S("sq_ready"), -1)
            e.tensor_tensor(TMP[:, 2, 0:n], TMP[:, 2, 0:n], TMP[:, s, 0:n], ALU.add).then_inc(S("dve_done"), 1)
            e.wait_ge(S("dve_done"), 1)
            e.sem_inc(S("dve_done"), -1)
            give(e, "sq_free")

        def sum_squares(n=T):
            e.memset(TMP[:, 2, 0:n], 0.0).then_inc(S("dve_done"), 1)
            e.wait_ge(S("dve_done"), 1)
            e.sem_inc(S("dve_done"), -1)
            for b in range(DB):
                add_square(b % 2, n)
            give(e, "sq_sum")
            e.wait_ge(S("rms_ready"), 1)
            e.sem_inc(S("rms_ready"), -1)

        def scaled(dst, src, gain, n=T):
            return e.scalar_tensor_tensor(out=dst, in0=src, scalar=PRM[:, gain:gain + 1], in1=TMP[:, 0, 0:n], op0=ALU.mult, op1=ALU.mult)

        in_tmp = lambda b: TMP[:, 1 + b % 2, :]
        in_r2 = lambda b: R2[:, b, :]

        def normed(src, which, t, n=T):
            g = G_AT + which * DB
            scaled(t(0)[:, 0:n], src[:, 0, 0:n], g, n).then_inc(S("ht_ready"), 1)
            for b in range(DB):
                if b < DB - 1:
                    scaled(t(b + 1)[:, 0:n], src[:, b + 1, 0:n], g + b + 1, n).then_inc(S("ht_ready"), 1)
                e.wait_ge(S("hh_ready"), 1)
                e.sem_inc(S("hh_ready"), -1)
                e.tensor_tensor(HL[:, b, 0:n], t(b)[:, 0:n], HH[:, b, 0:n].bitcast(F32), ALU.subtract).then_inc(S("dve_done"), 1)
                e.wait_ge(S("dve_done"), 1)
                e.sem_inc(S("dve_done"), -1)
                give(e, "h_ready")

        def add_normed(which, then=True):
            for b in range(DB):
                scaled(R2[:, b, :], R2[:, b, :], G_AT + which * DB + b).then_inc(S("dve_done"), 1)
                e.wait_ge(S("dve_done"), 1)
                e.sem_inc(S("dve_done"), -1)
                e.tensor_tensor(R1[:, b, :], R1[:, b, :], R2[:, b, :], ALU.add).then_inc(S("dve_done"), 1)
                e.wait_ge(S("dve_done"), 1)
                e.sem_inc(S("dve_done"), -1)
                if then:
                    give(e, "r1_ready")

        def add_and_norm(post, pre):
            add_normed(post)
            e.wait_ge(S("rms_ready"), 1)
            e.sem_inc(S("rms_ready"), -1)
            normed(R1, pre, in_r2)

        e.wait_ge(S("cst_dve"), 1)
        e.sem_inc(S("cst_dve"), -1)
        give(e, "xin_free0", "xin_free1", "w_free0", "w_free1", "praw_free", "rt_free")
        e.memset(SHC, 0.0).then_inc(S("dve_done"), 1)
        e.wait_ge(S("dve_done"), 1)
        e.sem_inc(S("dve_done"), -1)
        e.memset(PROW, 0.0).then_inc(S("dve_done"), 1)
        e.wait_ge(S("dve_done"), 1)
        e.sem_inc(S("dve_done"), -1)
        give(e, "prow_clear")

        def tokens_in(s, n, dst):
            e.wait_ge(S("xT_dve_psum"), 1)
            e.sem_inc(S("xT_dve_psum"), -1)
            e.tensor_copy(dst, bank(2 * s + 1).rearrange("p (b t) -> p b t", b=4)[:, :, 0:n]).then_inc(S("dve_done"), 1)
            e.wait_ge(S("dve_done"), 1)
            e.sem_inc(S("dve_done"), -1)
            give(e, f"bank{2 * s + 1}")
            e.wait_ge(S("xin_act"), 1)
            e.sem_inc(S("xin_act"), -1)
            give(e, f"xin_free{s}")

        for s in range(2):
            tokens_in(s, P, MEMT[:, 4:8, s * P:(s + 1) * P])
        give(e, "memT_ready")
        with e.Fori(0, TILES // 2) as j:
            for s in range(2):
                tokens_in(s, P, R1[:, 4:8, bass.ds((j * 2 + s) * P, P)])
        tokens_in(0, DEC_SEQ, R1[:, 4:8, SEQ:T])
        barrier(e, "dve")
        lo(0)
        lo(1)
        with e.Fori(0, DEPTH) as l:
            e.wait_ge(S("prm_rows"), 1)
            e.sem_inc(S("prm_rows"), -1)
            give(e, "prm_rows_pe")
            e.wait_ge(S("prm_ready"), 1)
            e.sem_inc(S("prm_ready"), -1)
            e.wait_ge(S("memT_dve"), 1)
            e.sem_inc(S("memT_dve"), -1)
            sum_squares(MEM)
            normed(R2, N_MEM, in_tmp, MEM)
            e.memset(TMP[:, 2, :], 0.0).then_inc(S("dve_done"), 1)
            e.wait_ge(S("dve_done"), 1)
            e.sem_inc(S("dve_done"), -1)
            with e.Fori(0, 4) as i:
                for s in range(2):
                    lo(s)
                    add_square(s)
            give(e, "sq_sum")
            e.wait_ge(S("rms_ready"), 1)
            e.sem_inc(S("rms_ready"), -1)
            barrier(e, "dve")
            normed(R1, MIX_PRE, in_tmp)
            los(3)
            lo(0)

            def shifted(dst, mu, sh, m=P):
                e.memset(PRAW[0:m, 0:1], 0.0).then_inc(S("dve_done"), 1)
                e.wait_ge(S("dve_done"), 1)
                e.sem_inc(S("dve_done"), -1)
                e.tensor_copy(PRAW[0:m, SEQ + 1:SEQ + 2], sh).then_inc(S("dve_done"), 1)
                e.wait_ge(S("dve_done"), 1)
                e.sem_inc(S("dve_done"), -1)
                e.wait_ge(S("praw_ready"), 1)
                e.sem_inc(S("praw_ready"), -1)
                e.tensor_tensor(dst[:, 0:SEQ], PRAW[0:m, 0:SEQ], PRAW[0:m, 1:SEQ + 1], ALU.subtract).then_inc(S("dve_done"), 1)
                e.wait_ge(S("dve_done"), 1)
                e.sem_inc(S("dve_done"), -1)
                e.tensor_tensor(dst[:, SEQ:T], PRAW[0:m, SEQ + 1:T + 1], PRAW[0:m, SEQ + 2:T + 2], ALU.subtract).then_inc(S("dve_done"), 1)
                e.wait_ge(S("dve_done"), 1)
                e.sem_inc(S("dve_done"), -1)
                e.scalar_tensor_tensor(out=dst[:, 0:SEQ], in0=dst[:, 0:SEQ], scalar=mu, in1=PRAW[0:m, 1:SEQ + 1], op0=ALU.mult, op1=ALU.add).then_inc(S("dve_done"), 1)
                e.wait_ge(S("dve_done"), 1)
                e.sem_inc(S("dve_done"), -1)
                e.scalar_tensor_tensor(out=dst[:, SEQ:T], in0=dst[:, SEQ:T], scalar=mu, in1=PRAW[0:m, SEQ + 2:T + 2], op0=ALU.mult, op1=ALU.add).then_inc(S("dve_done"), 1)
                e.wait_ge(S("dve_done"), 1)
                e.sem_inc(S("dve_done"), -1)

            def kept(at, m=P):
                for g, col in ((0, SEQ), (16, T + 1)):
                    e.tensor_copy(at(g), PRAW[0:m, col:col + 1]).then_inc(S("dve_done"), 1)
                    e.wait_ge(S("dve_done"), 1)
                    e.sem_inc(S("dve_done"), -1)
                give(e, "praw_free")

            for b, (dst, m) in enumerate(((TWA, P), (SG1, P), (SG2[0:32, :], 32))):
                shifted(dst, PRM[0:m, MU_AT + 12 + b:MU_AT + 13 + b], PRM[0:m, SH_AT + 12 + b:SH_AT + 13 + b], m)
                kept(lambda g: SHC[0:m, 12 + b + g:13 + b + g], m)
                if b < 2:
                    lo(1 - b)
            give(e, "lora_ready", "cos_free")
            e.wait_ge(S("cos_ready"), 1)
            e.sem_inc(S("cos_ready"), -1)
            give(e, "cos_pe")
            e.memset(KR[:, :, 1, :], 0.0).then_inc(S("dve_done"), 1)
            e.wait_ge(S("dve_done"), 1)
            e.sem_inc(S("dve_done"), -1)
            e.memset(VT[:, 1, :], 0.0).then_inc(S("dve_done"), 1)
            e.wait_ge(S("dve_done"), 1)
            e.sem_inc(S("dve_done"), -1)

            def rotary(i, n, slot):
                sn = SIN[:, bass.ds(i, n)].unsqueeze(1).broadcast_to([P, 4, n])
                e.wait_ge(S("swap_psum"), 1)
                e.sem_inc(S("swap_psum"), -1)
                e.tensor_tensor(RU[:, 0:4, 0:n], PS[:, 2560:2560 + 4 * n].rearrange("p (a t) -> p a t", a=4), sn, ALU.mult)
                e.tensor_tensor(RU[:, 4:6, 0:n], PS[:, 3072:3072 + 2 * n].rearrange("p (a t) -> p a t", a=2), sn[:, 0:2, :], ALU.mult).then_inc(S("dve_done"), 1)
                e.wait_ge(S("dve_done"), 1)
                e.sem_inc(S("dve_done"), -1)
                give(e, "bank5", "bank6")
                e.wait_ge(S("rt_ready"), 1)
                e.sem_inc(S("rt_ready"), -1)
                e.tensor_tensor(QR[:, :, 0:n], RT[:, 0:4, 0:n], RU[:, 0:4, 0:n], ALU.add)
                e.tensor_tensor(KR[:, :, slot, 0:n], RT[:, 4:6, 0:n], RU[:, 4:6, 0:n], ALU.add).then_inc(S("dve_done"), 1)
                e.wait_ge(S("dve_done"), 1)
                e.sem_inc(S("dve_done"), -1)
                give(e, "rt_free", "qk_ready")

            def masked(g, n, width, mask):
                at = g * 20
                e.wait_ge(S("score_psum"), 1)
                e.sem_inc(S("score_psum"), -1)
                e.wait_ge(S("sc_free"), 1)
                e.sem_inc(S("sc_free"), -1)
                src = PS[0:n, 1024 + g * 1536:2048 + g * 1536].rearrange("p (h k) -> p h k", h=4)[:, :, 0:width]
                dst = SC[0:n, 4 * g:4 * g + 4, 0:width]
                if mask is None:
                    e.tensor_scalar(dst, src, HEAD ** -0.5, None, ALU.mult).then_inc(S("dve_done"), 1)
                    e.wait_ge(S("dve_done"), 1)
                    e.sem_inc(S("dve_done"), -1)
                    give(e, f"bank{2 + 3 * g}", f"bank{3 + 3 * g}")
                else:
                    e.scalar_tensor_tensor(out=dst, in0=src, scalar=HEAD ** -0.5, in1=mask.unsqueeze(1).broadcast_to([n, 4, width]),
                                                op0=ALU.mult, op1=ALU.add).then_inc(S("dve_done"), 1)
                    e.wait_ge(S("dve_done"), 1)
                    e.sem_inc(S("dve_done"), -1)
                    give(e, f"bank{2 + 3 * g}", f"bank{3 + 3 * g}")
                e.tensor_reduce(ST[0:n, at:at + 4], dst, AX.X, ALU.max).then_inc(S("dve_done"), 1)
                e.wait_ge(S("dve_done"), 1)
                e.sem_inc(S("dve_done"), -1)
                e.scalar_tensor_tensor(out=ST[0:n, at + 4:at + 8], in0=ST[0:n, at:at + 4], scalar=-1.0, in1=ST[0:n, 48 + 4 * g:52 + 4 * g],
                                            op0=ALU.mult, op1=ALU.min).then_inc(S("dve_done"), 1)
                e.wait_ge(S("dve_done"), 1)
                e.sem_inc(S("dve_done"), -1)
                e.tensor_tensor(ST[0:n, at + 12:at + 16], ST[0:n, 40 + 4 * g:44 + 4 * g], ST[0:n, at + 4:at + 8], ALU.add).then_inc(S("dve_done"), 1)
                e.wait_ge(S("dve_done"), 1)
                e.sem_inc(S("dve_done"), -1)
                give(e, "nm_ready")

            def normalised(g, n, width):
                at = g * 20
                s = SC[0:n, 4 * g:4 * g + 4, 0:width]
                e.wait_ge(S("exp_ready"), 1)
                e.sem_inc(S("exp_ready"), -1)
                e.tensor_tensor(ST[0:n, at + 16:at + 20], ST[0:n, at + 8:at + 12], ST[0:n, at + 12:at + 16], ALU.add).then_inc(S("dve_done"), 1)
                e.wait_ge(S("dve_done"), 1)
                e.sem_inc(S("dve_done"), -1)
                e.reciprocal(ST[0:n, at + 16:at + 20], ST[0:n, at + 16:at + 20]).then_inc(S("dve_done"), 1)
                e.wait_ge(S("dve_done"), 1)
                e.sem_inc(S("dve_done"), -1)
                e.tensor_tensor(s, s, ST[0:n, at + 16:at + 20].unsqueeze(2).broadcast_to([n, 4, width]), ALU.mult).then_inc(S("prob_ready"), 1)

            e.tensor_copy(ST[:, 40:44], SINK[:, 0:8:2]).then_inc(S("dve_done"), 1)
            e.wait_ge(S("dve_done"), 1)
            e.sem_inc(S("dve_done"), -1)
            e.tensor_copy(ST[:, 44:48], SINK[:, 1:8:2]).then_inc(S("dve_done"), 1)
            e.wait_ge(S("dve_done"), 1)
            e.sem_inc(S("dve_done"), -1)
            e.tensor_scalar(ST[:, 48:56], ST[:, 40:48], -1.0, None, ALU.mult).then_inc(S("dve_done"), 1)
            e.wait_ge(S("dve_done"), 1)
            e.sem_inc(S("dve_done"), -1)

            def tile(i, slot, mask, last):
                normalised(0, P, 256)
                if not last:
                    rotary(i, P, slot)
                normalised(1, P, 256)
                if not last:
                    masked(0, P, 256, mask)
                    masked(1, P, 256, mask)

            even = lambda i: CST[:, bass.ds(C_AE + i * 256, 256)]
            odd = CST[:, C_AO:C_AO + 256]
            rotary(0, P, 0)
            masked(0, P, 256, even(0))
            masked(1, P, 256, even(0))
            with e.Fori(0, TILES // 2 - 1) as i:
                tile((i * 2 + 1) * P, 1, odd, False)
                tile((i * 2 + 2) * P, 0, even(i + 1), False)
            tile(SEQ - P, 1, odd, False)
            tile(None, None, None, True)
            e.wait_ge(S("kc_ready"), 1)
            e.sem_inc(S("kc_ready"), -1)
            rotary(SEQ, DEC_SEQ, 0)
            for g in range(2):
                masked(g, DEC_SEQ, DEC_SEQ + P, None)
                normalised(g, DEC_SEQ, DEC_SEQ + P)
            barrier(e, "dve")

            def scores(u, x):
                _, n, tiles, _ = unit(u)
                e.wait_ge(S("sm_psum"), 2)
                e.sem_inc(S("sm_psum"), -2)
                src = PS[0:n, 1024 * (1 - x):1024 * (2 - x)].rearrange("p (h c) -> p h c", h=2)
                dst = LTM[0:n, :].rearrange("p (a c) -> p a c", a=3)[:, :, 0:2 * tiles * n].rearrange("p a (g t) -> p g a t", t=n)
                m3 = CST[0:n, C_M3:C_M3 + 3 * P].rearrange("p (a t) -> p a t", a=3)[:, :, 0:n]
                e.tensor_tensor(dst[:, 2 * x:2 * x + 2, :, :], src[:, :, 0:3 * n].rearrange("p h (a t) -> p h a t", a=3),
                                m3.unsqueeze(1).broadcast_to([n, 2, 3, n]), ALU.mult)
                e.tensor_tensor(heads(tflat, 1536 + (u % 2) * 512, n, tiles)[:, 2 * x:2 * x + 2, :], src[:, :, 3 * n:4 * n],
                                     m3[:, 2, :].unsqueeze(1).broadcast_to([n, 2, n]), ALU.mult).then_inc(S("dve_done"), 1)
                e.wait_ge(S("dve_done"), 1)
                e.sem_inc(S("dve_done"), -1)
                give(e, f"bank{2 - 2 * x}", f"bank{3 - 2 * x}")
                if x == tiles - 1:
                    give(e, "lt_ready", "sm_ready")

            def low(u):
                _, n, tiles, _ = unit(u)
                e.wait_ge(S("l_psum"), 2)
                e.sem_inc(S("l_psum"), -2)
                mask = lambda at: CST[0:n, at:at + n].unsqueeze(1).broadcast_to([n, 2 * tiles, n])
                src = PS[0:n, 1024:2048].rearrange("p (h c) -> p h c", h=2)[:, :, 0:tiles * n].rearrange("p h (x t) -> p x h t", x=tiles)
                dst = heads(XXF, 0, n, tiles)
                e.tensor_tensor(dst.rearrange("p (x h) t -> p x h t", h=2), src,
                                     mask(C_NL).rearrange("p (x h) t -> p x h t", h=2), ALU.mult).then_inc(S("dve_done"), 1)
                e.wait_ge(S("dve_done"), 1)
                e.sem_inc(S("dve_done"), -1)
                give(e, "bank2", "bank3")
                e.tensor_tensor(dst, dst, mask(C_ID), ALU.add).then_inc(S("x_ready"), 1)

            def level_right(u, s):
                _, n, tiles, levels = unit(u)
                w = 2 * tiles * n
                for k in range(0 if s < levels - 1 else 1, 2):
                    xx = XXF[0:n, k * 512:k * 512 + w]
                    e.wait_ge(S("dx_psum"), 1)
                    e.sem_inc(S("dx_psum"), -1)
                    e.tensor_tensor(xx, xx, PS[0:n, k * 512:k * 512 + w], ALU.subtract).then_inc(S(("x_ready", "xt_ready")[k]), 1)

            def chunk_u(u, c):
                _, n, _, _ = unit(u)
                r, x = slice((c % 2) * CHUNK, (c % 2) * CHUNK + min(n, CHUNK)), c // 2
                if c == 0:
                    e.wait_ge(S("q_ready"), 1)
                    e.sem_inc(S("q_ready"), -1)
                e.wait_ge(S("u_psum"), 1)
                e.sem_inc(S("u_psum"), -1)
                e.scalar_tensor_tensor(out=US[r, x, :], in0=PS[r, 3072:3072 + P], scalar=-1.0, in1=QS[r, x, :],
                                       op0=ALU.mult, op1=ALU.subtract).then_inc(S("u_ready"), 1)
                ec = 20 + 4 * u + c
                e.tensor_scalar(STMP, SBD, EC[:, ec:ec + 1], None, ALU.mult).then_inc(S("dve_done"), 1)
                e.wait_ge(S("dve_done"), 1)
                e.sem_inc(S("dve_done"), -1)

            def chunk_state(u, c):
                ec = 20 + 4 * u + c
                e.wait_ge(S("ds_psum"), 1)
                e.sem_inc(S("ds_psum"), -1)
                for h in range(2):
                    p, q = slice(h * HEAD, (h + 1) * HEAD), 2560 + h * HEAD
                    ins = e.scalar_tensor_tensor(out=SBD[p, h * HEAD:(h + 1) * HEAD], in0=PS[p, q:q + HEAD], scalar=EC[p, ec:ec + 1],
                                                 in1=STMP[p, h * HEAD:(h + 1) * HEAD], op0=ALU.mult, op1=ALU.add)
                ins.then_inc(S("state_ready"), 1)

            give(e, "y_saved", "states_saved")
            with e.Fori(0, PAIRS) as j:
                e.wait_ge(S("states_saved"), 1)
                e.sem_inc(S("states_saved"), -1)
                e.wait_ge(S("wh_ready1"), 1)
                e.sem_inc(S("wh_ready1"), -1)
                e.tensor_copy(LW, WRAW[:, 1, 0:3 * P]).then_inc(S("dve_done"), 1)
                e.wait_ge(S("dve_done"), 1)
                e.sem_inc(S("dve_done"), -1)
                give(e, "lw_ready", "w_free1")
                e.tensor_copy(PC[:, 0:3], PRM[:, bass.ds(MU_AT + j, 9)][:, 0:9:4])
                e.tensor_copy(PC[:, 9:12], PRM[:, bass.ds(SH_AT + j, 9)][:, 0:9:4])
                e.tensor_copy(PC[:, 12:13], PRM[:, bass.ds(RK_AT + j, 1)])
                e.tensor_copy(PC[:, 3:9], PRM[:, bass.ds(RV_AT + j, 21)][:, 0:21:4]).then_inc(S("dve_done"), 1)
                e.wait_ge(S("dve_done"), 1)
                e.sem_inc(S("dve_done"), -1)
                e.tensor_scalar(PC[:, 13:14], PC[:, 6:7], -1.0, 1.0, ALU.mult, ALU.add).then_inc(S("dve_done"), 1)
                e.wait_ge(S("dve_done"), 1)
                e.sem_inc(S("dve_done"), -1)
                give(e, "pc_ready")

                def row(b, dst):
                    shifted(dst, PC[:, b:b + 1], PC[:, 9 + b:10 + b])
                    kept(lambda g: SHC[:, bass.ds(j + (b * 4 + g), 1)])

                row(0, RR)
                lo(0)
                e.memset(SEG, 1.0).then_inc(S("dve_done"), 1)
                e.wait_ge(S("dve_done"), 1)
                e.sem_inc(S("dve_done"), -1)
                e.memset(SEG[:, 0:T:CHUNK], 0.0).then_inc(S("dve_done"), 1)
                e.wait_ge(S("dve_done"), 1)
                e.sem_inc(S("dve_done"), -1)
                e.wait_ge(S("sig_ready"), 1)
                e.sem_inc(S("sig_ready"), -1)
                e.tensor_tensor_scan(DD, SEG, DD2, 0.0, ALU.mult, ALU.add).then_inc(S("dve_done"), 1)
                e.wait_ge(S("dve_done"), 1)
                e.sem_inc(S("dve_done"), -1)
                d = DD[:, 0:SEQ].rearrange("p (c t) -> p c t", t=CHUNK)
                e.tensor_copy(ST[:, 0:16], d[:, :, 31])
                e.tensor_copy(ST[:, 16:17], DD[:, SEQ + 15:SEQ + 16]).then_inc(S("dve_done"), 1)
                e.wait_ge(S("dve_done"), 1)
                e.sem_inc(S("dve_done"), -1)
                e.tensor_tensor(EC[:, 16:17], DD[:, T - 1:T], ST[:, 16:17], ALU.subtract)
                e.tensor_copy(EC[:, 17:18], ST[:, 16:17])
                e.tensor_tensor(EC[:, 0:16], d[:, :, 63], ST[:, 0:16], ALU.subtract).then_inc(S("dve_done"), 1)
                e.wait_ge(S("dve_done"), 1)
                e.sem_inc(S("dve_done"), -1)
                e.tensor_tensor(EC[:, 0:15], EC[:, 0:15], ST[:, 1:16], ALU.add).then_inc(S("dve_done"), 1)
                e.wait_ge(S("dve_done"), 1)
                e.sem_inc(S("dve_done"), -1)
                e.tensor_tensor(d, d, ST[:, 0:16].unsqueeze(2).broadcast_to([P, 16, CHUNK]), ALU.subtract)
                e.tensor_scalar(DD[:, SEQ:T], DD[:, SEQ:T], ST[:, 16:17], None, ALU.subtract).then_inc(S("dve_done"), 1)
                e.wait_ge(S("dve_done"), 1)
                e.sem_inc(S("dve_done"), -1)
                e.tensor_tensor(DD2, DD, DD2, ALU.subtract).then_inc(S("dve_done"), 1)
                e.wait_ge(S("dve_done"), 1)
                e.sem_inc(S("dve_done"), -1)
                give(e, "dd_ready")
                lo(1)
                row(1, KF)
                e.tensor_scalar(KK, KF, PC[:, 5:6], None, ALU.mult).then_inc(S("dve_done"), 1)
                e.wait_ge(S("dve_done"), 1)
                e.sem_inc(S("dve_done"), -1)
                give(e, "kkr_ready")
                e.tensor_scalar(TMP[:, 1, :], BB, PC[:, 6:7], PC[:, 13:14], ALU.mult, ALU.add).then_inc(S("dve_done"), 1)
                e.wait_ge(S("dve_done"), 1)
                e.sem_inc(S("dve_done"), -1)
                e.tensor_tensor(KF, KF, TMP[:, 1, :], ALU.mult).then_inc(S("dve_done"), 1)
                e.wait_ge(S("dve_done"), 1)
                e.sem_inc(S("dve_done"), -1)
                e.scalar_tensor_tensor(out=TMP[:, 1, :], in0=RR, scalar=PC[:, 12:13], in1=KF, op0=ALU.mult, op1=ALU.mult).then_inc(S("dve_done"), 1)
                e.wait_ge(S("dve_done"), 1)
                e.sem_inc(S("dve_done"), -1)
                give(e, "rk_ready", "rk_formed")
                for c in range(CH):
                    e.wait_ge(S("kk_psum"), 1)
                    e.sem_inc(S("kk_psum"), -1)
                    e.tensor_scalar(TMP[:, 2, chunk(c)], bank(c, 0, CW), 1e-24, None, ALU.max).then_inc(S("dve_done"), 1)
                    e.wait_ge(S("dve_done"), 1)
                    e.sem_inc(S("dve_done"), -1)
                    give(e, f"bank{c}")
                give(e, "kkn_ready")
                lo(0)
                row(2, VV)
                e.wait_ge(S("e_ready"), 1)
                e.sem_inc(S("e_ready"), -1)
                e.tensor_tensor(BB, BB, DD, ALU.mult)
                e.memset(SAMPLE_IN, 0.0).then_inc(S("dve_done"), 1)
                e.wait_ge(S("dve_done"), 1)
                e.sem_inc(S("dve_done"), -1)
                give(e, "sin_free")
                e.wait_ge(S("kks_ready"), 1)
                e.sem_inc(S("kks_ready"), -1)
                e.tensor_tensor(KK, KK, TMP[:, 2, :], ALU.mult).then_inc(S("dve_done"), 1)
                e.wait_ge(S("dve_done"), 1)
                e.sem_inc(S("dve_done"), -1)
                e.tensor_tensor(BB, BB, KK, ALU.mult)
                e.tensor_tensor(KK, KK, DD2, ALU.mult)
                e.wait_ge(S("rk_scaled"), 1)
                e.sem_inc(S("rk_scaled"), -1)
                e.wait_ge(S("y_saved"), 1)
                e.sem_inc(S("y_saved"), -1)
                e.memset(SBD, 0.0).then_inc(S("dve_done"), 1)
                e.wait_ge(S("dve_done"), 1)
                e.sem_inc(S("dve_done"), -1)
                give(e, "state_ready", "til_ready")
                for c in range(CH):
                    e.wait_ge(S("rk_psum"), 1)
                    e.sem_inc(S("rk_psum"), -1)
                    e.tensor_tensor(BON[:, chunk(c)], VV[:, chunk(c)], bank(3 + c, 0, CW), ALU.mult).then_inc(S("dve_done"), 1)
                    e.wait_ge(S("dve_done"), 1)
                    e.sem_inc(S("dve_done"), -1)
                    give(e, f"bank{3 + c}")
                for u in range(UNITS + 1):
                    _, _, tiles, levels = unit(u)
                    if u > 0:
                        chunk_u(u - 1, 0)
                    scores(u, 0)
                    if u > 0:
                        chunk_state(u - 1, 0)
                    if tiles == 2:
                        scores(u, 1)
                    low(u)
                    for s in range(levels):
                        if u > 0 and s < 3:
                            chunk_u(u - 1, s + 1)
                        level_right(u, s)
                        if u > 0 and s < 3:
                            chunk_state(u - 1, s + 1)
                e.wait_ge(S("sin_psum"), 1)
                e.sem_inc(S("sin_psum"), -1)
                e.tensor_scalar(SBD, PS[:, 512:512 + P], EC[:, 37:38], None, ALU.mult).then_inc(S("dve_done"), 1)
                e.wait_ge(S("dve_done"), 1)
                e.sem_inc(S("dve_done"), -1)
                give(e, "bank1", "state_ready")
                chunk_u(UNITS, 0)
                chunk_state(UNITS, 0)
                e.wait_ge(S("rms_ready"), 1)
                e.sem_inc(S("rms_ready"), -1)
                e.tensor_tensor(YY, TMP[:, 1, :], TMP[:, 2, :], ALU.mult).then_inc(S("dve_done"), 1)
                e.wait_ge(S("dve_done"), 1)
                e.sem_inc(S("dve_done"), -1)
                e.tensor_scalar(YY, YY, PC[:, 7:8], PC[:, 8:9], ALU.mult, ALU.add).then_inc(S("dve_done"), 1)
                e.wait_ge(S("dve_done"), 1)
                e.sem_inc(S("dve_done"), -1)
                e.tensor_tensor(YY, YY, BON, ALU.add).then_inc(S("dve_done"), 1)
                e.wait_ge(S("dve_done"), 1)
                e.sem_inc(S("dve_done"), -1)
                e.tensor_tensor(YY, YY, GG, ALU.mult).then_inc(S("dve_done"), 1)
                e.wait_ge(S("dve_done"), 1)
                e.sem_inc(S("dve_done"), -1)
                give(e, "y_ready")
            lo(1)
            e.wait_ge(S("y_saved"), 1)
            e.sem_inc(S("y_saved"), -1)
            e.wait_ge(S("states_saved"), 1)
            e.sem_inc(S("states_saved"), -1)
            give(e, "shc_full")
            barrier(e, "dve")
            for b in range(DB):
                e.wait_ge(S("hh_ready"), 1)
                e.sem_inc(S("hh_ready"), -1)
                e.tensor_tensor(HL[:, b, :], R2[:, b, :], HH[:, b, :].bitcast(F32), ALU.subtract).then_inc(S("dve_done"), 1)
                e.wait_ge(S("dve_done"), 1)
                e.sem_inc(S("dve_done"), -1)
                give(e, "h_ready")
            give(e, "r2_free")
            e.memset(TMP[:, 2, :], 0.0).then_inc(S("dve_done"), 1)
            e.wait_ge(S("dve_done"), 1)
            e.sem_inc(S("dve_done"), -1)
            with e.Fori(0, 4) as i:
                for s in range(2):
                    lo(s)
                    add_square(s)
            give(e, "sq_sum")
            e.wait_ge(S("rms_ready"), 1)
            e.sem_inc(S("rms_ready"), -1)
            barrier(e, "dve")
            add_and_norm(MIX_POST, X_PRE)
            give(e, "ckr_free")
            los(2)

            def cross_probs(n):
                e.wait_ge(S("cs_psum"), 1)
                e.sem_inc(S("cs_psum"), -1)
                e.tensor_reduce(ST[0:n, 0:4], PS[0:n, 0:1024].rearrange("p (h k) -> p h k", h=4), AX.X, ALU.max).then_inc(S("dve_done"), 1)
                e.wait_ge(S("dve_done"), 1)
                e.sem_inc(S("dve_done"), -1)
                e.tensor_scalar(ST[0:n, 4:8], ST[0:n, 0:4], -float(P) ** -0.5, None, ALU.mult).then_inc(S("dve_done"), 1)
                e.wait_ge(S("dve_done"), 1)
                e.sem_inc(S("dve_done"), -1)
                give(e, "cnm_ready")
                e.wait_ge(S("cexp_ready"), 1)
                e.sem_inc(S("cexp_ready"), -1)
                e.reciprocal(ST[0:n, 0:4], ST[0:n, 8:12]).then_inc(S("dve_done"), 1)
                e.wait_ge(S("dve_done"), 1)
                e.sem_inc(S("dve_done"), -1)
                e.tensor_tensor(CP[0:n, :, :], CP[0:n, :, :], ST[0:n, 0:4].unsqueeze(2).broadcast_to([n, 4, MEM]), ALU.mult).then_inc(S("dve_done"), 1)
                e.wait_ge(S("dve_done"), 1)
                e.sem_inc(S("dve_done"), -1)
                give(e, "cp_ready")

            def cross_low(i, n):
                e.wait_ge(S("coh_ready"), 1)
                e.sem_inc(S("coh_ready"), -1)
                e.tensor_tensor(HL[:, 0:4, bass.ds(i, n)], PS[:, 2048:2048 + 4 * n].rearrange("p (h q) -> p h q", h=4),
                                     HH[:, 0:4, bass.ds(i, n)].bitcast(F32), ALU.subtract).then_inc(S("dve_done"), 1)
                e.wait_ge(S("dve_done"), 1)
                e.sem_inc(S("dve_done"), -1)
                give(e, "bank4")

            cross_probs(P)
            with e.Fori(0, TILES - 1) as t:
                cross_probs(P)
                cross_low(t * P, P)
            cross_low(SEQ - P, P)
            cross_probs(DEC_SEQ)
            cross_low(SEQ, DEC_SEQ)
            give(e, "ch_ready")
            e.memset(TMP[:, 2, :], 0.0).then_inc(S("dve_done"), 1)
            e.wait_ge(S("dve_done"), 1)
            e.sem_inc(S("dve_done"), -1)
            with e.Fori(0, 2) as i:
                for s in range(2):
                    add_square(0)
                    lo(s)
                    add_square(1)
            give(e, "sq_sum")
            e.wait_ge(S("rms_ready"), 1)
            e.sem_inc(S("rms_ready"), -1)
            barrier(e, "dve")
            add_and_norm(X_POST, FFN_PRE)
            give(e, "silu_free", "silu_free", "silu_free")

            def inner_low(f, c):
                e.wait_ge(S("gh_ready"), 1)
                e.sem_inc(S("gh_ready"), -1)
                e.tensor_tensor(GL[:, f, chunk(c)], TMP[:, 1, chunk(c)], GH[:, f, chunk(c)].bitcast(F32), ALU.subtract).then_inc(S("dve_done"), 1)
                e.wait_ge(S("dve_done"), 1)
                e.sem_inc(S("dve_done"), -1)
                if f == 1:
                    give(e, "g_ready")

            def group(first):
                for f in range(2):
                    lo(0)
                    for c in range(CH):
                        e.wait_ge(S("silu_ready"), 1)
                        e.sem_inc(S("silu_ready"), -1)
                        e.wait_ge(S("up_psum"), 1)
                        e.sem_inc(S("up_psum"), -1)
                        if c == CH - 1:
                            give(e, "w1_used")
                        e.tensor_tensor(TMP[:, 1, chunk(c)], TMP[:, 0, chunk(c)], bank(3 + c, 0, CW), ALU.mult).then_inc(S("dve_done"), 1)
                        e.wait_ge(S("dve_done"), 1)
                        e.sem_inc(S("dve_done"), -1)
                        give(e, f"bank{3 + c}", "gu_ready", "silu_free")
                        if c == 1:
                            inner_low(f, 0)
                    lo(1)
                    inner_low(f, 1)
                    inner_low(f, 2)
                for c in range(CH):
                    for m in range(DB):
                        if c == CH - 1 and m == 3:
                            lo(0)
                        b = DOWN_BANKS[m]
                        e.wait_ge(S("down_psum"), 1)
                        e.sem_inc(S("down_psum"), -1)
                        if c == CH - 1 and m == DB - 1:
                            give(e, "w1_used")
                        if first:
                            e.tensor_copy(R2[:, m, chunk(c)], bank(b, 0, CW)).then_inc(S(f"bank{b}"), 1)
                        else:
                            e.tensor_tensor(R2[:, m, chunk(c)], R2[:, m, chunk(c)], bank(b, 0, CW), ALU.add).then_inc(S(f"bank{b}"), 1)
                lo(1)

            e.memset(PROW, 0.0).then_inc(S("dve_done"), 1)
            e.wait_ge(S("dve_done"), 1)
            e.sem_inc(S("dve_done"), -1)
            give(e, "prow_clear")
            group(True)
            with e.Fori(1, FB // 2) as i:
                group(False)
            e.wait_ge(S("silu_free"), 3)
            e.sem_inc(S("silu_free"), -3)
            give(e, "r2_ready")
            sum_squares()
            add_normed(FFN_POST, False)
            barrier(e, "dve")


INPUTS = ["x_prompt", "mem_prompt", "x_sample", "cache_swa_k", "cache_swa_v", "cache_mem_k", "cache_mem_v", "state_rwkv",
          "state_shift", "norm_gains", "w_in", "attn_sink", "shift_mu", "rwkv_vecs", "rwkv_rk", "rwkv_w2", "rwkv_a2",
          "rwkv_g2", "w_out", "w_mem_q", "w_mem_kv", "w_mem_o", "w_gate_up", "w_down"]
OUTPUTS = [("y_prompt", (1, SEQ, D_MODEL)), ("y_sample", (1, DEC_SEQ, D_MODEL)),
           ("new_swa_k_prompt", (DEPTH, 1, WINDOW, 2, HEAD)), ("new_swa_v_prompt", (DEPTH, 1, WINDOW, 2, HEAD)),
           ("new_mem_k_prompt", (DEPTH, 1, MEM, MEM_HEADS, P)), ("new_mem_v_prompt", (DEPTH, 1, MEM, MEM_HEADS, P)),
           ("new_state_rwkv_prompt", (DEPTH, 1, 8, HEAD, HEAD)), ("new_state_shift_prompt", (DEPTH, 1, 1, RWKV_PROJ)),
           ("new_swa_k_sample", (DEPTH, 1, DEC_SEQ, 2, HEAD)), ("new_swa_v_sample", (DEPTH, 1, DEC_SEQ, 2, HEAD)),
           ("new_state_rwkv_sample", (DEPTH, 1, 8, HEAD, HEAD)), ("new_state_shift_sample", (DEPTH, 1, 1, RWKV_PROJ))]


def kernel(**inputs):
    import concourse.bacc as bacc
    from concourse.bass_utils import run_bass_kernel_spmd

    nc = bacc.Bacc("TRN2", target_bir_lowering=False, num_devices=1)
    arrays, io = {}, {}
    c, long = constants()
    for name, a in [(n, inputs[n]) for n in INPUTS] + [("consts", c), ("long", long)]:
        arrays[f"in_{name}"] = np.ascontiguousarray(a)
        io[name] = nc.dram_tensor(f"in_{name}", arrays[f"in_{name}"].shape, F32, kind="ExternalInput").ap()
    for name, shape in OUTPUTS:
        io[name] = nc.dram_tensor(f"out_{name}", shape, F32, kind="ExternalOutput").ap()
    program(nc, io)
    r = run_bass_kernel_spmd(nc, [arrays], core_ids=[0])
    return tuple(r.results[0][f"out_{name}"] for name, _ in OUTPUTS)
```
